# Optimizing a Trainium2 kernel written in Bass

```python
import math
import jax, jax.numpy as jnp
from jax import lax
import numpy as np

D_MODEL = 1024
BATCH = 1
SEQ = 256
DEPTH = 1

EPS = 1e-6
GLA_HEADS = 4
GLA_DK = D_MODEL // (2 * GLA_HEADS)
GLA_DV = D_MODEL // GLA_HEADS
GLA_KEY = GLA_HEADS * GLA_DK
GLA_VAL = GLA_HEADS * GLA_DV
GLA_RANK = 16
GLA_GATE_TEMP = 16.0
GLA_CHUNK = 64
HY_WIDTH = D_MODEL
HY_BANDS = 16
HY_EMB = 1 + 2 * HY_BANDS
HY_FFN = 64
HY_TARGET = 1e-2
HY_FAST_PCT = 0.3
HY_SLOW_PCT = 1.5
N_EXPERTS = 32
TOP_K = 4
D_FF = D_MODEL
SWIGLU_LIMIT = 7.0
SWIGLU_ALPHA = 1.702
IN_SIZES = (GLA_KEY, GLA_KEY, GLA_VAL, GLA_VAL, 2 * GLA_RANK, 3 * HY_WIDTH, 2 * D_MODEL)
IN_TOTAL = sum(IN_SIZES)
IN_SPLITS = tuple(int(v) for v in np.cumsum(IN_SIZES)[:-1])

kernel_name = "hybrid_gla_hyena_moe_encoder"

def rms_norm(x, w):
    xf = x.astype(jnp.float32)
    y = xf * lax.rsqrt(jnp.mean(xf * xf, axis=-1, keepdims=True) + EPS)
    return (y * w.astype(jnp.float32)).astype(x.dtype)

def gla_one_direction(q, k, v, g, strict):
    B, L, _ = q.shape
    N = L // GLA_CHUNK

    def chunks(t, d):
        return t.reshape(B, N, GLA_CHUNK, GLA_HEADS, d).transpose(0, 3, 1, 2, 4)

    qc, kc, gc, vc = chunks(q, GLA_DK), chunks(k, GLA_DK), chunks(g, GLA_DK), chunks(v, GLA_DV)
    b = jnp.cumsum(gc, axis=-2)
    b_last = b[..., -1:, :]
    q_t = qc * jnp.exp(b)
    k_t = kc * jnp.exp(-b)
    idx = jnp.arange(GLA_CHUNK)
    mask = (idx[:, None] > idx[None, :]) if strict else (idx[:, None] >= idx[None, :])
    scores = jnp.einsum('bhncd,bhnsd->bhncs', q_t, k_t)
    scores = jnp.where(mask, scores, 0.0)
    o_intra = jnp.einsum('bhncs,bhnse->bhnce', scores, vc)
    k_end = kc * jnp.exp(b_last - b)
    upd = jnp.einsum('bhncd,bhnce->bhnde', k_end, vc)
    dec = jnp.exp(b_last[..., 0, :])

    def step(state, inp):
        d_n, u_n = inp
        return d_n[..., None] * state + u_n, state

    init = jnp.zeros((B, GLA_HEADS, GLA_DK, GLA_DV), jnp.float32)
    _, s_prev = lax.scan(step, init, (jnp.moveaxis(dec, 2, 0), jnp.moveaxis(upd, 2, 0)))
    s_prev = jnp.moveaxis(s_prev, 0, 2)
    o_inter = jnp.einsum('bhncd,bhnde->bhnce', q_t, s_prev)
    o = o_intra + o_inter
    return o.transpose(0, 2, 3, 1, 4).reshape(B, L, GLA_HEADS, GLA_DV)

def gla_branch(q, k, v, r, a_low, gla_gate_w2, gla_gate_b, gla_norm_w):
    dt = q.dtype
    B, L, _ = q.shape
    qf = q.astype(jnp.float32) * (GLA_DK ** -0.5)
    kf = k.astype(jnp.float32)
    vf = v.astype(jnp.float32)
    a2 = a_low.astype(jnp.float32).reshape(B, L, 2, GLA_RANK)
    logits = jnp.einsum('bldr,drk->bldk', a2, gla_gate_w2.astype(jnp.float32)) + gla_gate_b.astype(jnp.float32)
    log_a = jax.nn.log_sigmoid(logits) / GLA_GATE_TEMP
    o_f = gla_one_direction(qf, kf, vf, log_a[:, :, 0], strict=False)
    flip = lambda t: jnp.flip(t, axis=1)
    o_b = flip(gla_one_direction(flip(qf), flip(kf), flip(vf), flip(log_a[:, :, 1]), strict=True))
    o = o_f + o_b
    o = o * lax.rsqrt(jnp.mean(o * o, axis=-1, keepdims=True) + EPS) * gla_norm_w.astype(jnp.float32)
    o = o.reshape(B, L, GLA_VAL).astype(dt)
    return o * jax.nn.silu(r)

def short_conv3(u, w, b):
    up = jnp.pad(u, ((0, 0), (1, 1), (0, 0)))
    return w[0] * up[:, :-2] + w[1] * up[:, 1:-1] + w[2] * up[:, 2:] + b

def hyena_filters(L, hy_freq, w1, b1, w2, b2, w3, hy_decay):
    f32 = jnp.float32
    t = jnp.linspace(0.0, 1.0, L, dtype=f32)[:, None]
    omega = 2.0 * math.pi * jnp.arange(L, dtype=f32) / L
    f = jnp.linspace(1e-4, HY_BANDS - 1, HY_BANDS, dtype=f32)
    ang = omega[:, None] * f[None, :]
    z = jnp.concatenate([t, jnp.cos(ang), -jnp.sin(ang)], axis=-1)
    fr = hy_freq.astype(f32)
    h = jnp.sin(fr * (z @ w1.astype(f32) + b1.astype(f32)))
    h = jnp.sin(fr * (h @ w2.astype(f32) + b2.astype(f32)))
    h = (h @ w3.astype(f32)).reshape(L, 2, HY_WIDTH)
    h = h * jnp.exp(-t[:, :, None] * jnp.abs(hy_decay.astype(f32))[None])
    kern = jnp.concatenate([h[:, 0], jnp.zeros((1, HY_WIDTH), f32), h[:0:-1, 1]], axis=0)
    return kern * lax.rsqrt(jnp.sum(kern * kern, axis=0, keepdims=True) + EPS)

def hyena_branch(u_proj, conv_w, conv_b, kern, hy_bias):
    dt = u_proj.dtype
    u = short_conv3(u_proj, conv_w, conv_b)
    x0, x1, v = jnp.split(u, 3, axis=-1)
    z = (v * x1).astype(jnp.float32)
    L = z.shape[1]
    Z = jnp.fft.rfft(z, n=2 * L, axis=1)
    K = jnp.fft.rfft(kern, n=2 * L, axis=0)
    y = jnp.fft.irfft(Z * K[None], n=2 * L, axis=1)[:, :L] + z * hy_bias.astype(jnp.float32)
    return y.astype(dt) * x0

def moe_ffn(h, router_w, router_b, w_gate_up, b_gate_up, w_down, b_down):
    B, L, D = h.shape
    ht = h.reshape(B * L, D)
    logits = ht.astype(jnp.float32) @ router_w.astype(jnp.float32) + router_b.astype(jnp.float32)
    top_vals, top_idx = lax.top_k(logits, TOP_K)
    weights = jax.nn.softmax(top_vals, axis=-1)
    combine = jnp.sum(jax.nn.one_hot(top_idx, N_EXPERTS, dtype=jnp.float32) * weights[..., None], axis=1)
    combine = combine.astype(ht.dtype)
    out = jnp.zeros_like(ht)
    for e in range(N_EXPERTS):
        gu = ht @ w_gate_up[e] + b_gate_up[e]
        gate, up = gu[:, :D_FF], gu[:, D_FF:]
        gate = jnp.minimum(gate, SWIGLU_LIMIT)
        up = jnp.clip(up, -SWIGLU_LIMIT, SWIGLU_LIMIT)
        act = gate * jax.nn.sigmoid(SWIGLU_ALPHA * gate) * (up + 1.0)
        out = out + combine[:, e:e + 1] * (act @ w_down[e] + b_down[e])
    return out.reshape(B, L, D)

def setup_inputs(seed: int = 0) -> dict:
    key = jax.random.key(seed)
    ks = jax.random.split(key, 32)
    f32 = jnp.float32
    nrm = lambda k, shape, s: jax.random.normal(k, shape, f32) * s
    min_decay = abs(math.log(HY_TARGET) / HY_SLOW_PCT)
    max_decay = abs(math.log(HY_TARGET) / HY_FAST_PCT)
    base_decay = jnp.linspace(min_decay, max_decay, HY_WIDTH, dtype=f32)
    return {
        "x": nrm(ks[0], (BATCH, SEQ, D_MODEL), 1.0),
        "norm1_w": 1.0 + nrm(ks[1], (D_MODEL,), 0.02),
        "w_in": nrm(ks[2], (D_MODEL, IN_TOTAL), D_MODEL ** -0.5),
        "gla_gate_w2": nrm(ks[3], (2, GLA_RANK, GLA_KEY), GLA_RANK ** -0.5),
        "gla_gate_b": nrm(ks[4], (2, GLA_KEY), 0.5),
        "gla_norm_w": 1.0 + nrm(ks[5], (GLA_DV,), 0.02),
        "hy_conv_w": nrm(ks[6], (3, 3 * HY_WIDTH), 0.5),
        "hy_conv_b": nrm(ks[7], (3 * HY_WIDTH,), 0.02),
        "hy_freq": 1.0 + nrm(ks[8], (HY_FFN,), 0.05),
        "hy_ffn_w1": nrm(ks[9], (HY_EMB, HY_FFN), HY_EMB ** -0.5),
        "hy_ffn_b1": nrm(ks[10], (HY_FFN,), 0.1),
        "hy_ffn_w2": nrm(ks[11], (HY_FFN, HY_FFN), HY_FFN ** -0.5),
        "hy_ffn_b2": nrm(ks[12], (HY_FFN,), 0.1),
        "hy_ffn_w3": nrm(ks[13], (HY_FFN, 2 * HY_WIDTH), HY_FFN ** -0.5),
        "hy_decay": base_decay[None, :] * (1.0 + nrm(ks[14], (2, HY_WIDTH), 0.05)),
        "hy_bias": nrm(ks[15], (HY_WIDTH,), 0.1),
        "w_branch_gla": nrm(ks[16], (GLA_VAL, D_MODEL), GLA_VAL ** -0.5),
        "w_branch_hy": nrm(ks[17], (HY_WIDTH, D_MODEL), HY_WIDTH ** -0.5),
        "w_out": nrm(ks[18], (D_MODEL, D_MODEL), D_MODEL ** -0.5),
        "norm2_w": 1.0 + nrm(ks[19], (D_MODEL,), 0.02),
        "router_w": nrm(ks[20], (D_MODEL, N_EXPERTS), D_MODEL ** -0.5),
        "router_b": nrm(ks[21], (N_EXPERTS,), 0.01),
        "w_gate_up": nrm(ks[22], (N_EXPERTS, D_MODEL, 2 * D_FF), D_MODEL ** -0.5),
        "b_gate_up": nrm(ks[23], (N_EXPERTS, 2 * D_FF), 0.01),
        "w_down": nrm(ks[24], (N_EXPERTS, D_FF, D_MODEL), D_FF ** -0.5),
        "b_down": nrm(ks[25], (N_EXPERTS, D_MODEL), 0.01),
        "norm_f_w": 1.0 + nrm(ks[26], (D_MODEL,), 0.02),
    }

def reference(x, norm1_w, w_in, gla_gate_w2, gla_gate_b, gla_norm_w, hy_conv_w, hy_conv_b,
              hy_freq, hy_ffn_w1, hy_ffn_b1, hy_ffn_w2, hy_ffn_b2, hy_ffn_w3, hy_decay, hy_bias,
              w_branch_gla, w_branch_hy, w_out, norm2_w, router_w, router_b,
              w_gate_up, b_gate_up, w_down, b_down, norm_f_w):
    h = x
    L = x.shape[1]
    for _ in range(DEPTH):
        xn = rms_norm(h, norm1_w)
        proj = xn @ w_in
        q, k, v, r, a_low, hy_in, gates = jnp.split(proj, IN_SPLITS, axis=-1)
        o_gla = gla_branch(q, k, v, r, a_low, gla_gate_w2, gla_gate_b, gla_norm_w)
        kern = hyena_filters(L, hy_freq, hy_ffn_w1, hy_ffn_b1, hy_ffn_w2, hy_ffn_b2, hy_ffn_w3, hy_decay)
        o_hy = hyena_branch(hy_in, hy_conv_w, hy_conv_b, kern, hy_bias)
        g_gla, g_hy = jnp.split(gates, 2, axis=-1)
        merged = jax.nn.sigmoid(g_gla) * (o_gla @ w_branch_gla) + jax.nn.sigmoid(g_hy) * (o_hy @ w_branch_hy)
        h = h + merged @ w_out
        hn = rms_norm(h, norm2_w)
        h = h + moe_ffn(hn, router_w, router_b, w_gate_up, b_gate_up, w_down, b_down)
    return rms_norm(h, norm_f_w)


_drawn_inputs = setup_inputs


def setup_inputs(seed=0):
    import zlib

    import numpy as np

    out = dict(_drawn_inputs(seed))
    spreads = {}
    factors = {'b_gate_up': 8.0, 'b_down': 8.0, 'norm_f_w': 2.799}
    for name, (base, spread) in spreads.items():
        noise = np.random.default_rng([zlib.crc32(name.encode()), seed]).standard_normal(out[name].shape)
        drawn = base * np.exp(spread * noise) if base else spread * noise
        out[name] = __import__('jax').numpy.asarray(drawn.astype(out[name].dtype))
    for name, factor in factors.items():
        out[name] = (out[name] * factor).astype(out[name].dtype)
    return out
```

```python
from contextlib import ExitStack

import numpy as np

import concourse.bass as bass
from concourse import mybir

ALU = mybir.AluOpType
ACT = mybir.ActivationFunctionType
AX = mybir.AxisListType
F32 = mybir.dt.float32
I32 = mybir.dt.int32

P = 128
SEQ = 256
D = 1024
TB = SEQ // P
DB = D // P
EPS = 1e-6
HEADS = 4
DK = 128
DV = 256
CHUNK = 64
RANK = 16
BANDS = 16
EMB = 1 + 2 * BANDS
FFN = 64
E = 32
TOPK = 4
LIMIT = 7.0
ALPHA = 1.702
GATE_TEMP = 16.0

Q0 = 0
K0 = Q0 + HEADS * DK
V0 = K0 + HEADS * DK
R0 = V0 + HEADS * DV
A0 = R0 + HEADS * DV
HY0 = A0 + 2 * RANK
GG0 = HY0 + 3 * D
GH0 = GG0 + D

SLOT = 2048
SLOTS = 16
HALF = 512
PAIRS = 4
MOE_SHIFT = 8

CAP = 64
GU_CH = 8
DN_CH = 4
CH = GU_CH + DN_CH
UNROLL = 4
NEG = -3.0e38

T_ID = 0
T_TRIF = T_ID + P
T_TRIB = T_TRIF + P
T_MASKB = T_TRIB + P
T_UP = T_MASKB + P
T_IOTA = T_UP + P
T_NEGT = T_IOTA + CAP
T_COLS = T_NEGT + TB

C_N1 = 0
C_N2 = C_N1 + DB
C_CW = C_N2 + DB
C_CB = C_CW + 3 * 3 * DB
C_HB = C_CB + 3 * DB
C_GN = C_HB + DB
C_FR = C_GN + DV // P
C_B1 = C_FR + 1
C_B2 = C_B1 + 1
C_ALL = C_B2 + 1

TWO_PI_HI = 6.28125
TWO_PI_MID = float((np.float32(2 * np.pi - TWO_PI_HI).view(np.uint32) & np.uint32(0xFFFFF000)).view(np.float32))
TWO_PI_LO = 2 * np.pi - TWO_PI_HI - TWO_PI_MID
ROUND = 1.5 * 2.0 ** 23
PI_IN = 3.1415925


def shape_tables():
    t = np.zeros((P, T_COLS), np.float32)
    s = np.arange(P)
    same = (s[:, None] // CHUNK) == (s[None, :] // CHUNK)
    t[:, T_ID:T_ID + P] = np.eye(P)
    t[:, T_TRIF:T_TRIF + P] = (same & (s[:, None] <= s[None, :])) / GATE_TEMP
    t[:, T_TRIB:T_TRIB + P] = (same & (s[:, None] >= s[None, :])) / GATE_TEMP
    t[:, T_MASKB:T_MASKB + P] = same & (s[:, None] > s[None, :])
    t[:, T_UP:T_UP + P] = s[:, None] < s[None, :]
    t[:, T_IOTA:T_IOTA + CAP] = np.arange(CAP)[None, :]
    lin = np.linspace(0.0, 1.0, SEQ, dtype=np.float32)
    t[:, T_NEGT:T_NEGT + TB] = -lin.reshape(TB, P).T
    w = 2 * np.pi * (np.arange(SEQ) + 0.5) / (2 * SEQ)
    ang = np.arange(SEQ)[:, None] * w[None, :]
    fwd = np.concatenate([np.cos(ang), np.sin(ang)], 1)
    inv = fwd.T / SEQ
    dft = np.concatenate([fwd.reshape(TB, P, 2 * SEQ).transpose(1, 0, 2).reshape(P, -1),
                          inv.reshape(4, P, SEQ).transpose(1, 0, 2).reshape(P, -1)], 1).astype(np.float32)
    omega = (np.float32(2.0 * np.pi) * np.arange(SEQ, dtype=np.float32) / np.float32(SEQ)).astype(np.float32)
    f = np.linspace(1e-4, BANDS - 1, BANDS, dtype=np.float32)
    a = (omega[:, None] * f[None, :]).astype(np.float32).astype(np.float64)
    z = np.concatenate([lin[:, None], np.cos(a), -np.sin(a)], 1).T.astype(np.float32)
    return np.ascontiguousarray(t), np.ascontiguousarray(dft), np.ascontiguousarray(z)


def psum_plan():
    names = ["cols", "biasT", "f1"] + [f"xT{n}" for n in range(4)] + ["f2"]
    names += [f"hf{tb}{c}" for tb in range(TB) for c in range(4)] + ["ksum"]
    names += [f"K{ri}{kc}{half}" for ri in range(2) for kc in range(2) for half in range(2)]
    names += [f"{n}{b}" for half in range(2) for n in ("hv", "hx") for b in range(4 * half, 4 * half + 4)]
    names += [f"zt{tb}{half}" for half in range(2) for tb in range(TB)]
    names += [f"h0{b}" for b in range(DB)]
    names += [f"Z{kc}{half}{ri}" for kc in range(2) for half in range(2) for ri in range(2)]
    names += [f"y{b}" for b in range(DB)]
    names += [f"q{h}" for h in range(HEADS)] + [f"k{h}" for h in range(HEADS)] + ["al"]
    names += [f"v{half}{tb}" for half in range(2) for tb in range(TB)] + ["lg0"]
    for h in range(HEADS):
        names += [f"bT{h}"] + ([f"lg{h + 1}"] if h + 1 < HEADS else []) + [f"sc{h}", f"ke{h}"]
        names += [f"U{h}{k}" for k in range(4)] + [f"o{h}"]
    names += [f"r{b}" for b in range(DB)]
    names += [f"oT{n}" for n in range(4)]
    for half in range(2):
        for n in ("gg", "wg", "gh", "wh"):
            names += [f"{n}{b}" for b in range(4 * half, 4 * half + 4)]
    names += [f"wo{half}{tb}" for half in range(2) for tb in range(TB)]
    names += [f"hnT{n}" for n in range(4)] + ["rl", "rank", "cnt", "cT"]
    names += [f"bd{tb}{half}" for tb in range(TB) for half in range(2)]
    return {n: (i % 8, i // 8 + 1) for i, n in enumerate(names)}, [(len(names) - b + 7) // 8 for b in range(8)]


FRONT = [("w_in", HY0 + 2 * D), ("w_in", HY0 + D), ("w_in", HY0 + 2 * D + HALF), ("w_in", HY0 + D + HALF),
         ("w_in", HY0), ("w_in", HY0 + HALF), ("w_in", Q0), ("w_in", K0), ("w_in", V0), ("w_in", V0 + HALF),
         ("w_in", R0), ("w_in", R0 + HALF),
         ("w_in", GG0), ("w_branch_gla", 0), ("w_in", GH0), ("w_branch_hy", 0),
         ("w_in", GG0 + HALF), ("w_branch_gla", HALF), ("w_in", GH0 + HALF), ("w_branch_hy", HALF),
         ("w_out", 0), ("w_out", HALF)]
LAST_TILE = ["hv3", "hx3", "hv7", "hx7", "h03", "h07", "q3", "k3", "v01", "v11", "r3", "r7",
             "gg3", "wg3", "gh3", "wh3", "gg7", "wg7", "gh7", "wh7", "wo01", "wo11"]
FIRST_PAIR = -len(FRONT) % PAIRS


def build(nc, ins, out):
    plan, bank_uses = psum_plan()
    with ExitStack() as ctx:
        def sb(name, shape, dt=F32):
            return ctx.enter_context(nc.sbuf_tensor(name, shape, dt))

        def sem(name):
            return ctx.enter_context(nc.semaphore(name))

        ring = sb("ring", [P, SLOTS * SLOT])
        x = sb("x", [P, TB, D])
        xn_area = sb("xn_area", [P, DB * SEQ])
        hy_area = sb("hy_area", [P, DB * SEQ])
        qk_area = sb("qk_area", [P, DB * SEQ])
        v_area = sb("v_area", [P, DB * SEQ])
        gla_area = sb("gla_area", [P, DB * SEQ])
        tmp_area = sb("tmp_area", [P, 5504])
        tab = sb("tab", [P, T_COLS])
        ones = sb("ones", [P, P])
        colw = sb("colw", [P, P])
        vecrows = sb("vecrows", [P, P])
        biasT = sb("biasT_sb", [P, E * 2 * DB])
        w_a = sb("w_a", [P, DB, 2 * RANK])
        small = sb("small", [P, 64])
        flag = sb("flag", [1, 1], I32)

        banks = [ctx.enter_context(nc.psum_tensor(f"bank{b}", [P, 512], F32)) for b in range(8)]

        ident = tab[:, T_ID:T_ID + P]
        tri = [tab[:, T_TRIF:T_TRIF + P], tab[:, T_TRIB:T_TRIB + P]]
        gla_mask = [tab[:, T_TRIF:T_TRIF + P].bitcast(I32), tab[:, T_MASKB:T_MASKB + P].bitcast(I32)]
        upper = tab[:, T_UP:T_UP + P]
        iota = tab[:, T_IOTA:T_IOTA + CAP]

        def col(c, rows=P):
            return colw[0:rows, c:c + 1]

        xnT = xn_area[:, :].rearrange("p (b t) -> p b t", b=DB)
        hnT = xnT
        ohyT = hy_area[:, :].rearrange("p (b t) -> p b t", b=DB)
        oglaT = gla_area[:, :].rearrange("p (b t) -> p b t", b=DB)
        mergedT = qk_area[:, :].rearrange("p (b t) -> p b t", b=DB)
        qkT = qk_area[:, :].rearrange("p (a h t) -> p a h t", a=2, h=HEADS)
        vtok = v_area[:, :].rearrange("p (a n) -> p a n", a=TB)
        xhat = vtok
        hn = vtok

        def hyreg(lo, n):
            return ring[:, 8 * SLOT + lo:8 * SLOT + lo + n]

        Kf = hyreg(0, 4096).rearrange("p (r k c) -> p r k c", r=2, k=2)
        hf = hyreg(4096, 4096).rearrange("p (a n) -> p a n", a=TB)
        Yf = hyreg(4096, 4096).rearrange("p (r k c) -> p r k c", r=2, k=2)
        zreg = hyreg(8192, 2048)
        zT = zreg.rearrange("p (b t) -> p b t", b=DB)
        sumh = zreg.rearrange("p (a n) -> p a n", a=TB)
        ztokreg = hyreg(10240, 2048)
        ztok = ztokreg.rearrange("p (a n) -> p a n", a=TB)
        dec = [zreg, ztokreg]
        dft = hyreg(12288, 1024).rearrange("p (a k) -> p a k", a=TB)
        idft = hyreg(13312, 1024).rearrange("p (a t) -> p a t", a=4)
        w3 = hyreg(14336, 2048)
        absdec = hy_area[:, :]
        sq = [qk_area[:, :], gla_area[:, :]]
        vbuf = gla_area[:, 0:1024].rearrange("p (b t) -> p b t", b=4)
        xbuf = gla_area[:, 1024:2048].rearrange("p (b t) -> p b t", b=4)
        ytmp = v_area[:, :].rearrange("p (q a n) -> p q a n", q=2, a=2)
        zfeat = tmp_area[0:EMB, 0:SEQ]
        w1 = tmp_area[0:EMB, 256:256 + FFN]
        w2 = tmp_area[0:FFN, 320:320 + FFN]
        arg = tmp_area[0:FFN, 384:640]
        turns = tmp_area[0:FFN, 640:896]
        s1 = tmp_area[0:FFN, 896:1152]
        s2 = tmp_area[0:FFN, 1152:1408]
        biasrows = tmp_area[:, 1408:1920].rearrange("p (a n) -> p a n", a=4)
        junk = tmp_area[:, 1920:2944]
        aT = gla_area[0:2 * RANK + 1, 0:SEQ]
        w2ext = gla_area[0:2 * RANK + 1, 256:256 + 2 * HEADS * DK].rearrange("p (a n) -> p a n", a=2)
        glog = tmp_area[:, 0:512].rearrange("p (d a n) -> p d a n", d=2, a=TB)
        bs = tmp_area[:, 512:1024].rearrange("p (d t) -> p d t", d=2)
        e1 = tmp_area[:, 1024:1536].rearrange("p (d t) -> p d t", d=2)
        kt = tmp_area[:, 1536:2048].rearrange("p (d t) -> p d t", d=2)
        ke = tmp_area[:, 2048:2560].rearrange("p (d t) -> p d t", d=2)
        qt = tmp_area[:, 2560:3072].rearrange("p (d t) -> p d t", d=2)
        ketok = tmp_area[:, 3072:3584].rearrange("p (d a n) -> p d a n", d=2, a=TB)
        scm = tmp_area[:, 3584:3840].rearrange("p (a n) -> p a n", a=TB)
        state = tmp_area[:, 3840:5376].rearrange("p (d n e) -> p d n e", d=2, n=3)
        silu_r = qk_area[:, :].rearrange("p (b t) -> p b t", b=DB)
        sg = tmp_area[:, 0:1024].rearrange("p (b t) -> p b t", b=4)
        mtmp = tmp_area[:, 1024:1536].rearrange("p (b t) -> p b t", b=2)
        junk2 = gla_area[:, 0:1024]
        rw = tmp_area[:, 1536:1792].rearrange("p (b e) -> p b e", b=DB)
        rb = tmp_area[:, 1792:1824]
        LW = E + 8
        logit = tmp_area[:, 1824:1824 + TB * LW].rearrange("p (a e) -> p a e", a=TB)
        gone = tmp_area[:, 1904:1904 + TB * LW].rearrange("p (a e) -> p a e", a=TB)
        mask = tmp_area[:, 1984:2048].rearrange("p (a e) -> p a e", a=TB)
        expo = tmp_area[:, 2048:2112].rearrange("p (a e) -> p a e", a=TB)
        top8 = tmp_area[:, 2112:2128].rearrange("p (a e) -> p a e", a=TB)
        PW = E + 2
        pos = tmp_area[:, 2128:2128 + TB * PW].rearrange("p (a e) -> p a e", a=TB)
        comb = tmp_area[:, 2196:2196 + TB * PW].rearrange("p (a e) -> p a e", a=TB)
        combT = tmp_area[0:E, 2264:2264 + SEQ]
        bdown = tmp_area[0:E, 2520:2520 + D]
        normf = tmp_area[:, 3544:3544 + D]
        sel = tmp_area[:, 4568:4824].rearrange("p (q a s) -> p q a s", q=2, a=TB)
        biasrow_end = 4824
        xeT = hy_area[:, 0:1024].rearrange("p (q b s) -> p q b s", q=2, b=DB)
        act = hy_area[:, 1024:1536].rearrange("p (b s) -> p b s", b=DB)
        gate = hy_area[:, 1536:2048].rearrange("p (b s) -> p b s", b=DB)
        sig = qk_area[:, 0:512].rearrange("p (b s) -> p b s", b=DB)
        up = qk_area[:, 512:1024].rearrange("p (b s) -> p b s", b=DB)
        yT = qk_area[:, 1024:1536].rearrange("p (b s) -> p b s", b=DB)
        ytok = gla_area[0:CAP, 0:D]
        selT = gla_area[0:CAP, D:D + 4 * SEQ].rearrange("p (q t) -> p q t", q=4)
        bias = biasT[:, :].rearrange("p (e b) -> p e b", e=E)
        def small_junk(a):
            return gla_area[:, 1280 + a * DV:1280 + (a + 1) * DV]

        ss1, sd1, rs1 = small[:, 0:2], small[:, 2:4], small[:, 4:6]
        kss, krs = small[:, 6:14], small[:, 14:22]
        ssg, rsg = small[:, 22:30], small[:, 30:38]
        ss2, rs2 = small[:, 38:40], small[:, 40:42]
        m1n, den = small[:, 42:44], small[:, 44:46]
        ss3, rs3 = small[:, 46:48], small[:, 48:50]
        cntm = small[:, 50:51]

        tile_ready = [sem(f"tile_ready{b}") for b in range(8)]
        tile_read = [sem(f"tile_read{b}") for b in range(8)]
        x_loaded = sem("x_loaded")
        tab_loaded = sem("tab_loaded")
        filt_loaded = sem("filt_loaded")
        dft_loaded = sem("dft_loaded")
        vec_loaded = sem("vec_loaded")
        gla_loaded = sem("gla_loaded")
        router_loaded = sem("router_loaded")
        front_loaded = [sem(f"front_loaded{p}") for p in range(PAIRS)]
        cleared = sem("cleared")
        dve_step = sem("dve_step")
        act_step = sem("act_step")
        ss_ready = sem("ss_ready")
        rs_ready = sem("rs_ready")
        xhat_ready = sem("xhat_ready")
        arg_ready = sem("arg_ready")
        sin_ready = sem("sin_ready")
        dec_ready = sem("dec_ready")
        hf_ready = sem("hf_ready")
        sq_ready = sem("sq_ready")
        sd_ready = sem("sd_ready")
        conv_mid = sem("conv_mid")
        z_ready = sem("z_ready")
        x0_ready = sem("x0_ready")
        Y_ready = sem("Y_ready")
        ohy_ready = sem("ohy_ready")
        softplus = sem("softplus")
        glog_ready = sem("glog_ready")
        b_ready = sem("b_ready")
        bdiff_ready = sem("bdiff_ready")
        exp_ready = sem("exp_ready")
        qk_scaled = sem("qk_scaled")
        ke_ready = sem("ke_ready")
        state_ready = sem("state_ready")
        osq_ready = sem("osq_ready")
        onorm_ready = sem("onorm_ready")
        ogla_ready = sem("ogla_ready")
        sig_ready = sem("sig_ready")
        merged_ready = sem("merged_ready")
        hn_ready = sem("hn_ready")
        expo_ready = sem("expo_ready")
        mask_ready = sem("mask_ready")
        comb_ready = sem("comb_ready")
        sel_ready = sem("sel_ready")
        moe_loaded = [sem(f"moe_loaded{s}") for s in range(SLOTS)]
        chunks_used = sem("chunks_used")
        gu_free = sem("gu_free")
        moe_step = sem("gate_biased")
        up_clipped = sem("up_clipped")
        up_gated = sem("up_gated")
        gate_ready = sem("gate_ready")
        sigm_ready = sem("sigm_ready")
        act_ready = sem("act_ready")
        yT_ready = sem("yT_ready")
        ytr_ready = sem("ytr_ready")
        y_ready = sem("y_ready")
        selT_psum = sem("selT_psum")
        selT_ready = sem("selT_ready")
        gather_psum = sem("gather_psum")
        xe_ready = sem("xe_ready")
        scat_psum = sem("scat_psum")
        scat_read = sem("scat_read")
        out_ready = sem("out_ready")
        stored = sem("stored")

        def bank(name):
            return banks[plan[name][0]]

        def filled(eng, name):
            b, g = plan[name]
            eng.wait_ge(tile_ready[b], g)

        def emptied(eng, name):
            b, g = plan[name]
            eng.wait_ge(tile_read[b], g)

        def fill(name):
            return tile_ready[plan[name][0]]

        def empty(name):
            return tile_read[plan[name][0]]

        def front_tile(c):
            p = (c + FIRST_PAIR) % PAIRS
            return ring[:, 2 * p * SLOT:(2 * p + 2) * SLOT].rearrange("p (b n) -> p b n", b=DB)

        def front_arrival(c):
            p = (c + FIRST_PAIR) % PAIRS
            first = (p - FIRST_PAIR) % PAIRS
            return front_loaded[p], 16 * ((c - first) // PAIRS + 1)

        def slot(s):
            return ring[:, s * SLOT:(s + 1) * SLOT]

        wgu, wdn = ins["w_gate_up"], ins["w_down"]

        block = ctx.enter_context(nc.Block())

        @block.sync
        def _(sp):
            sp.dma_start(x[:, :, :], ins["x"][0].rearrange("(a p) d -> p a d", p=P)).then_inc(x_loaded, 16)

            def front(c):
                w, c0 = FRONT[c]
                if c >= PAIRS:
                    filled(sp, LAST_TILE[c - PAIRS])
                src = ins[w][:, c0:c0 + HALF].rearrange("(b p) n -> p b n", p=P)
                sp.dma_start(front_tile(c), src).then_inc(front_arrival(c)[0], 16)

            def moe(n, e, j):
                s = (n + MOE_SHIFT) % SLOTS
                if j < GU_CH:
                    sp.dma_start(slot(s), wgu[e, j * P:(j + 1) * P, :]).then_inc(moe_loaded[s], 16)
                else:
                    r = (j - GU_CH) * 2 * P
                    sp.dma_start(slot(s).rearrange("p (c n) -> p c n", c=2),
                                 wdn[e, r:r + 2 * P, :].rearrange("(c p) n -> p c n", p=P)).then_inc(moe_loaded[s], 16)

            ahead = 12
            for c in range(ahead):
                front(c)
            sp.wait_ge(ohy_ready, DB)
            for n in range(8):
                moe(n, 0, n)
            for c in range(ahead, len(FRONT)):
                front(c)
            for n in range(8, 16):
                filled(sp, LAST_TILE[len(FRONT) - PAIRS + (n - 8) // 2])
                moe(n, n // CH, n % CH)
            with sp.Fori(0, E // UNROLL - 1) as i:
                for m in range(16, 16 + UNROLL * CH):
                    sp.wait_ge(chunks_used, i * (UNROLL * CH) + (m - 15))
                    moe(m, i * UNROLL + m // CH, m % CH)
            for n in range(E * CH - UNROLL * CH + 16, E * CH):
                sp.wait_ge(chunks_used, n - 15)
                moe(n, n // CH, n % CH)
            sp.wait_ge(out_ready, TB)
            sp.dma_start(out[0].rearrange("(a p) d -> p a d", p=P), x[:, :, :]).then_inc(stored, 16)
            sp.wait_ge(stored, 16)

        @block.tensor
        def _(pe):
            def begin(name):
                b, g = plan[name]
                if g > 1:
                    pe.wait_ge(tile_read[b], g - 1)
                return banks[b]

            def transposes(name, parts):
                t = begin(name)
                for o, i, idn in parts:
                    last = pe.transpose(t[o], i, idn)
                last.then_inc(fill(name), 1)

            def project(name, w, c, rhs):
                t = begin(name)
                for b in range(DB):
                    last = pe.matmul(t[:, 0:SEQ], w[:, b, c:c + P], rhs[:, b, :], start=(b == 0), stop=(b == DB - 1))
                last.then_inc(fill(name), 1)

            def arrive(c):
                s, v = front_arrival(c)
                pe.wait_ge(s, v)

            def four(names, c, rhs):
                arrive(c)
                w = front_tile(c)
                for k, n in enumerate(names):
                    project(n, w, k * P, rhs)

            pe.wait_ge(cleared, 2)
            pe.wait_ge(tab_loaded, 16)
            pe.wait_ge(vec_loaded, 16 * 12)
            transposes("cols", [((slice(None), slice(0, P)), vecrows[:, :], ident)])
            transposes("biasT", [((slice(None), slice(k * P, (k + 1) * P)), biasrows[:, k, :], ident) for k in range(4)])
            pe.wait_ge(filt_loaded, 16 * 5)
            t = begin("f1")
            pe.matmul(t[0:FFN, 0:SEQ], w1, zfeat, start=True, stop=True).then_inc(fill("f1"), 1)
            pe.wait_ge(xhat_ready, TB)
            for n in range(4):
                transposes(f"xT{n}", [((slice(None), slice((2 * k + a) * P, (2 * k + a + 1) * P)),
                                       xhat[:, a, (2 * n + k) * P:(2 * n + k + 1) * P], ident)
                                      for k in range(2) for a in range(TB)])
            t = begin("f2")
            pe.wait_ge(sin_ready, 1)
            pe.matmul(t[0:FFN, 0:SEQ], w2, s1, start=True, stop=True).then_inc(fill("f2"), 1)
            pe.wait_ge(sin_ready, 2)
            for a in range(TB):
                for c in range(4):
                    t = begin(f"hf{a}{c}")
                    pe.matmul(t[:, :], s2[:, a * P:(a + 1) * P], w3[0:FFN, c * 512:(c + 1) * 512],
                              start=True, stop=True).then_inc(fill(f"hf{a}{c}"), 1)
            t = begin("ksum")
            pe.wait_ge(sq_ready, TB)
            for b in range(DB):
                for k in range(4):
                    last = pe.matmul(t[:, b:b + 1], sq[k // 2][:, (k % 2) * D + b * P:(k % 2) * D + (b + 1) * P],
                                     ones[:, 0:1], start=(k == 0), stop=(k == 3))
            last.then_inc(fill("ksum"), 1)
            pe.wait_ge(sd_ready, 2 * TB)
            pe.wait_ge(dft_loaded, 16)
            for ri in range(2):
                for kc in range(2):
                    for half in range(2):
                        n = f"K{ri}{kc}{half}"
                        t = begin(n)
                        for a in range(TB):
                            src = sumh[:, a, half * 512:(half + 1) * 512] if ri == 0 else \
                                hf[:, a, D + half * 512:D + (half + 1) * 512]
                            last = pe.matmul(t[:, :], dft[:, a, ri * SEQ + kc * P:ri * SEQ + (kc + 1) * P], src,
                                             start=(a == 0), stop=(a == TB - 1))
                        last.then_inc(fill(n), 1)
            for n in range(4):
                emptied(pe, f"xT{n}")
            c = 0
            for half in range(2):
                for nm in ("hv", "hx"):
                    four([f"{nm}{b}" for b in range(4 * half, 4 * half + 4)], c, xnT)
                    c += 1
            for half in range(2):
                pe.wait_ge(z_ready, 4 * (half + 1))
                for a in range(TB):
                    transposes(f"zt{a}{half}", [((slice(None), slice(k * P, (k + 1) * P)),
                                                 zT[:, 4 * half + k, a * P:(a + 1) * P], ident) for k in range(4)])
            for half in range(2):
                four([f"h0{b}" for b in range(4 * half, 4 * half + 4)], 4 + half, xnT)
            for half in range(2):
                for a in range(TB):
                    emptied(pe, f"zt{a}{half}")
            for kc in range(2):
                for half in range(2):
                    for ri in range(2):
                        n = f"Z{kc}{half}{ri}"
                        t = begin(n)
                        for a in range(TB):
                            last = pe.matmul(t[:, :], dft[:, a, ri * SEQ + kc * P:ri * SEQ + (kc + 1) * P],
                                             ztok[:, a, half * 512:(half + 1) * 512], start=(a == 0), stop=(a == TB - 1))
                        last.then_inc(fill(n), 1)
            pe.wait_ge(Y_ready, 4)
            for b in range(DB):
                t = begin(f"y{b}")
                for k in range(4):
                    last = pe.matmul(t[:, 0:SEQ], Yf[:, k // 2, k % 2, b * P:(b + 1) * P], idft[:, k, :],
                                     start=(k == 0), stop=(k == 3))
                last.then_inc(fill(f"y{b}"), 1)
            four([f"q{h}" for h in range(HEADS)], 6, xnT)
            four([f"k{h}" for h in range(HEADS)], 7, xnT)
            t = begin("al")
            for b in range(DB):
                last = pe.matmul(t[0:2 * RANK, 0:SEQ], w_a[:, b, :], xnT[:, b, :], start=(b == 0), stop=(b == DB - 1))
            last.then_inc(fill("al"), 1)
            for half in range(2):
                arrive(8 + half)
                for a in range(TB):
                    t = begin(f"v{half}{a}")
                    for b in range(DB):
                        last = pe.matmul(t[:, :], xnT[:, b, a * P:(a + 1) * P], front_tile(8 + half)[:, b, :],
                                         start=(b == 0), stop=(b == DB - 1))
                    last.then_inc(fill(f"v{half}{a}"), 1)

            def gate_logits(h):
                t = begin(f"lg{h}")
                if h == 0:
                    emptied(pe, "al")
                for d in range(2):
                    for a in range(TB):
                        o = (d * TB + a) * P
                        last = pe.matmul(t[:, o:o + P], aT[:, a * P:(a + 1) * P], w2ext[:, d, h * DK:(h + 1) * DK],
                                         start=True, stop=True)
                last.then_inc(fill(f"lg{h}"), 1)

            pe.wait_ge(cleared, 5)
            pe.wait_ge(gla_loaded, 16 * 4)
            gate_logits(0)
            for half in range(2):
                for a in range(TB):
                    emptied(pe, f"v{half}{a}")
            for h in range(HEADS):
                hv = slice(h * DV, (h + 1) * DV)
                t = begin(f"bT{h}")
                pe.wait_ge(glog_ready, h + 1)
                for d in range(2):
                    for a in range(TB):
                        o = (d * TB + a) * P
                        last = pe.matmul(t[:, o:o + P], glog[:, d, a, :], tri[d], start=True, stop=True)
                last.then_inc(fill(f"bT{h}"), 1)
                if h + 1 < HEADS:
                    gate_logits(h + 1)
                t = begin(f"sc{h}")
                pe.wait_ge(qk_scaled, 4 * (h + 1))
                for d in range(2):
                    for a in range(TB):
                        o = (d * TB + a) * P
                        last = pe.matmul(t[:, o:o + P], kt[:, d, a * P:(a + 1) * P], qt[:, d, a * P:(a + 1) * P],
                                         start=True, stop=True)
                last.then_inc(fill(f"sc{h}"), 1)
                pe.wait_ge(ke_ready, 2 * (h + 1))
                transposes(f"ke{h}", [((slice(None), slice((d * TB + a) * P, (d * TB + a + 1) * P)),
                                       ke[:, d, a * P:(a + 1) * P], ident) for d in range(2) for a in range(TB)])
                emptied(pe, f"ke{h}")
                for k, parts in enumerate((((0, 0), (0, 2)), ((0, 1), (1, 1)), ((1, 2),), ((1, 3),))):
                    t = begin(f"U{h}{k}")
                    for m, (d, n) in enumerate(parts):
                        r = (n % 2) * CHUNK
                        last = pe.matmul(t[:, m * DV:(m + 1) * DV], ketok[r:r + CHUNK, d, n // 2, :],
                                         vtok[r:r + CHUNK, n // 2, hv], start=True, stop=True)
                    last.then_inc(fill(f"U{h}{k}"), 1)
                t = begin(f"o{h}")
                emptied(pe, f"sc{h}")
                pe.wait_ge(state_ready, 6 * (h + 1))
                for a in range(TB):
                    o = a * DV
                    pe.matmul(t[:, o:o + DV], scm[:, a, :], vtok[:, a, hv], start=True, stop=True)
                    for n in (2 * a, 2 * a + 1):
                        r = (n % 2) * CHUNK
                        for d in range(2):
                            m = n - 1 if d == 0 else 2 - n
                            if m >= 0:
                                last = pe.matmul(t[r:r + CHUNK, o:o + DV], qt[:, d, n * CHUNK:(n + 1) * CHUNK],
                                                 state[:, d, m, :], start=False, stop=True, skip_group_check=True)
                last.then_inc(fill(f"o{h}"), 1)
            four([f"r{b}" for b in range(4)], 10, xnT)
            four([f"r{b}" for b in range(4, 8)], 11, xnT)
            pe.wait_ge(onorm_ready, 8)
            for n in range(4):
                transposes(f"oT{n}", [((slice(None), slice((2 * k + a) * P, (2 * k + a + 1) * P)),
                                       vtok[:, a, (2 * n + k) * P:(2 * n + k + 1) * P], ident)
                                      for k in range(2) for a in range(TB)])
            pe.wait_ge(ohy_ready, DB)
            for half in range(2):
                bs4 = range(4 * half, 4 * half + 4)
                four([f"gg{b}" for b in bs4], 12 + 4 * half, xnT)
                pe.wait_ge(ogla_ready, DB)
                four([f"wg{b}" for b in bs4], 13 + 4 * half, oglaT)
                four([f"gh{b}" for b in bs4], 14 + 4 * half, xnT)
                four([f"wh{b}" for b in bs4], 15 + 4 * half, ohyT)
            pe.wait_ge(merged_ready, DB)
            for half in range(2):
                arrive(20 + half)
                for a in range(TB):
                    t = begin(f"wo{half}{a}")
                    for b in range(DB):
                        last = pe.matmul(t[:, :], mergedT[:, b, a * P:(a + 1) * P], front_tile(20 + half)[:, b, :],
                                         start=(b == 0), stop=(b == DB - 1))
                    last.then_inc(fill(f"wo{half}{a}"), 1)
            pe.wait_ge(hn_ready, TB)
            for n in range(4):
                transposes(f"hnT{n}", [((slice(None), slice((2 * k + a) * P, (2 * k + a + 1) * P)),
                                        hn[:, a, (2 * n + k) * P:(2 * n + k + 1) * P], ident)
                                       for k in range(2) for a in range(TB)])
            for n in range(4):
                emptied(pe, f"hnT{n}")
            pe.wait_ge(router_loaded, 16 * 4)
            t = begin("rl")
            for a in range(TB):
                for b in range(DB):
                    last = pe.matmul(t[:, a * E:(a + 1) * E], hnT[:, b, a * P:(a + 1) * P], rw[:, b, :],
                                     start=(b == 0), stop=(b == DB - 1))
            last.then_inc(fill("rl"), 1)
            pe.wait_ge(mask_ready, 1)
            t = begin("rank")
            pe.matmul(t[:, 0:E], upper, mask[:, 0, :], start=True, stop=True)
            pe.matmul(t[:, E:2 * E], ones[:, :], mask[:, 0, :], start=True, stop=False)
            pe.matmul(t[:, E:2 * E], upper, mask[:, 1, :], start=False, stop=True).then_inc(fill("rank"), 1)
            t = begin("cnt")
            pe.matmul(t[:, 0:E], ones[:, :], mask[:, 0, :], start=True, stop=False)
            pe.matmul(t[:, 0:E], ones[:, :], mask[:, 1, :], start=False, stop=True).then_inc(fill("cnt"), 1)
            pe.wait_ge(comb_ready, 1)
            t = begin("cT")
            for a in range(TB):
                last = pe.transpose(t[0:E, a * P:(a + 1) * P], comb[:, a, 1:1 + E], ident)
            last.then_inc(fill("cT"), 1)
            emptied(pe, "cT")
            for a in range(TB):
                for half in range(2):
                    t = begin(f"bd{a}{half}")
                    pe.matmul(t[:, :], combT[:, a * P:(a + 1) * P], bdown[:, half * 512:(half + 1) * 512],
                              start=True, stop=True).then_inc(fill(f"bd{a}{half}"), 1)
            for b in range(8):
                pe.wait_ge(tile_read[b], bank_uses[b])

            def select_T(q):
                for a in range(TB):
                    last = pe.transpose(banks[2][0:CAP, a * P:(a + 1) * P], sel[:, q % 2, a, :], ident)
                last.then_inc(selT_psum, 1)

            def gather(q, count):
                pe.wait_ge(selT_ready, count)
                for b in range(DB):
                    for a in range(TB):
                        last = pe.matmul(banks[2][:, b * CAP:(b + 1) * CAP], hn[:, a, b * P:(b + 1) * P],
                                         sel[:, q % 2, a, :], start=(a == 0), stop=(a == TB - 1))
                last.then_inc(gather_psum, 1)

            def y_by_slot():
                for b in range(DB):
                    last = pe.transpose(banks[4 + b // 4][0:CAP, (b % 4) * P:(b % 4 + 1) * P], yT[:, b, :], ident)
                last.then_inc(ytr_ready, 1)

            def scatter(q, e):
                pe.wait_ge(y_ready, e + 1)
                for k in range(4):
                    pe.wait_ge(scat_read, 4 * e + k + 1)
                    pe.matmul(banks[6 + k % 2][:, :], selT[:, q % 4, (k // 2) * P:(k // 2 + 1) * P],
                              ytok[:, (k % 2) * 512:(k % 2 + 1) * 512], start=True, stop=True).then_inc(scat_psum, 1)

            pe.wait_ge(sel_ready, 1)
            select_T(0)
            gather(0, 1)
            with pe.Fori(0, E // UNROLL) as i:
                for q in range(UNROLL):
                    e = i * UNROLL + q
                    pe.wait_ge(xe_ready, e + 1)
                    pe.wait_ge(gu_free, e + 1)
                    for j in range(GU_CH):
                        if j == 1:
                            pe.wait_ge(yT_ready, e + 1)
                        if j == 2:
                            pe.wait_ge(sel_ready, e + 2)
                        n = q * CH + j
                        s = (n + MOE_SHIFT) % SLOTS
                        pe.wait_ge(moe_loaded[s], (i * 3 + (n // SLOTS + 1)) * 16)
                        for f in range(2 * DB):
                            last = pe.matmul(banks[f // DB][:, (f % DB) * CAP:(f % DB + 1) * CAP],
                                             slot(s)[:, f * P:(f + 1) * P], xeT[:, q % 2, j, :],
                                             start=(j == 0 and f % DB == 0), stop=(j == GU_CH - 1), skip_group_check=True)
                        last.then_inc(chunks_used, 1)
                    y_by_slot()
                    select_T(q + 1)
                    scatter(q - 1, e)
                    gather(q + 1, e + 2)
                    pe.wait_ge(act_ready, e + 1)
                    for j in range(GU_CH, CH):
                        n = q * CH + j
                        s = (n + MOE_SHIFT) % SLOTS
                        pe.wait_ge(moe_loaded[s], (i * 3 + (n // SLOTS + 1)) * 16)
                        for c in range(2):
                            f = 2 * (j - GU_CH) + c
                            for b in range(DB):
                                last = pe.matmul(banks[3][:, b * CAP:(b + 1) * CAP],
                                                 slot(s)[:, c * D + b * P:c * D + (b + 1) * P], act[:, f, :],
                                                 start=(f == 0 and b == 0), stop=(f == DB - 1), skip_group_check=True)
                        last.then_inc(chunks_used, 1)
            pe.wait_ge(yT_ready, E + 1)
            y_by_slot()
            scatter(UNROLL - 1, E)

        @block.scalar
        def _(sc):
            steps = [0]

            def link(i):
                steps[0] += 1
                i.then_inc(act_step, 1)
                sc.wait_ge(act_step, steps[0])

            sc.dma_start(tab[:, :], ins["shape_table"]).then_inc(tab_loaded, 16)
            sc.wait_ge(cleared, 2)
            rows = [("norm1_w", C_N1), ("norm2_w", C_N2), ("hy_conv_b", C_CB), ("hy_bias", C_HB), ("gla_norm_w", C_GN)]
            for nm, r in rows:
                n = ins[nm].shape[0] // P
                sc.dma_start(vecrows[r:r + n, :], ins[nm].rearrange("(a n) -> a n", n=P)).then_inc(vec_loaded, 16)
            sc.dma_start(vecrows[C_CW:C_CW + 9 * DB, :],
                         ins["hy_conv_w"].rearrange("k (a n) -> (k a) n", n=P)).then_inc(vec_loaded, 16)
            for nm, r in (("hy_freq", C_FR), ("hy_ffn_b1", C_B1), ("hy_ffn_b2", C_B2)):
                sc.dma_start(vecrows[r:r + 1, 0:FFN], ins[nm].rearrange("(a n) -> a n", a=1)).then_inc(vec_loaded, 16)
            bsrc = ins["b_gate_up"].rearrange("e (b n) -> (e b) n", n=P).rearrange("(a p) n -> p a n", p=P)
            sc.dma_start(biasrows[:, 0:2, :], bsrc[:, 0:2, :]).then_inc(vec_loaded, 16)
            sc.dma_start(biasrows[:, 2:4, :], bsrc[:, 2:4, :]).then_inc(vec_loaded, 16)
            sc.dma_start(w_a[:, :, :], ins["w_in"][:, A0:A0 + 2 * RANK].rearrange("(b p) n -> p b n", p=P)).then_inc(vec_loaded, 16)
            sc.dma_start(zfeat, ins["filter_features"]).then_inc(filt_loaded, 16)
            sc.dma_start(w1, ins["hy_ffn_w1"]).then_inc(filt_loaded, 16)
            sc.dma_start(w2, ins["hy_ffn_w2"]).then_inc(filt_loaded, 16)
            sc.dma_start(w3[0:FFN, :], ins["hy_ffn_w3"]).then_inc(filt_loaded, 16)
            sc.dma_start(absdec, ins["hy_decay"].rearrange("(o a) n -> o (a n)", o=1).to_broadcast([P, 2 * D])).then_inc(filt_loaded, 16)
            sc.dma_start(hyreg(12288, 2048), ins["dft_table"]).then_inc(dft_loaded, 16)

            def sumsq(src, scratch, dst):
                return nc.scalar.activation(scratch, src, ACT.Square, accum_out=dst)

            sc.wait_ge(x_loaded, 16)
            link(sumsq(x[:, 0, :], junk, ss1[:, 0:1]))
            link(sumsq(x[:, 1, :], junk, ss1[:, 1:2]))
            sc.wait_ge(cleared, 3)
            nc.scalar.activation(sd1, ss1, ACT.Sqrt, bias=small[:, 63:64], scale=1.0 / D).then_inc(ss_ready, 1)
            filled(sc, "biasT")
            nc.scalar.copy(biasT[:, :], bank("biasT")[:, :]).then_inc(empty("biasT"), 1)
            sc.wait_ge(rs_ready, 1)
            for a in range(TB):
                nc.scalar.mul(xhat[:, a, :], x[:, a, :], rs1[:, a:a + 1]).then_inc(xhat_ready, 1)
            sc.wait_ge(filt_loaded, 16 * 5)
            link(nc.scalar.activation(absdec, absdec, ACT.Abs))
            for a in range(TB):
                nc.scalar.activation(dec[a], absdec, ACT.Exp, scale=tab[:, T_NEGT + a:T_NEGT + a + 1]).then_inc(dec_ready, 1)
            sc.wait_ge(arg_ready, 1)
            nc.scalar.activation(s1, arg, ACT.Sin).then_inc(sin_ready, 1)
            sc.wait_ge(arg_ready, 2)
            nc.scalar.activation(s2, arg, ACT.Sin).then_inc(sin_ready, 1)
            for a in range(TB):
                sc.wait_ge(hf_ready, 1)
                nc.scalar.activation(sq[a], hf[:, a, :], ACT.Square).then_inc(sq_ready, 1)
            filled(sc, "ksum")
            nc.scalar.activation(kss, bank("ksum")[:, 0:DB], ACT.Sqrt, bias=small[:, 63:64]).then_inc(empty("ksum"), 1)
            for ri in range(2):
                for kc in range(2):
                    for half in range(2):
                        n = f"K{ri}{kc}{half}"
                        filled(sc, n)
                        nc.scalar.copy(Kf[:, ri, kc, half * 512:(half + 1) * 512], bank(n)[:, :]).then_inc(empty(n), 1)

            def conv_centre(name, dst, blk):
                filled(sc, name)
                nc.scalar.activation(dst, bank(name)[:, 0:SEQ], ACT.Identity, bias=col(C_CB + blk),
                                     scale=col(C_CW + 3 * DB + blk)).then_inc(conv_mid, 1)

            emptied(sc, "cols")
            emptied(sc, "ksum")
            for half in range(2):
                for b in range(4 * half, 4 * half + 4):
                    if half:
                        sc.wait_ge(z_ready, b - 3)
                    conv_centre(f"hv{b}", vbuf[:, b % 4, :], 2 * DB + b)
                for b in range(4 * half, 4 * half + 4):
                    conv_centre(f"hx{b}", xbuf[:, b % 4, :], DB + b)
            for half in range(2):
                for a in range(TB):
                    n = f"zt{a}{half}"
                    filled(sc, n)
                    nc.scalar.copy(ztok[:, a, half * 512:(half + 1) * 512], bank(n)[:, :]).then_inc(empty(n), 1)
            for b in range(DB):
                conv_centre(f"h0{b}", ohyT[:, b, :], b)
            for a, nm in enumerate("qk"):
                for h in range(HEADS):
                    filled(sc, f"{nm}{h}")
                    nc.scalar.copy(qkT[:, a, h, :], bank(f"{nm}{h}")[:, 0:SEQ]).then_inc(empty(f"{nm}{h}"), 1)
            filled(sc, "al")
            sc.wait_ge(cleared, 5)
            nc.scalar.copy(aT[0:2 * RANK, :], bank("al")[0:2 * RANK, 0:SEQ]).then_inc(empty("al"), 1)
            sc.wait_ge(Y_ready, 4)
            for half in range(2):
                for a in range(TB):
                    n = f"v{half}{a}"
                    filled(sc, n)
                    nc.scalar.copy(vtok[:, a, half * 512:(half + 1) * 512], bank(n)[:, :]).then_inc(empty(n), 1)

            def softplus_part(h):
                filled(sc, f"lg{h}")
                g2 = tmp_area[:, 0:512]
                if h:
                    filled(sc, f"bT{h - 1}")
                link(nc.scalar.activation(g2, bank(f"lg{h}")[:, :], ACT.Abs))
                link(nc.scalar.activation(g2, g2, ACT.Exp, scale=-1.0))
                nc.scalar.activation(g2, g2, ACT.Ln, bias=small[:, 62:63]).then_inc(softplus, 1)

            softplus_part(0)
            for h in range(HEADS):
                filled(sc, f"bT{h}")
                nc.scalar.copy(tmp_area[:, 512:1024], bank(f"bT{h}")[:, :]).then_inc(empty(f"bT{h}"), 1)
                emptied(sc, f"bT{h}")
                if h:
                    sc.wait_ge(state_ready, 6 * h)
                    filled(sc, f"sc{h - 1}")
                    filled(sc, f"ke{h - 1}")
                nc.scalar.activation(tmp_area[:, 1024:1536], tmp_area[:, 512:1024], ACT.Exp).then_inc(exp_ready, 1)
                nc.scalar.activation(tmp_area[:, 1536:2048], tmp_area[:, 512:1024], ACT.Exp, scale=-1.0).then_inc(exp_ready, 1)
                sc.wait_ge(bdiff_ready, 2 * (h + 1))
                nc.scalar.activation(tmp_area[:, 2048:2560], tmp_area[:, 2048:2560], ACT.Exp).then_inc(exp_ready, 1)
                if h + 1 < HEADS:
                    softplus_part(h + 1)
                filled(sc, f"ke{h}")
                nc.scalar.copy(tmp_area[:, 3072:3584], bank(f"ke{h}")[:, :]).then_inc(empty(f"ke{h}"), 1)
                filled(sc, f"o{h}")
                nc.scalar.copy(vtok[:, :, h * DV:(h + 1) * DV],
                               bank(f"o{h}")[:, :].rearrange("p (a n) -> p a n", a=TB)).then_inc(empty(f"o{h}"), 1)
                emptied(sc, f"o{h}")
                for a in range(TB):
                    last = sumsq(vtok[:, a, h * DV:(h + 1) * DV], small_junk(a), ssg[:, a * HEADS + h:a * HEADS + h + 1])
                last.then_inc(osq_ready, 1)
            sc.wait_ge(osq_ready, HEADS)
            nc.scalar.activation(ssg, ssg, ACT.Sqrt, bias=small[:, 63:64], scale=1.0 / DV).then_inc(ss_ready, 1)

            def sigmoid_of(name, k, count):
                filled(sc, name)
                nc.scalar.activation(sg[:, k, :], bank(name)[:, 0:SEQ], ACT.Sigmoid).then_inc(sig_ready, 1)

            filled(sc, f"o{HEADS - 1}")
            for b in range(DB):
                if b >= 4:
                    emptied(sc, f"r{b - 4}")
                sigmoid_of(f"r{b}", b % 4, b + 1)
            for half in range(2):
                for b in range(4 * half, 4 * half + 4):
                    emptied(sc, f"r{4 + b % 4}" if not half else f"wh{b - 4}")
                    filled(sc, f"gg{b}")
                    nc.scalar.activation(sg[:, b % 4, :], bank(f"gg{b}")[:, 0:SEQ], ACT.Sigmoid).then_inc(empty(f"gg{b}"), 1)
                for b in range(4 * half, 4 * half + 4):
                    emptied(sc, f"wg{b}")
                    filled(sc, f"gh{b}")
                    nc.scalar.activation(sg[:, b % 4, :], bank(f"gh{b}")[:, 0:SEQ], ACT.Sigmoid).then_inc(empty(f"gh{b}"), 1)
            sc.wait_ge(ogla_ready, DB)
            sc.dma_start(rw, ins["router_w"].rearrange("(b p) e -> p b e", p=P)).then_inc(router_loaded, 16)
            sc.dma_start(rb, ins["router_b"].rearrange("(o n) -> o n", o=1).to_broadcast([P, E])).then_inc(router_loaded, 16)
            sc.dma_start(bdown, ins["b_down"]).then_inc(router_loaded, 16)
            sc.dma_start(normf, ins["norm_f_w"].rearrange("(o n) -> o n", o=1).to_broadcast([P, D])).then_inc(router_loaded, 16)
            for b in range(4, 8):
                filled(sc, f"wg{b}")
            for a in range(TB):
                emptied(sc, f"wo1{a}")
                emptied(sc, f"wo0{a}")
                link(sumsq(x[:, a, :], junk2, ss2[:, a:a + 1]))
            nc.scalar.activation(ss2, ss2, ACT.Sqrt, bias=small[:, 63:64], scale=1.0 / D).then_inc(ss_ready, 1)
            sc.wait_ge(rs_ready, 4)
            for a in range(TB):
                nc.scalar.mul(hn[:, a, :], x[:, a, :], rs2[:, a:a + 1]).then_inc(hn_ready, 1)
            sc.wait_ge(expo_ready, 1)
            for a in range(TB):
                nc.scalar.activation(expo[:, a, :], logit[:, a, 0:E], ACT.Exp, bias=m1n[:, a:a + 1]).then_inc(expo_ready, 1)
            filled(sc, "cT")
            nc.scalar.copy(combT, bank("cT")[0:E, 0:SEQ]).then_inc(empty("cT"), 1)

            def copy_selT(q, count):
                sc.wait_ge(selT_psum, count)
                nc.scalar.copy(selT[:, q % 4, :], banks[2][0:CAP, 0:SEQ]).then_inc(selT_ready, 1)

            def copy_y(count):
                sc.wait_ge(ytr_ready, count)
                for half in range(2):
                    last = nc.scalar.copy(ytok[:, half * 512:(half + 1) * 512], banks[4 + half][0:CAP, :])
                last.then_inc(y_ready, 1)

            copy_selT(0, 1)
            with sc.Fori(0, E // UNROLL) as i:
                for q in range(UNROLL):
                    e = i * UNROLL + q
                    sc.wait_ge(gate_ready, e + 1)
                    nc.scalar.activation(sig, gate, ACT.Sigmoid, scale=ALPHA).then_inc(sigm_ready, 1)
                    copy_y(e + 1)
                    copy_selT(q + 1, e + 2)
                    sc.wait_ge(chunks_used, (e + 1) * CH)
                    nc.scalar.copy(yT, banks[3][:, :].rearrange("p (b s) -> p b s", b=DB)).then_inc(yT_ready, 1)
            copy_y(E + 1)
            for a in range(TB):
                sc.wait_ge(scat_read, 2 + 4 * (E + 1))
                link(sumsq(x[:, a, :], v_area[:, 0:D], ss3[:, a:a + 1]))
            nc.scalar.activation(ss3, ss3, ACT.Sqrt, bias=small[:, 63:64], scale=1.0 / D).then_inc(ss_ready, 1)

        @block.vector
        def _(dve):
            steps = [0]

            def link(i):
                steps[0] += 1
                i.then_inc(dve_step, 1)
                dve.wait_ge(dve_step, steps[0])

            nc.vector.memset(ones[:, :], 1.0).then_inc(cleared, 1)
            nc.vector.memset(vecrows[:, :], 0.0).then_inc(cleared, 1)
            nc.vector.memset(small[:, 63:64], EPS)
            nc.vector.memset(small[:, 62:63], 1.0).then_inc(cleared, 1)
            filled(dve, "cols")
            nc.vector.tensor_copy(colw[:, :], bank("cols")[:, 0:P]).then_inc(empty("cols"), 1)
            emptied(dve, "cols")
            dve.wait_ge(ss_ready, 1)
            nc.vector.reciprocal(rs1, sd1).then_inc(rs_ready, 1)

            def sine_argument(name, bias_col):
                filled(dve, name)
                i = nc.vector.tensor_scalar(arg, bank(name)[0:FFN, 0:SEQ], col(bias_col, FFN), col(C_FR, FFN), ALU.add, ALU.mult)
                i.then_inc(empty(name), 1)
                emptied(dve, name)
                link(nc.vector.tensor_scalar(turns, arg, 1.0 / (2 * np.pi), ROUND, ALU.mult, ALU.add))
                link(nc.vector.tensor_scalar(turns, turns, -ROUND, None, ALU.add))
                for part in (TWO_PI_HI, TWO_PI_MID, TWO_PI_LO):
                    link(nc.vector.scalar_tensor_tensor(out=arg, in0=turns, scalar=-part, in1=arg, op0=ALU.mult, op1=ALU.add))
                nc.vector.tensor_scalar(arg, arg, PI_IN, -PI_IN, ALU.min, ALU.max).then_inc(arg_ready, 1)

            sine_argument("f1", C_B1)
            for n in range(4):
                filled(dve, f"xT{n}")
                for k in range(2):
                    last = nc.vector.tensor_scalar(xnT[:, 2 * n + k, :], bank(f"xT{n}")[:, k * SEQ:(k + 1) * SEQ],
                                                   col(C_N1 + 2 * n + k), None, ALU.mult)
                last.then_inc(empty(f"xT{n}"), 1)
            dve.wait_ge(sin_ready, 1)
            sine_argument("f2", C_B2)
            dve.wait_ge(dec_ready, TB)
            for a in range(TB):
                for c in range(4):
                    n = f"hf{a}{c}"
                    filled(dve, n)
                    nc.vector.tensor_tensor(hf[:, a, c * 512:(c + 1) * 512], bank(n)[:, :], dec[a][:, c * 512:(c + 1) * 512],
                                            ALU.mult).then_inc(empty(n), 1)
            for c in range(2, 4):
                emptied(dve, f"hf0{c}")
            nc.vector.memset(hf[0:1, 0, D:2 * D], 0.0).then_inc(hf_ready, 1)
            dve.wait_ge(hf_ready, 1)
            for a in range(TB):
                nc.vector.tensor_tensor(sumh[:, a, :], hf[:, a, 0:D], hf[:, a, D:2 * D], ALU.add).then_inc(sd_ready, 1)
            dve.wait_ge(sq_ready, TB)
            for a in range(TB):
                nc.vector.tensor_tensor(hf[:, a, D:2 * D], hf[:, a, 0:D], hf[:, a, D:2 * D], ALU.subtract).then_inc(sd_ready, 1)
            emptied(dve, "ksum")
            nc.vector.reciprocal(krs, kss).then_inc(rs_ready, 1)

            mids = [0]

            def conv_sides(name, dst, blk):
                mids[0] += 1
                dve.wait_ge(conv_mid, mids[0])
                link(nc.vector.scalar_tensor_tensor(out=dst[:, 1:SEQ], in0=bank(name)[:, 0:SEQ - 1], scalar=col(C_CW + blk),
                                                    in1=dst[:, 1:SEQ], op0=ALU.mult, op1=ALU.add))
                i = nc.vector.scalar_tensor_tensor(out=dst[:, 0:SEQ - 1], in0=bank(name)[:, 1:SEQ],
                                                   scalar=col(C_CW + 6 * DB + blk), in1=dst[:, 0:SEQ - 1],
                                                   op0=ALU.mult, op1=ALU.add)
                i.then_inc(empty(name), 1)

            for half in range(2):
                for b in range(4 * half, 4 * half + 4):
                    conv_sides(f"hv{b}", vbuf[:, b % 4, :], 2 * DB + b)
                for b in range(4 * half, 4 * half + 4):
                    conv_sides(f"hx{b}", xbuf[:, b % 4, :], DB + b)
                    emptied(dve, f"hv{b}")
                    emptied(dve, f"hx{b}")
                    filled(dve, "K111")
                    nc.vector.tensor_tensor(zT[:, b, :], vbuf[:, b % 4, :], xbuf[:, b % 4, :], ALU.mult).then_inc(z_ready, 1)
            for b in range(DB):
                conv_sides(f"h0{b}", ohyT[:, b, :], b)
            for half in range(2):
                for a in range(TB):
                    filled(dve, f"zt{a}{half}")
            for b in range(DB):
                last = nc.vector.tensor_scalar(zT[:, b, :], zT[:, b, :], col(C_HB + b), None, ALU.mult)
            link(last)
            for ri in range(2):
                for kc in range(2):
                    for half in range(2):
                        emptied(dve, f"K{ri}{kc}{half}")
            for kc in range(2):
                for half in range(2):
                    cs = slice(half * 512, (half + 1) * 512)
                    zr, zi = f"Z{kc}{half}0", f"Z{kc}{half}1"
                    filled(dve, zr)
                    filled(dve, zi)
                    tmp = ytmp[:, half]
                    if kc:
                        dve.wait_ge(Y_ready, half + 1)
                    nc.vector.tensor_tensor(Yf[:, 0, kc, cs], bank(zr)[:, :], Kf[:, 0, kc, cs], ALU.mult)
                    nc.vector.tensor_tensor(tmp[:, 0, :], bank(zi)[:, :], Kf[:, 1, kc, cs], ALU.mult)
                    nc.vector.tensor_tensor(Yf[:, 1, kc, cs], bank(zr)[:, :], Kf[:, 1, kc, cs], ALU.mult).then_inc(empty(zr), 1)
                    nc.vector.tensor_tensor(tmp[:, 1, :], bank(zi)[:, :], Kf[:, 0, kc, cs], ALU.mult).then_inc(empty(zi), 1)
                    emptied(dve, zi)
                    nc.vector.tensor_tensor(Yf[:, 0, kc, cs], Yf[:, 0, kc, cs], tmp[:, 0, :], ALU.subtract)
                    nc.vector.tensor_tensor(Yf[:, 1, kc, cs], Yf[:, 1, kc, cs], tmp[:, 1, :], ALU.add).then_inc(Y_ready, 1)
            dve.wait_ge(rs_ready, 2)
            for b in range(DB):
                filled(dve, f"y{b}")
                nc.vector.scalar_tensor_tensor(out=zT[:, b, :], in0=bank(f"y{b}")[:, 0:SEQ], scalar=krs[:, b:b + 1],
                                               in1=zT[:, b, :], op0=ALU.mult, op1=ALU.add).then_inc(empty(f"y{b}"), 1)
                emptied(dve, f"y{b}")
                nc.vector.tensor_tensor(ohyT[:, b, :], zT[:, b, :], ohyT[:, b, :], ALU.mult).then_inc(ohy_ready, 1)

            dve.wait_ge(z_ready, DB)
            nc.vector.memset(gla_area[0:2 * RANK + 1, 0:1280], 0.0).then_inc(cleared, 1)
            dve.wait_ge(cleared, 4)
            nc.vector.memset(gla_area[2 * RANK:2 * RANK + 1, 0:SEQ], 1.0).then_inc(cleared, 1)
            link(nc.vector.memset(tmp_area[:, 3584:3840], 0.0))

            def log_gates(h):
                dve.wait_ge(softplus, h + 1)
                i = nc.vector.scalar_tensor_tensor(out=tmp_area[:, 0:512], in0=bank(f"lg{h}")[:, :], scalar=0.0,
                                                   in1=tmp_area[:, 0:512], op0=ALU.min, op1=ALU.subtract)
                i.then_inc(empty(f"lg{h}"), 1)
                emptied(dve, f"lg{h}")
                nc.vector.engine_nop().then_inc(glog_ready, 1)

            log_gates(0)
            edge = [CHUNK - 1, 0]
            for h in range(HEADS):
                emptied(dve, f"bT{h}")
                if h:
                    filled(dve, f"ke{h - 1}")
                for d in range(2):
                    b4 = bs[:, d, :].rearrange("p (n t) -> p n t", n=4)
                    nc.vector.tensor_tensor(ke[:, d, :].rearrange("p (n t) -> p n t", n=4),
                                            b4[:, :, edge[d]:edge[d] + 1].to_broadcast([P, 4, CHUNK]), b4,
                                            ALU.subtract).then_inc(bdiff_ready, 1)
                if h:
                    filled(dve, f"o{h - 1}")
                dve.wait_ge(exp_ready, 3 * h + 2)
                for d in range(2):
                    nc.vector.scalar_tensor_tensor(out=qt[:, d, :], in0=qkT[:, 0, h, :], scalar=float(DK) ** -0.5,
                                                   in1=e1[:, d, :], op0=ALU.mult, op1=ALU.mult).then_inc(qk_scaled, 1)
                    nc.vector.tensor_tensor(kt[:, d, :], qkT[:, 1, h, :], kt[:, d, :], ALU.mult).then_inc(qk_scaled, 1)
                dve.wait_ge(exp_ready, 3 * h + 3)
                for d in range(2):
                    nc.vector.tensor_tensor(ke[:, d, :], qkT[:, 1, h, :], ke[:, d, :], ALU.mult).then_inc(ke_ready, 1)
                if h + 1 < HEADS:
                    log_gates(h + 1)
                filled(dve, f"sc{h}")
                for d in range(2):
                    for a in range(TB):
                        o = (d * TB + a) * P
                        last = nc.vector.copy_predicated(scm[:, a, :], gla_mask[d], bank(f"sc{h}")[:, o:o + P])
                    if d == 0:
                        link(last)
                last.then_inc(empty(f"sc{h}"), 1)

                def decay(d, n):
                    t = n * CHUNK + edge[d]
                    return e1[:, d, t:t + 1]

                def update(d, m, n, k, half, last):
                    src = bank(f"U{h}{k}")[:, half * DV:(half + 1) * DV]
                    if m == 0:
                        i = nc.vector.tensor_copy(state[:, d, 0, :], src)
                    else:
                        i = nc.vector.scalar_tensor_tensor(out=state[:, d, m, :], in0=state[:, d, m - 1, :], scalar=decay(d, n),
                                                           in1=src, op0=ALU.mult, op1=ALU.add)
                    i.then_inc(state_ready, 1)
                    return i

                for k in range(4):
                    filled(dve, f"U{h}{k}")
                n_st = 6 * h
                for m, (f_tile, b_tile) in enumerate((((0, 0, 0), (3, 3, 0)), ((1, 1, 0), (2, 2, 0)), ((2, 0, 1), (1, 1, 1)))):
                    if m:
                        dve.wait_ge(state_ready, n_st)
                    update(0, m, f_tile[0], f_tile[1], f_tile[2], False)
                    update(1, m, b_tile[0], b_tile[1], b_tile[2], False)
                    n_st += 2
                for k in range(4):
                    nc.vector.engine_nop().then_inc(empty(f"U{h}{k}"), 1)

            dve.wait_ge(ss_ready, 2)
            nc.vector.reciprocal(rsg, ssg).then_inc(rs_ready, 1)
            dve.wait_ge(rs_ready, 3)
            for a in range(TB):
                for h in range(HEADS):
                    nc.vector.tensor_scalar(vtok[:, a, h * DV:(h + 1) * DV], vtok[:, a, h * DV:(h + 1) * DV],
                                            rsg[:, a * HEADS + h:a * HEADS + h + 1], None, ALU.mult).then_inc(onorm_ready, 1)
            for b in range(DB):
                dve.wait_ge(sig_ready, b + 1)
                nc.vector.tensor_tensor(silu_r[:, b, :], bank(f"r{b}")[:, 0:SEQ], sg[:, b % 4, :], ALU.mult).then_inc(empty(f"r{b}"), 1)
            for n in range(4):
                for k in range(2):
                    emptied(dve, f"r{2 * n + k}")
                filled(dve, f"oT{n}")
                for k in range(2):
                    b = 2 * n + k
                    i = nc.vector.scalar_tensor_tensor(out=oglaT[:, b, :], in0=bank(f"oT{n}")[:, k * SEQ:(k + 1) * SEQ],
                                                       scalar=col(C_GN + b % 2), in1=silu_r[:, b, :],
                                                       op0=ALU.mult, op1=ALU.mult)
                    i.then_inc(ogla_ready, 1)
                nc.vector.engine_nop().then_inc(empty(f"oT{n}"), 1)
            for half in range(2):
                for b in range(4 * half, 4 * half + 4):
                    emptied(dve, f"gg{b}")
                    filled(dve, f"wg{b}")
                    nc.vector.tensor_tensor(mergedT[:, b, :], bank(f"wg{b}")[:, 0:SEQ], sg[:, b % 4, :], ALU.mult).then_inc(empty(f"wg{b}"), 1)
                for b in range(4 * half, 4 * half + 4):
                    emptied(dve, f"gh{b}")
                    filled(dve, f"wh{b}")
                    nc.vector.tensor_tensor(mtmp[:, b % 2, :], bank(f"wh{b}")[:, 0:SEQ], sg[:, b % 4, :], ALU.mult).then_inc(empty(f"wh{b}"), 1)
                    emptied(dve, f"wh{b}")
                    nc.vector.tensor_tensor(mergedT[:, b, :], mergedT[:, b, :], mtmp[:, b % 2, :], ALU.add).then_inc(merged_ready, 1)
            for half in range(2):
                for a in range(TB):
                    n = f"wo{half}{a}"
                    filled(dve, n)
                    xs = x[:, a, half * 512:(half + 1) * 512]
                    nc.vector.tensor_tensor(xs, bank(n)[:, :], xs, ALU.add).then_inc(empty(n), 1)
            dve.wait_ge(ss_ready, 3)
            nc.vector.reciprocal(rs2, ss2).then_inc(rs_ready, 1)
            for n in range(4):
                filled(dve, f"hnT{n}")
                for k in range(2):
                    last = nc.vector.tensor_scalar(hnT[:, 2 * n + k, :], bank(f"hnT{n}")[:, k * SEQ:(k + 1) * SEQ],
                                                   col(C_N2 + 2 * n + k), None, ALU.mult)
                last.then_inc(empty(f"hnT{n}"), 1)
            dve.wait_ge(router_loaded, 16 * 4)
            nc.vector.memset(tmp_area[:, 1824:1984], NEG)
            link(nc.vector.memset(tmp_area[:, 2128:2264], -1.0))
            link(nc.vector.memset(comb[:, :, 0:1], 0.0))
            filled(dve, "rl")
            for a in range(TB):
                last = nc.vector.tensor_tensor(logit[:, a, 0:E], bank("rl")[:, a * E:(a + 1) * E], rb, ALU.add)
            last.then_inc(empty("rl"), 1)
            emptied(dve, "rl")
            for a in range(TB):
                link(nc.vector.max(top8[:, a, :], logit[:, a, 0:E]))
            nc.vector.tensor_scalar(m1n, top8[:, :, 0], -1.0, None, ALU.mult).then_inc(expo_ready, 1)
            dve.wait_ge(expo_ready, 1)
            link(nc.vector.memset(top8[:, :, TOPK:8], NEG))
            for a in range(TB):
                link(nc.vector.match_replace(gone[:, a, :], top8[:, a, :], logit[:, a, :], NEG))
            nc.vector.tensor_tensor(mask, gone[:, :, 0:E], logit[:, :, 0:E], ALU.not_equal).then_inc(mask_ready, 1)
            dve.wait_ge(mask_ready, 1)
            dve.wait_ge(expo_ready, 1 + TB)
            link(nc.vector.tensor_tensor(expo, expo, mask, ALU.mult))
            link(nc.vector.tensor_reduce(den, expo, AX.X, ALU.add))
            link(nc.vector.reciprocal(den, den))
            for a in range(TB):
                last = nc.vector.tensor_scalar(comb[:, a, 1:1 + E], expo[:, a, :], den[:, a:a + 1], None, ALU.mult)
            last.then_inc(comb_ready, 1)
            filled(dve, "rank")
            for a in range(TB):
                link(nc.vector.scalar_tensor_tensor(out=pos[:, a, 0:E], in0=bank("rank")[:, a * E:(a + 1) * E], scalar=1.0,
                                                    in1=mask[:, a, :], op0=ALU.add, op1=ALU.mult))
            nc.vector.engine_nop().then_inc(empty("rank"), 1)
            link(nc.vector.tensor_scalar(pos[:, :, 0:E], pos[:, :, 0:E], -1.0, None, ALU.add))
            filled(dve, "cnt")
            nc.vector.tensor_reduce(cntm, bank("cnt")[:, 0:E], AX.X, ALU.max).then_inc(empty("cnt"), 1)
            emptied(dve, "cnt")
            link(nc.vector.tensor_copy(flag[:, :], cntm[0:1, :]))

            def select(q, e):
                nc.vector.tensor_tensor(sel[:, q % 2, :, :], iota.rearrange("p (o s) -> p o s", o=1).to_broadcast([P, TB, CAP]),
                                        pos[:, :, bass.ds(e, 1)].to_broadcast([P, TB, CAP]), ALU.is_equal).then_inc(sel_ready, 1)

            norm2 = colw[:, C_N2:C_N2 + DB].rearrange("p (b o) -> p b o", o=1).to_broadcast([P, DB, CAP])

            def gathered(q, count):
                dve.wait_ge(gather_psum, count)
                nc.vector.tensor_tensor(xeT[:, q % 2, :, :], banks[2][:, :].rearrange("p (b s) -> p b s", b=DB), norm2,
                                        ALU.mult).then_inc(xe_ready, 1)

            def add_back(e):
                for k in range(4):
                    a, half = k // 2, k % 2
                    dve.wait_ge(scat_psum, 4 * e + k + 1)
                    xs = x[:, a, half * 512:(half + 1) * 512]
                    nc.vector.scalar_tensor_tensor(out=xs, in0=banks[6 + half][:, :], scalar=comb[:, a, bass.ds(e, 1)], in1=xs,
                                                   op0=ALU.mult, op1=ALU.add).then_inc(scat_read, 1)

            select(0, 0)
            select(1, 1)
            for a in range(TB):
                for half in range(2):
                    n = f"bd{a}{half}"
                    filled(dve, n)
                    xs = x[:, a, half * 512:(half + 1) * 512]
                    nc.vector.tensor_tensor(xs, bank(n)[:, :], xs, ALU.add).then_inc(empty(n), 1)
                    emptied(dve, n)
            link(nc.vector.memset(qk_area[:, 1024:1536], 0.0))
            link(nc.vector.memset(selT[:, 3, :], 0.0))
            nc.vector.engine_nop().then_inc(yT_ready, 1)
            nc.vector.engine_nop().then_inc(gu_free, 1)
            for _ in range(2):
                nc.vector.engine_nop().then_inc(scat_read, 1)
            gathered(0, 1)
            with dve.Fori(0, E // UNROLL) as i:
                for q in range(UNROLL):
                    e = i * UNROLL + q
                    dve.wait_ge(chunks_used, e * CH + GU_CH)
                    nc.vector.tensor_tensor(gate, banks[0][:, :].rearrange("p (b s) -> p b s", b=DB),
                                            bias[:, bass.ds(e, 1), 0:DB].rearrange("p o b -> p b o").to_broadcast([P, DB, CAP]),
                                            ALU.add).then_inc(moe_step, 1)
                    nc.vector.tensor_tensor(up, banks[1][:, :].rearrange("p (b s) -> p b s", b=DB),
                                            bias[:, bass.ds(e, 1), DB:2 * DB].rearrange("p o b -> p b o").to_broadcast([P, DB, CAP]),
                                            ALU.add).then_inc(gu_free, 1)
                    dve.wait_ge(moe_step, e + 1)
                    nc.vector.tensor_scalar(gate, gate, LIMIT, None, ALU.min).then_inc(gate_ready, 1)
                    dve.wait_ge(gu_free, e + 2)
                    nc.vector.tensor_scalar(up, up, LIMIT, -LIMIT, ALU.min, ALU.max).then_inc(up_clipped, 1)
                    dve.wait_ge(up_clipped, e + 1)
                    nc.vector.scalar_tensor_tensor(out=up, in0=up, scalar=1.0, in1=gate, op0=ALU.add, op1=ALU.mult).then_inc(up_gated, 1)
                    dve.wait_ge(up_gated, e + 1)
                    dve.wait_ge(sigm_ready, e + 1)
                    nc.vector.tensor_tensor(act, up, sig, ALU.mult).then_inc(act_ready, 1)
                    add_back(e)
                    gathered(q + 1, e + 2)
                    select(q + 2, e + 2)
            add_back(E)
            dve.wait_ge(ss_ready, 4)
            nc.vector.reciprocal(rs3, ss3).then_inc(rs_ready, 1)
            dve.wait_ge(rs_ready, 5)
            for a in range(TB):
                nc.vector.scalar_tensor_tensor(out=x[:, a, :], in0=x[:, a, :], scalar=rs3[:, a:a + 1], in1=normf,
                                               op0=ALU.mult, op1=ALU.mult).then_inc(out_ready, 1)

        @block.gpsimd
        def _(pool):
            pool.wait_ge(cleared, 5)
            for d in range(2):
                pool.dma_start(w2ext[d * RANK:(d + 1) * RANK, d, :], ins["gla_gate_w2"][d]).then_inc(gla_loaded, 16)
                pool.dma_start(w2ext[2 * RANK:2 * RANK + 1, d, :], ins["gla_gate_b"][d:d + 1, :]).then_inc(gla_loaded, 16)


_INS = ["x", "norm1_w", "w_in", "gla_gate_w2", "gla_gate_b", "gla_norm_w", "hy_conv_w", "hy_conv_b", "hy_freq",
        "hy_ffn_w1", "hy_ffn_b1", "hy_ffn_w2", "hy_ffn_b2", "hy_ffn_w3", "hy_decay", "hy_bias", "w_branch_gla",
        "w_branch_hy", "w_out", "norm2_w", "router_w", "router_b", "w_gate_up", "b_gate_up", "w_down", "b_down",
        "norm_f_w"]


def kernel(**inputs):
    import concourse.bacc as bacc
    from concourse.bass_utils import run_bass_kernel_spmd

    nc = bacc.Bacc("TRN2", target_bir_lowering=False, num_devices=1)
    arrays = {n: np.ascontiguousarray(inputs[n]) for n in _INS}
    arrays["shape_table"], arrays["dft_table"], arrays["filter_features"] = shape_tables()
    aps = {n: nc.dram_tensor(f"in_{n}", a.shape, mybir.dt.from_np(a.dtype), kind="ExternalInput").ap()
           for n, a in arrays.items()}
    out = nc.dram_tensor("out_y", (1, SEQ, D), F32, kind="ExternalOutput").ap()
    build(nc, aps, out)
    r = run_bass_kernel_spmd(nc, [{f"in_{n}": a for n, a in arrays.items()}], core_ids=[0])
    return r.results[0]["out_y"]
```

```python
from contextlib import ExitStack

import numpy as np

import concourse.bass as bass
from concourse import mybir

ALU = mybir.AluOpType
ACT = mybir.ActivationFunctionType
AX = mybir.AxisListType
F32 = mybir.dt.float32
I32 = mybir.dt.int32

P = 128
SEQ = 256
D = 1024
TB = SEQ // P
DB = D // P
EPS = 1e-6
HEADS = 4
DK = 128
DV = 256
CHUNK = 64
RANK = 16
BANDS = 16
EMB = 1 + 2 * BANDS
FFN = 64
E = 32
TOPK = 4
LIMIT = 7.0
ALPHA = 1.702
GATE_TEMP = 16.0

Q0 = 0
K0 = Q0 + HEADS * DK
V0 = K0 + HEADS * DK
R0 = V0 + HEADS * DV
A0 = R0 + HEADS * DV
HY0 = A0 + 2 * RANK
GG0 = HY0 + 3 * D
GH0 = GG0 + D

SLOT = 2048
SLOTS = 16
HALF = 512
PAIRS = 4
MOE_SHIFT = 8

CAP = 64
GU_CH = 8
DN_CH = 4
CH = GU_CH + DN_CH
MORE = SEQ // CAP - 1
UNROLL = 4
NEG = -3.0e38

T_ID = 0
T_TRIF = T_ID + P
T_TRIB = T_TRIF + P
T_MASKB = T_TRIB + P
T_UP = T_MASKB + P
T_IOTA = T_UP + P
T_NEGT = T_IOTA + 2 * CAP
T_COLS = T_NEGT + TB

C_N1 = 0
C_N2 = C_N1 + DB
C_CW = C_N2 + DB
C_CB = C_CW + 3 * 3 * DB
C_HB = C_CB + 3 * DB
C_GN = C_HB + DB
C_FR = C_GN + DV // P
C_B1 = C_FR + 1
C_B2 = C_B1 + 1
C_ALL = C_B2 + 1

TWO_PI_HI = 6.28125
TWO_PI_MID = float((np.float32(2 * np.pi - TWO_PI_HI).view(np.uint32) & np.uint32(0xFFFFF000)).view(np.float32))
TWO_PI_LO = 2 * np.pi - TWO_PI_HI - TWO_PI_MID
ROUND = 1.5 * 2.0 ** 23
PI_IN = 3.1415925


def shape_tables():
    t = np.zeros((P, T_COLS), np.float32)
    s = np.arange(P)
    same = (s[:, None] // CHUNK) == (s[None, :] // CHUNK)
    t[:, T_ID:T_ID + P] = np.eye(P)
    t[:, T_TRIF:T_TRIF + P] = (same & (s[:, None] <= s[None, :])) / GATE_TEMP
    t[:, T_TRIB:T_TRIB + P] = (same & (s[:, None] >= s[None, :])) / GATE_TEMP
    t[:, T_MASKB:T_MASKB + P] = same & (s[:, None] > s[None, :])
    t[:, T_UP:T_UP + P] = s[:, None] < s[None, :]
    t[:, T_IOTA:T_IOTA + 2 * CAP] = (np.arange(2 * CAP) % CAP)[None, :]
    lin = np.linspace(0.0, 1.0, SEQ, dtype=np.float32)
    t[:, T_NEGT:T_NEGT + TB] = -lin.reshape(TB, P).T
    w = 2 * np.pi * (np.arange(SEQ) + 0.5) / (2 * SEQ)
    ang = np.arange(SEQ)[:, None] * w[None, :]
    fwd = np.concatenate([np.cos(ang), np.sin(ang)], 1)
    inv = fwd.T / SEQ
    dft = np.concatenate([fwd.reshape(TB, P, 2 * SEQ).transpose(1, 0, 2).reshape(P, -1),
                          inv.reshape(4, P, SEQ).transpose(1, 0, 2).reshape(P, -1)], 1).astype(np.float32)
    omega = (np.float32(2.0 * np.pi) * np.arange(SEQ, dtype=np.float32) / np.float32(SEQ)).astype(np.float32)
    f = np.linspace(1e-4, BANDS - 1, BANDS, dtype=np.float32)
    a = (omega[:, None] * f[None, :]).astype(np.float32).astype(np.float64)
    z = np.concatenate([lin[:, None], np.cos(a), -np.sin(a)], 1).T.astype(np.float32)
    return np.ascontiguousarray(t), np.ascontiguousarray(dft), np.ascontiguousarray(z)


def psum_plan():
    names = ["cols", "f1"] + [f"xT{n}" for n in range(4)] + ["f2"]
    names += [f"hf{tb}{c}" for tb in range(TB) for c in range(4)] + ["ksum"]
    names += [f"K{ri}{kc}{half}" for ri in range(2) for kc in range(2) for half in range(2)]
    names += [f"{n}{b}" for half in range(2) for n in ("hv", "hx") for b in range(4 * half, 4 * half + 4)]
    names += [f"zt{tb}{half}" for half in range(2) for tb in range(TB)]
    names += [f"h0{b}" for b in range(DB)]
    names += [f"Z{kc}{half}{ri}" for kc in range(2) for half in range(2) for ri in range(2)]
    names += [f"y{b}" for b in range(DB)]
    names += [f"q{h}" for h in range(HEADS)] + [f"k{h}" for h in range(HEADS)] + ["al"]
    names += [f"v{half}{tb}" for half in range(2) for tb in range(TB)] + ["lg0"]
    for h in range(HEADS):
        names += [f"bT{h}"] + ([f"lg{h + 1}"] if h + 1 < HEADS else []) + [f"sc{h}", f"ke{h}"]
        names += [f"U{h}{k}" for k in range(4)] + [f"o{h}"]
    names += [f"r{b}" for b in range(DB)]
    names += [f"oT{n}" for n in range(4)]
    for half in range(2):
        for n in ("gg", "wg", "gh", "wh"):
            names += [f"{n}{b}" for b in range(4 * half, 4 * half + 4)]
    names += [f"wo{half}{tb}" for half in range(2) for tb in range(TB)]
    names += [f"hnT{n}" for n in range(4)] + ["rl", "rank", "cnt", "cT"]
    names += [f"bd{tb}{half}" for tb in range(TB) for half in range(2)]
    return {n: (i % 8, i // 8 + 1) for i, n in enumerate(names)}, [(len(names) - b + 7) // 8 for b in range(8)]


FRONT = [("w_in", HY0 + 2 * D), ("w_in", HY0 + D), ("w_in", HY0 + 2 * D + HALF), ("w_in", HY0 + D + HALF),
         ("w_in", HY0), ("w_in", HY0 + HALF), ("w_in", Q0), ("w_in", K0), ("w_in", V0), ("w_in", V0 + HALF),
         ("w_in", R0), ("w_in", R0 + HALF),
         ("w_in", GG0), ("w_branch_gla", 0), ("w_in", GH0), ("w_branch_hy", 0),
         ("w_in", GG0 + HALF), ("w_branch_gla", HALF), ("w_in", GH0 + HALF), ("w_branch_hy", HALF),
         ("w_out", 0), ("w_out", HALF)]
LAST_TILE = ["hv3", "hx3", "hv7", "hx7", "h03", "h07", "q3", "k3", "v01", "v11", "r3", "r7",
             "gg3", "wg3", "gh3", "wh3", "gg7", "wg7", "gh7", "wh7", "wo01", "wo11"]
FIRST_PAIR = -len(FRONT) % PAIRS


def build(nc, ins, out):
    plan, bank_uses = psum_plan()
    with ExitStack() as ctx:
        def sb(name, shape, dt=F32):
            return ctx.enter_context(nc.sbuf_tensor(name, shape, dt))

        def sem(name):
            return ctx.enter_context(nc.semaphore(name))

        ring = sb("ring", [P, SLOTS * SLOT])
        x = sb("x", [P, TB, D])
        xn_area = sb("xn_area", [P, DB * SEQ])
        hy_area = sb("hy_area", [P, DB * SEQ])
        qk_area = sb("qk_area", [P, DB * SEQ])
        v_area = sb("v_area", [P, DB * SEQ])
        gla_area = sb("gla_area", [P, DB * SEQ])
        tmp_area = sb("tmp_area", [P, 5632])
        tab = sb("tab", [P, T_COLS])
        ones = sb("ones", [P, P])
        colw = sb("colw", [P, P])
        vecrows = sb("vecrows", [P, P])
        w_a = sb("w_a", [P, DB, 2 * RANK])
        small = sb("small", [P, 64])
        flag = sb("flag", [1, 1], I32)

        banks = [ctx.enter_context(nc.psum_tensor(f"bank{b}", [P, 512], F32)) for b in range(8)]

        ident = tab[:, T_ID:T_ID + P]
        tri = [tab[:, T_TRIF:T_TRIF + P], tab[:, T_TRIB:T_TRIB + P]]
        gla_mask = [tab[:, T_TRIF:T_TRIF + P].bitcast(I32), tab[:, T_MASKB:T_MASKB + P].bitcast(I32)]
        upper = tab[:, T_UP:T_UP + P]
        iota = tab[:, T_IOTA:T_IOTA + 2 * CAP]

        def col(c, rows=P):
            return colw[0:rows, c:c + 1]

        xnT = xn_area[:, :].rearrange("p (b t) -> p b t", b=DB)
        hnT = xnT
        ohyT = hy_area[:, :].rearrange("p (b t) -> p b t", b=DB)
        oglaT = gla_area[:, :].rearrange("p (b t) -> p b t", b=DB)
        mergedT = qk_area[:, :].rearrange("p (b t) -> p b t", b=DB)
        qkT = qk_area[:, :].rearrange("p (a h t) -> p a h t", a=2, h=HEADS)
        vtok = v_area[:, :].rearrange("p (a n) -> p a n", a=TB)
        xhat = vtok
        hn = vtok

        def hyreg(lo, n):
            return ring[:, 8 * SLOT + lo:8 * SLOT + lo + n]

        Kf = hyreg(0, 4096).rearrange("p (r k c) -> p r k c", r=2, k=2)
        hf = hyreg(4096, 4096).rearrange("p (a n) -> p a n", a=TB)
        Yf = hyreg(4096, 4096).rearrange("p (r k c) -> p r k c", r=2, k=2)
        zreg = hyreg(8192, 2048)
        zT = zreg.rearrange("p (b t) -> p b t", b=DB)
        sumh = zreg.rearrange("p (a n) -> p a n", a=TB)
        ztokreg = hyreg(10240, 2048)
        ztok = ztokreg.rearrange("p (a n) -> p a n", a=TB)
        dec = [zreg, ztokreg]
        dft = hyreg(12288, 1024).rearrange("p (a k) -> p a k", a=TB)
        idft = hyreg(13312, 1024).rearrange("p (a t) -> p a t", a=4)
        w3 = hyreg(14336, 2048)
        absdec = hy_area[:, :]
        sq = [qk_area[:, :], gla_area[:, :]]
        vbuf = gla_area[:, 0:1024].rearrange("p (b t) -> p b t", b=4)
        xbuf = gla_area[:, 1024:2048].rearrange("p (b t) -> p b t", b=4)
        ytmp = v_area[:, :].rearrange("p (q a n) -> p q a n", q=2, a=2)
        zfeat = tmp_area[0:EMB, 0:SEQ]
        w1 = tmp_area[0:EMB, 256:256 + FFN]
        w2 = tmp_area[0:FFN, 320:320 + FFN]
        arg = tmp_area[0:FFN, 384:640]
        turns = tmp_area[0:FFN, 640:896]
        s1 = tmp_area[0:FFN, 896:1152]
        s2 = tmp_area[0:FFN, 1152:1408]
        junk = tmp_area[:, 1920:2944]
        aT = gla_area[0:2 * RANK + 1, 0:SEQ]
        w2ext = gla_area[0:2 * RANK + 1, 256:256 + 2 * HEADS * DK].rearrange("p (a n) -> p a n", a=2)
        glog = tmp_area[:, 0:512].rearrange("p (d a n) -> p d a n", d=2, a=TB)
        bs = tmp_area[:, 512:1024].rearrange("p (d t) -> p d t", d=2)
        e1 = tmp_area[:, 1024:1536].rearrange("p (d t) -> p d t", d=2)
        kt = tmp_area[:, 1536:2048].rearrange("p (d t) -> p d t", d=2)
        ke = tmp_area[:, 2048:2560].rearrange("p (d t) -> p d t", d=2)
        qt = tmp_area[:, 2560:3072].rearrange("p (d t) -> p d t", d=2)
        ketok = tmp_area[:, 3072:3584].rearrange("p (d a n) -> p d a n", d=2, a=TB)
        scm = tmp_area[:, 3584:3840].rearrange("p (a n) -> p a n", a=TB)
        state = tmp_area[:, 3840:5376].rearrange("p (d n e) -> p d n e", d=2, n=3)
        silu_r = qk_area[:, :].rearrange("p (b t) -> p b t", b=DB)
        sg = tmp_area[:, 0:1024].rearrange("p (b t) -> p b t", b=4)
        mtmp = tmp_area[:, 1024:1536].rearrange("p (b t) -> p b t", b=2)
        junk2 = gla_area[:, 0:1024]
        rw = tmp_area[:, 1536:1792].rearrange("p (b e) -> p b e", b=DB)
        rb = tmp_area[:, 1792:1824]
        LW = E + 8
        logit = tmp_area[:, 1824:1824 + TB * LW].rearrange("p (a e) -> p a e", a=TB)
        gone = tmp_area[:, 1904:1904 + TB * LW].rearrange("p (a e) -> p a e", a=TB)
        mask = tmp_area[:, 1984:2048].rearrange("p (a e) -> p a e", a=TB)
        expo = tmp_area[:, 2048:2112].rearrange("p (a e) -> p a e", a=TB)
        top8 = tmp_area[:, 2112:2128].rearrange("p (a e) -> p a e", a=TB)
        PW = E + 2
        pos = tmp_area[:, 2128:2128 + TB * PW].rearrange("p (a e) -> p a e", a=TB)
        comb = tmp_area[:, 2196:2196 + TB * PW].rearrange("p (a e) -> p a e", a=TB)
        combT = tmp_area[0:E, 2264:2264 + SEQ]
        bdown = tmp_area[0:E, 2520:2520 + D]
        normf = tmp_area[:, 3544:3544 + D]
        sel = tmp_area[:, 4568:4568 + 512].rearrange("p (q a s) -> p q a s", q=2, a=TB)
        xe = tmp_area[:, 5080:5080 + 512]
        xeT = hy_area[:, 0:1024].rearrange("p (q c s) -> p q c s", q=2, c=4)
        act = hy_area[:, 1024:1536]
        gate = hy_area[:, 1536:2048]
        sig = qk_area[:, 0:512]
        up = qk_area[:, 512:1024]
        actT = qk_area[:, 1024:1536].rearrange("p (c s) -> p c s", c=4)
        ysb = qk_area[:, 1536:2048]
        selT = gla_area[:, 0:1024].rearrange("p (q t) -> p q t", q=4)
        ebias = gla_area[0:4, 1024:2048].rearrange("p (q n) -> p q n", q=2)
        def small_junk(a):
            return gla_area[:, 1280 + a * DV:1280 + (a + 1) * DV]

        ss1, sd1, rs1 = small[:, 0:2], small[:, 2:4], small[:, 4:6]
        kss, krs = small[:, 6:14], small[:, 14:22]
        ssg, rsg = small[:, 22:30], small[:, 30:38]
        ss2, rs2 = small[:, 38:40], small[:, 40:42]
        m1n, den = small[:, 42:44], small[:, 44:46]
        ss3, rs3 = small[:, 46:48], small[:, 48:50]
        cntm = small[:, 50:51]

        tile_ready = [sem(f"tile_ready{b}") for b in range(8)]
        tile_read = [sem(f"tile_read{b}") for b in range(8)]
        x_loaded = sem("x_loaded")
        tab_loaded = sem("tab_loaded")
        filt_loaded = sem("filt_loaded")
        dft_loaded = sem("dft_loaded")
        vec_loaded = sem("vec_loaded")
        gla_loaded = sem("gla_loaded")
        router_loaded = sem("router_loaded")
        front_loaded = [sem(f"front_loaded{p}") for p in range(PAIRS)]
        cleared = sem("cleared")
        dve_step = sem("dve_step")
        act_step = sem("act_step")
        ss_ready = sem("ss_ready")
        rs_ready = sem("rs_ready")
        xhat_ready = sem("xhat_ready")
        arg_ready = sem("arg_ready")
        sin_ready = sem("sin_ready")
        dec_ready = sem("dec_ready")
        hf_ready = sem("hf_ready")
        sq_ready = sem("sq_ready")
        sd_ready = sem("sd_ready")
        conv_mid = sem("conv_mid")
        z_ready = sem("z_ready")
        x0_ready = sem("x0_ready")
        Y_ready = sem("Y_ready")
        ohy_ready = sem("ohy_ready")
        softplus = sem("softplus")
        glog_ready = sem("glog_ready")
        b_ready = sem("b_ready")
        bdiff_ready = sem("bdiff_ready")
        exp_ready = sem("exp_ready")
        qk_scaled = sem("qk_scaled")
        ke_ready = sem("ke_ready")
        state_ready = sem("state_ready")
        osq_ready = sem("osq_ready")
        onorm_ready = sem("onorm_ready")
        ogla_ready = sem("ogla_ready")
        sig_ready = sem("sig_ready")
        merged_ready = sem("merged_ready")
        hn_ready = sem("hn_ready")
        expo_ready = sem("expo_ready")
        mask_ready = sem("mask_ready")
        comb_ready = sem("comb_ready")
        sel_ready = sem("sel_ready")
        moe_loaded = [sem(f"moe_loaded{s}") for s in range(SLOTS)]
        chunks_used = sem("chunks_used")
        bias_loaded = [sem(f"bias_loaded{b}") for b in range(2)]
        gate_ready = sem("gate_ready")
        up_clipped = sem("up_clipped")
        up_gated = sem("up_gated")
        sigm_ready = sem("sigm_ready")
        act_ready = sem("act_ready")
        actT_psum = sem("actT_psum")
        actT_ready = sem("actT_ready")
        y_ready = sem("y_ready")
        selT_psum = sem("selT_psum")
        selT_ready = sem("selT_ready")
        xe_psum = sem("xe_psum")
        xe_ready = sem("xe_ready")
        xeT_psum = sem("xeT_psum")
        xeT_ready = sem("xeT_ready")
        scat_psum = sem("scat_psum")
        scat_read = sem("scat_read")
        count_ready = sem("count_ready")
        pos_moved = sem("pos_moved")
        more_loaded = sem("more_loaded")
        out_ready = sem("out_ready")
        stored = sem("stored")

        def bank(name):
            return banks[plan[name][0]]

        def filled(eng, name):
            b, g = plan[name]
            eng.wait_ge(tile_ready[b], g)

        def emptied(eng, name):
            b, g = plan[name]
            eng.wait_ge(tile_read[b], g)

        def fill(name):
            return tile_ready[plan[name][0]]

        def empty(name):
            return tile_read[plan[name][0]]

        def front_tile(c):
            p = (c + FIRST_PAIR) % PAIRS
            return ring[:, 2 * p * SLOT:(2 * p + 2) * SLOT].rearrange("p (b n) -> p b n", b=DB)

        def front_arrival(c):
            p = (c + FIRST_PAIR) % PAIRS
            first = (p - FIRST_PAIR) % PAIRS
            return front_loaded[p], 16 * ((c - first) // PAIRS + 1)

        def slot(s):
            return ring[:, s * SLOT:(s + 1) * SLOT]

        wgu, wdn = ins["w_gate_up"], ins["w_down"]

        block = ctx.enter_context(nc.Block())

        @block.sync
        def _(sp):
            sp.dma_start(x[:, :, :], ins["x"][0].rearrange("(a p) d -> p a d", p=P)).then_inc(x_loaded, 16)

            def front(c):
                w, c0 = FRONT[c]
                if c >= PAIRS:
                    filled(sp, LAST_TILE[c - PAIRS])
                src = ins[w][:, c0:c0 + HALF].rearrange("(b p) n -> p b n", p=P)
                sp.dma_start(front_tile(c), src).then_inc(front_arrival(c)[0], 16)

            def load_chunk(e, j, s, done):
                if j < GU_CH:
                    sp.dma_start(slot(s), wgu[e, j * P:(j + 1) * P, :]).then_inc(done, 16)
                else:
                    r = (j - GU_CH) * 2 * P
                    sp.dma_start(slot(s).rearrange("p (c n) -> p c n", c=2),
                                 wdn[e, r:r + 2 * P, :].rearrange("(c p) n -> p c n", p=P)).then_inc(done, 16)

            def load_bias(e, q, done):
                sp.dma_start(ebias[:, q, :], ins["b_gate_up"][e, :].rearrange("(r n) -> r n", r=4)).then_inc(done, 16)

            def moe(n, e, j):
                s = (n + MOE_SHIFT) % SLOTS
                load_chunk(e, j, s, moe_loaded[s])
                if j == 0 and n:
                    load_bias(e, n // CH % 2, bias_loaded[n // CH % 2])

            ahead = 12
            for c in range(ahead):
                front(c)
            sp.wait_ge(ohy_ready, DB)
            for n in range(8):
                moe(n, 0, n)
            for c in range(ahead, len(FRONT)):
                front(c)
            filled(sp, "wh7")
            for a in range(TB):
                emptied(sp, f"wo1{a}")
            load_bias(0, 0, bias_loaded[0])
            for n in range(8, 16):
                filled(sp, LAST_TILE[len(FRONT) - PAIRS + (n - 8) // 2])
                moe(n, n // CH, n % CH)
            with sp.Fori(0, E // UNROLL - 1) as i:
                for m in range(16, 16 + UNROLL * CH):
                    sp.wait_ge(chunks_used, i * (UNROLL * CH) + (m - 15))
                    moe(m, i * UNROLL + m // CH, m % CH)
            for n in range(E * CH - UNROLL * CH + 16, E * CH):
                sp.wait_ge(chunks_used, n - 15)
                moe(n, n // CH, n % CH)
            sp.wait_ge(count_ready, 1)
            longest = sp.value_load(flag[0:1, 0:1], min_val=0, max_val=SEQ)
            with sp.If(longest > CAP):
                with sp.Fori(0, MORE) as r:
                    with sp.Fori(0, E) as e:
                        t = r * E + e
                        sp.wait_ge(chunks_used, t * CH + E * CH)
                        load_bias(e, 0, more_loaded)
                        for j in range(CH):
                            load_chunk(e, j, j, more_loaded)
            sp.wait_ge(out_ready, TB)
            sp.dma_start(out[0].rearrange("(a p) d -> p a d", p=P), x[:, :, :]).then_inc(stored, 16)
            sp.wait_ge(stored, 16)

        @block.tensor
        def _(pe):
            def begin(name):
                b, g = plan[name]
                if g > 1:
                    pe.wait_ge(tile_read[b], g - 1)
                return banks[b]

            def transposes(name, parts):
                t = begin(name)
                for o, i, idn in parts:
                    last = pe.transpose(t[o], i, idn)
                last.then_inc(fill(name), 1)

            def project(name, w, c, rhs):
                t = begin(name)
                for b in range(DB):
                    last = pe.matmul(t[:, 0:SEQ], w[:, b, c:c + P], rhs[:, b, :], start=(b == 0), stop=(b == DB - 1))
                last.then_inc(fill(name), 1)

            def arrive(c):
                s, v = front_arrival(c)
                pe.wait_ge(s, v)

            def four(names, c, rhs):
                arrive(c)
                w = front_tile(c)
                for k, n in enumerate(names):
                    project(n, w, k * P, rhs)

            pe.wait_ge(cleared, 2)
            pe.wait_ge(tab_loaded, 16)
            pe.wait_ge(vec_loaded, 16 * 10)
            transposes("cols", [((slice(None), slice(0, P)), vecrows[:, :], ident)])
            pe.wait_ge(filt_loaded, 16 * 5)
            t = begin("f1")
            pe.matmul(t[0:FFN, 0:SEQ], w1, zfeat, start=True, stop=True).then_inc(fill("f1"), 1)
            pe.wait_ge(xhat_ready, TB)
            for n in range(4):
                transposes(f"xT{n}", [((slice(None), slice((2 * k + a) * P, (2 * k + a + 1) * P)),
                                       xhat[:, a, (2 * n + k) * P:(2 * n + k + 1) * P], ident)
                                      for k in range(2) for a in range(TB)])
            t = begin("f2")
            pe.wait_ge(sin_ready, 1)
            pe.matmul(t[0:FFN, 0:SEQ], w2, s1, start=True, stop=True).then_inc(fill("f2"), 1)
            pe.wait_ge(sin_ready, 2)
            for a in range(TB):
                for c in range(4):
                    t = begin(f"hf{a}{c}")
                    pe.matmul(t[:, :], s2[:, a * P:(a + 1) * P], w3[0:FFN, c * 512:(c + 1) * 512],
                              start=True, stop=True).then_inc(fill(f"hf{a}{c}"), 1)
            t = begin("ksum")
            pe.wait_ge(sq_ready, TB)
            for b in range(DB):
                for k in range(4):
                    last = pe.matmul(t[:, b:b + 1], sq[k // 2][:, (k % 2) * D + b * P:(k % 2) * D + (b + 1) * P],
                                     ones[:, 0:1], start=(k == 0), stop=(k == 3))
            last.then_inc(fill("ksum"), 1)
            pe.wait_ge(sd_ready, 2 * TB)
            pe.wait_ge(dft_loaded, 16)
            for ri in range(2):
                for kc in range(2):
                    for half in range(2):
                        n = f"K{ri}{kc}{half}"
                        t = begin(n)
                        for a in range(TB):
                            src = sumh[:, a, half * 512:(half + 1) * 512] if ri == 0 else \
                                hf[:, a, D + half * 512:D + (half + 1) * 512]
                            last = pe.matmul(t[:, :], dft[:, a, ri * SEQ + kc * P:ri * SEQ + (kc + 1) * P], src,
                                             start=(a == 0), stop=(a == TB - 1))
                        last.then_inc(fill(n), 1)
            for n in range(4):
                emptied(pe, f"xT{n}")
            c = 0
            for half in range(2):
                for nm in ("hv", "hx"):
                    four([f"{nm}{b}" for b in range(4 * half, 4 * half + 4)], c, xnT)
                    c += 1
            for half in range(2):
                pe.wait_ge(z_ready, 4 * (half + 1))
                for a in range(TB):
                    transposes(f"zt{a}{half}", [((slice(None), slice(k * P, (k + 1) * P)),
                                                 zT[:, 4 * half + k, a * P:(a + 1) * P], ident) for k in range(4)])
            for half in range(2):
                four([f"h0{b}" for b in range(4 * half, 4 * half + 4)], 4 + half, xnT)
            for half in range(2):
                for a in range(TB):
                    emptied(pe, f"zt{a}{half}")
            for kc in range(2):
                for half in range(2):
                    for ri in range(2):
                        n = f"Z{kc}{half}{ri}"
                        t = begin(n)
                        for a in range(TB):
                            last = pe.matmul(t[:, :], dft[:, a, ri * SEQ + kc * P:ri * SEQ + (kc + 1) * P],
                                             ztok[:, a, half * 512:(half + 1) * 512], start=(a == 0), stop=(a == TB - 1))
                        last.then_inc(fill(n), 1)
            pe.wait_ge(Y_ready, 4)
            for b in range(DB):
                t = begin(f"y{b}")
                for k in range(4):
                    last = pe.matmul(t[:, 0:SEQ], Yf[:, k // 2, k % 2, b * P:(b + 1) * P], idft[:, k, :],
                                     start=(k == 0), stop=(k == 3))
                last.then_inc(fill(f"y{b}"), 1)
            four([f"q{h}" for h in range(HEADS)], 6, xnT)
            four([f"k{h}" for h in range(HEADS)], 7, xnT)
            t = begin("al")
            for b in range(DB):
                last = pe.matmul(t[0:2 * RANK, 0:SEQ], w_a[:, b, :], xnT[:, b, :], start=(b == 0), stop=(b == DB - 1))
            last.then_inc(fill("al"), 1)
            for half in range(2):
                arrive(8 + half)
                for a in range(TB):
                    t = begin(f"v{half}{a}")
                    for b in range(DB):
                        last = pe.matmul(t[:, :], xnT[:, b, a * P:(a + 1) * P], front_tile(8 + half)[:, b, :],
                                         start=(b == 0), stop=(b == DB - 1))
                    last.then_inc(fill(f"v{half}{a}"), 1)

            def gate_logits(h):
                t = begin(f"lg{h}")
                if h == 0:
                    emptied(pe, "al")
                for d in range(2):
                    for a in range(TB):
                        o = (d * TB + a) * P
                        last = pe.matmul(t[:, o:o + P], aT[:, a * P:(a + 1) * P], w2ext[:, d, h * DK:(h + 1) * DK],
                                         start=True, stop=True)
                last.then_inc(fill(f"lg{h}"), 1)

            pe.wait_ge(cleared, 5)
            pe.wait_ge(gla_loaded, 16 * 4)
            gate_logits(0)
            for half in range(2):
                for a in range(TB):
                    emptied(pe, f"v{half}{a}")
            for h in range(HEADS):
                hv = slice(h * DV, (h + 1) * DV)
                t = begin(f"bT{h}")
                pe.wait_ge(glog_ready, h + 1)
                for d in range(2):
                    for a in range(TB):
                        o = (d * TB + a) * P
                        last = pe.matmul(t[:, o:o + P], glog[:, d, a, :], tri[d], start=True, stop=True)
                last.then_inc(fill(f"bT{h}"), 1)
                if h + 1 < HEADS:
                    gate_logits(h + 1)
                t = begin(f"sc{h}")
                pe.wait_ge(qk_scaled, 4 * (h + 1))
                for d in range(2):
                    for a in range(TB):
                        o = (d * TB + a) * P
                        last = pe.matmul(t[:, o:o + P], kt[:, d, a * P:(a + 1) * P], qt[:, d, a * P:(a + 1) * P],
                                         start=True, stop=True)
                last.then_inc(fill(f"sc{h}"), 1)
                pe.wait_ge(ke_ready, 2 * (h + 1))
                transposes(f"ke{h}", [((slice(None), slice((d * TB + a) * P, (d * TB + a + 1) * P)),
                                       ke[:, d, a * P:(a + 1) * P], ident) for d in range(2) for a in range(TB)])
                emptied(pe, f"ke{h}")
                for k, parts in enumerate((((0, 0), (0, 2)), ((0, 1), (1, 1)), ((1, 2),), ((1, 3),))):
                    t = begin(f"U{h}{k}")
                    for m, (d, n) in enumerate(parts):
                        r = (n % 2) * CHUNK
                        last = pe.matmul(t[:, m * DV:(m + 1) * DV], ketok[r:r + CHUNK, d, n // 2, :],
                                         vtok[r:r + CHUNK, n // 2, hv], start=True, stop=True)
                    last.then_inc(fill(f"U{h}{k}"), 1)
                t = begin(f"o{h}")
                emptied(pe, f"sc{h}")
                pe.wait_ge(state_ready, 6 * (h + 1))
                for a in range(TB):
                    o = a * DV
                    pe.matmul(t[:, o:o + DV], scm[:, a, :], vtok[:, a, hv], start=True, stop=True)
                    for n in (2 * a, 2 * a + 1):
                        r = (n % 2) * CHUNK
                        for d in range(2):
                            m = n - 1 if d == 0 else 2 - n
                            if m >= 0:
                                last = pe.matmul(t[r:r + CHUNK, o:o + DV], qt[:, d, n * CHUNK:(n + 1) * CHUNK],
                                                 state[:, d, m, :], start=False, stop=True, skip_group_check=True)
                last.then_inc(fill(f"o{h}"), 1)
            four([f"r{b}" for b in range(4)], 10, xnT)
            four([f"r{b}" for b in range(4, 8)], 11, xnT)
            pe.wait_ge(onorm_ready, 8)
            for n in range(4):
                transposes(f"oT{n}", [((slice(None), slice((2 * k + a) * P, (2 * k + a + 1) * P)),
                                       vtok[:, a, (2 * n + k) * P:(2 * n + k + 1) * P], ident)
                                      for k in range(2) for a in range(TB)])
            pe.wait_ge(ohy_ready, DB)
            for half in range(2):
                bs4 = range(4 * half, 4 * half + 4)
                four([f"gg{b}" for b in bs4], 12 + 4 * half, xnT)
                pe.wait_ge(ogla_ready, DB)
                four([f"wg{b}" for b in bs4], 13 + 4 * half, oglaT)
                four([f"gh{b}" for b in bs4], 14 + 4 * half, xnT)
                four([f"wh{b}" for b in bs4], 15 + 4 * half, ohyT)
            pe.wait_ge(merged_ready, DB)
            for half in range(2):
                arrive(20 + half)
                for a in range(TB):
                    t = begin(f"wo{half}{a}")
                    for b in range(DB):
                        last = pe.matmul(t[:, :], mergedT[:, b, a * P:(a + 1) * P], front_tile(20 + half)[:, b, :],
                                         start=(b == 0), stop=(b == DB - 1))
                    last.then_inc(fill(f"wo{half}{a}"), 1)
            pe.wait_ge(hn_ready, TB)
            for n in range(4):
                transposes(f"hnT{n}", [((slice(None), slice((2 * k + a) * P, (2 * k + a + 1) * P)),
                                        hn[:, a, (2 * n + k) * P:(2 * n + k + 1) * P], ident)
                                       for k in range(2) for a in range(TB)])
            for n in range(4):
                emptied(pe, f"hnT{n}")
            pe.wait_ge(router_loaded, 16 * 4)
            t = begin("rl")
            for a in range(TB):
                for b in range(DB):
                    last = pe.matmul(t[:, a * E:(a + 1) * E], hnT[:, b, a * P:(a + 1) * P], rw[:, b, :],
                                     start=(b == 0), stop=(b == DB - 1))
            last.then_inc(fill("rl"), 1)
            pe.wait_ge(mask_ready, 1)
            t = begin("rank")
            pe.matmul(t[:, 0:E], upper, mask[:, 0, :], start=True, stop=True)
            pe.matmul(t[:, E:2 * E], ones[:, :], mask[:, 0, :], start=True, stop=False)
            pe.matmul(t[:, E:2 * E], upper, mask[:, 1, :], start=False, stop=True).then_inc(fill("rank"), 1)
            t = begin("cnt")
            pe.matmul(t[:, 0:E], ones[:, :], mask[:, 0, :], start=True, stop=False)
            pe.matmul(t[:, 0:E], ones[:, :], mask[:, 1, :], start=False, stop=True).then_inc(fill("cnt"), 1)
            pe.wait_ge(comb_ready, 1)
            t = begin("cT")
            for a in range(TB):
                last = pe.transpose(t[0:E, a * P:(a + 1) * P], comb[:, a, 1:1 + E], ident)
            last.then_inc(fill("cT"), 1)
            emptied(pe, "cT")
            for a in range(TB):
                for half in range(2):
                    t = begin(f"bd{a}{half}")
                    pe.matmul(t[:, :], combT[:, a * P:(a + 1) * P], bdown[:, half * 512:(half + 1) * 512],
                              start=True, stop=True).then_inc(fill(f"bd{a}{half}"), 1)
            for b in range(8):
                pe.wait_ge(tile_read[b], bank_uses[b])

            def gather(q):
                for a in range(TB):
                    for half in range(2):
                        last = pe.matmul(banks[2][half * CAP:(half + 1) * CAP, :], sel[:, q % 2, a, 0:CAP],
                                         hn[:, a, half * 512:(half + 1) * 512], start=(a == 0), stop=(a == TB - 1))
                last.then_inc(xe_psum, 1)

            def turn_sel(q):
                for a in range(TB):
                    last = pe.transpose(banks[3][:, a * P:(a + 1) * P], sel[:, q % 2, a, :], ident)
                last.then_inc(selT_psum, 1)

            def turn(dst, src, done):
                for c in range(4):
                    last = pe.transpose(dst[:, c * P:(c + 1) * P], src[:, c * P:(c + 1) * P], ident)
                last.then_inc(done, 1)

            def half_of(m, k):
                return m[:, k % 4, (k // 4) * CAP:(k // 4 + 1) * CAP]

            def gate_up(q, where, arrived):
                for bk in range(2):
                    for half in range(2):
                        r = 2 * bk + half
                        pe.matmul(banks[bk][half * CAP:(half + 1) * CAP, :], ident[0:4, r:r + 1].to_broadcast([4, CAP]),
                                  ebias[:, q % 2, :], start=True, stop=False)
                for j in range(GU_CH):
                    arrived(j)
                    for bk in range(2):
                        for half in range(2):
                            c = bk * D + half * 512
                            last = pe.matmul(banks[bk][half * CAP:(half + 1) * CAP, :], half_of(xeT[:, q % 2], j),
                                             slot(where(j))[:, c:c + 512], start=False, stop=(j == GU_CH - 1))
                    last.then_inc(chunks_used, 1)

            def down(where, arrived):
                for j in range(GU_CH, CH):
                    arrived(j)
                    for c in range(2):
                        f = 2 * (j - GU_CH) + c
                        for half in range(2):
                            last = pe.matmul(banks[5][half * CAP:(half + 1) * CAP, :], half_of(actT, f),
                                             slot(where(j))[:, c * D + half * 512:c * D + (half + 1) * 512],
                                             start=(f == 0), stop=(f == DB - 1))
                    last.then_inc(chunks_used, 1)

            def scatter(q, count):
                for k in range(4):
                    a, half = k // 2, k % 2
                    pe.wait_ge(scat_read, count + k + 1)
                    pe.matmul(banks[6 + half][:, :], selT[half * CAP:(half + 1) * CAP, q % 4, a * P:(a + 1) * P],
                              ysb[half * CAP:(half + 1) * CAP, :], start=True, stop=True).then_inc(scat_psum, 1)

            pe.wait_ge(sel_ready, 1)
            gather(0)
            turn_sel(0)
            pe.wait_ge(xe_ready, 1)
            turn(banks[4], xe, xeT_psum)
            pe.wait_ge(selT_ready, 2)
            with pe.Fori(0, E // UNROLL) as i:
                for q in range(UNROLL):
                    e = i * UNROLL + q

                    def where(j):
                        return (q * CH + j + MOE_SHIFT) % SLOTS

                    def arrived(j):
                        pe.wait_ge(moe_loaded[where(j)], (i * 3 + ((q * CH + j) // SLOTS + 1)) * 16)

                    pe.wait_ge(xeT_ready, e + 1)
                    pe.wait_ge(bias_loaded[q % 2], (i * 2 + (q // 2 + 1)) * 16)
                    gate_up(q, where, arrived)
                    pe.wait_ge(sel_ready, e + 2)
                    gather(q + 1)
                    turn_sel(q + 1)
                    pe.wait_ge(selT_ready, e + 1)
                    pe.wait_ge(y_ready, e + 1)
                    scatter(q - 1, e * 4)
                    pe.wait_ge(selT_ready, e + 3)
                    pe.wait_ge(act_ready, e + 1)
                    turn(banks[3], act, actT_psum)
                    pe.wait_ge(xe_ready, e + 2)
                    turn(banks[4], xe, xeT_psum)
                    pe.wait_ge(actT_ready, e + 1)
                    down(where, arrived)
            pe.wait_ge(y_ready, E + 1)
            scatter(UNROLL - 1, E * 4)

            longest = pe.value_load(flag[0:1, 0:1], min_val=0, max_val=SEQ)
            with pe.If(longest > CAP):
                with pe.Fori(0, MORE) as r:
                    with pe.Fori(0, E) as e:
                        t = r * E + e
                        pe.wait_ge(sel_ready, t + (E + 3))
                        gather(0)
                        turn_sel(0)
                        pe.wait_ge(xe_ready, t + (E + 2))
                        turn(banks[4], xe, xeT_psum)
                        pe.wait_ge(more_loaded, t * (16 * (CH + 1)) + 16 * (CH + 1))
                        pe.wait_ge(xeT_ready, t + (E + 2))
                        gate_up(0, lambda j: j, lambda j: None)
                        pe.wait_ge(selT_ready, t + (E + 3))
                        pe.wait_ge(act_ready, t + (E + 1))
                        turn(banks[3], act, actT_psum)
                        pe.wait_ge(actT_ready, t + (E + 1))
                        down(lambda j: j, lambda j: None)
                        pe.wait_ge(y_ready, t + (E + 2))
                        scatter(0, t * 4 + 4 * (E + 1))

        @block.scalar
        def _(sc):
            steps = [0]

            def link(i):
                steps[0] += 1
                i.then_inc(act_step, 1)
                sc.wait_ge(act_step, steps[0])

            sc.dma_start(tab[:, :], ins["shape_table"]).then_inc(tab_loaded, 16)
            sc.wait_ge(cleared, 2)
            rows = [("norm1_w", C_N1), ("norm2_w", C_N2), ("hy_conv_b", C_CB), ("hy_bias", C_HB), ("gla_norm_w", C_GN)]
            for nm, r in rows:
                n = ins[nm].shape[0] // P
                sc.dma_start(vecrows[r:r + n, :], ins[nm].rearrange("(a n) -> a n", n=P)).then_inc(vec_loaded, 16)
            sc.dma_start(vecrows[C_CW:C_CW + 9 * DB, :],
                         ins["hy_conv_w"].rearrange("k (a n) -> (k a) n", n=P)).then_inc(vec_loaded, 16)
            for nm, r in (("hy_freq", C_FR), ("hy_ffn_b1", C_B1), ("hy_ffn_b2", C_B2)):
                sc.dma_start(vecrows[r:r + 1, 0:FFN], ins[nm].rearrange("(a n) -> a n", a=1)).then_inc(vec_loaded, 16)
            sc.dma_start(w_a[:, :, :], ins["w_in"][:, A0:A0 + 2 * RANK].rearrange("(b p) n -> p b n", p=P)).then_inc(vec_loaded, 16)
            sc.dma_start(zfeat, ins["filter_features"]).then_inc(filt_loaded, 16)
            sc.dma_start(w1, ins["hy_ffn_w1"]).then_inc(filt_loaded, 16)
            sc.dma_start(w2, ins["hy_ffn_w2"]).then_inc(filt_loaded, 16)
            sc.dma_start(w3[0:FFN, :], ins["hy_ffn_w3"]).then_inc(filt_loaded, 16)
            sc.dma_start(absdec, ins["hy_decay"].rearrange("(o a) n -> o (a n)", o=1).to_broadcast([P, 2 * D])).then_inc(filt_loaded, 16)
            sc.dma_start(hyreg(12288, 2048), ins["dft_table"]).then_inc(dft_loaded, 16)

            def sumsq(src, scratch, dst):
                return nc.scalar.activation(scratch, src, ACT.Square, accum_out=dst)

            sc.wait_ge(x_loaded, 16)
            link(sumsq(x[:, 0, :], junk, ss1[:, 0:1]))
            link(sumsq(x[:, 1, :], junk, ss1[:, 1:2]))
            sc.wait_ge(cleared, 3)
            nc.scalar.activation(sd1, ss1, ACT.Sqrt, bias=small[:, 63:64], scale=1.0 / D).then_inc(ss_ready, 1)
            sc.wait_ge(rs_ready, 1)
            for a in range(TB):
                nc.scalar.mul(xhat[:, a, :], x[:, a, :], rs1[:, a:a + 1]).then_inc(xhat_ready, 1)
            sc.wait_ge(filt_loaded, 16 * 5)
            link(nc.scalar.activation(absdec, absdec, ACT.Abs))
            for a in range(TB):
                nc.scalar.activation(dec[a], absdec, ACT.Exp, scale=tab[:, T_NEGT + a:T_NEGT + a + 1]).then_inc(dec_ready, 1)
            sc.wait_ge(arg_ready, 1)
            nc.scalar.activation(s1, arg, ACT.Sin).then_inc(sin_ready, 1)
            sc.wait_ge(arg_ready, 2)
            nc.scalar.activation(s2, arg, ACT.Sin).then_inc(sin_ready, 1)
            for a in range(TB):
                sc.wait_ge(hf_ready, 1)
                nc.scalar.activation(sq[a], hf[:, a, :], ACT.Square).then_inc(sq_ready, 1)
            filled(sc, "ksum")
            nc.scalar.activation(kss, bank("ksum")[:, 0:DB], ACT.Sqrt, bias=small[:, 63:64]).then_inc(empty("ksum"), 1)
            for ri in range(2):
                for kc in range(2):
                    for half in range(2):
                        n = f"K{ri}{kc}{half}"
                        filled(sc, n)
                        nc.scalar.copy(Kf[:, ri, kc, half * 512:(half + 1) * 512], bank(n)[:, :]).then_inc(empty(n), 1)

            def conv_centre(name, dst, blk):
                filled(sc, name)
                nc.scalar.activation(dst, bank(name)[:, 0:SEQ], ACT.Identity, bias=col(C_CB + blk),
                                     scale=col(C_CW + 3 * DB + blk)).then_inc(conv_mid, 1)

            emptied(sc, "cols")
            emptied(sc, "ksum")
            for half in range(2):
                for b in range(4 * half, 4 * half + 4):
                    if half:
                        sc.wait_ge(z_ready, b - 3)
                    conv_centre(f"hv{b}", vbuf[:, b % 4, :], 2 * DB + b)
                for b in range(4 * half, 4 * half + 4):
                    conv_centre(f"hx{b}", xbuf[:, b % 4, :], DB + b)
            for half in range(2):
                for a in range(TB):
                    n = f"zt{a}{half}"
                    filled(sc, n)
                    nc.scalar.copy(ztok[:, a, half * 512:(half + 1) * 512], bank(n)[:, :]).then_inc(empty(n), 1)
            for b in range(DB):
                conv_centre(f"h0{b}", ohyT[:, b, :], b)
            for a, nm in enumerate("qk"):
                for h in range(HEADS):
                    filled(sc, f"{nm}{h}")
                    nc.scalar.copy(qkT[:, a, h, :], bank(f"{nm}{h}")[:, 0:SEQ]).then_inc(empty(f"{nm}{h}"), 1)
            filled(sc, "al")
            sc.wait_ge(cleared, 5)
            nc.scalar.copy(aT[0:2 * RANK, :], bank("al")[0:2 * RANK, 0:SEQ]).then_inc(empty("al"), 1)
            sc.wait_ge(Y_ready, 4)
            for half in range(2):
                for a in range(TB):
                    n = f"v{half}{a}"
                    filled(sc, n)
                    nc.scalar.copy(vtok[:, a, half * 512:(half + 1) * 512], bank(n)[:, :]).then_inc(empty(n), 1)

            def softplus_part(h):
                filled(sc, f"lg{h}")
                g2 = tmp_area[:, 0:512]
                if h:
                    filled(sc, f"bT{h - 1}")
                link(nc.scalar.activation(g2, bank(f"lg{h}")[:, :], ACT.Abs))
                link(nc.scalar.activation(g2, g2, ACT.Exp, scale=-1.0))
                nc.scalar.activation(g2, g2, ACT.Ln, bias=small[:, 62:63]).then_inc(softplus, 1)

            softplus_part(0)
            for h in range(HEADS):
                filled(sc, f"bT{h}")
                nc.scalar.copy(tmp_area[:, 512:1024], bank(f"bT{h}")[:, :]).then_inc(empty(f"bT{h}"), 1)
                emptied(sc, f"bT{h}")
                if h:
                    sc.wait_ge(state_ready, 6 * h)
                    filled(sc, f"sc{h - 1}")
                    filled(sc, f"ke{h - 1}")
                nc.scalar.activation(tmp_area[:, 1024:1536], tmp_area[:, 512:1024], ACT.Exp).then_inc(exp_ready, 1)
                nc.scalar.activation(tmp_area[:, 1536:2048], tmp_area[:, 512:1024], ACT.Exp, scale=-1.0).then_inc(exp_ready, 1)
                sc.wait_ge(bdiff_ready, 2 * (h + 1))
                nc.scalar.activation(tmp_area[:, 2048:2560], tmp_area[:, 2048:2560], ACT.Exp).then_inc(exp_ready, 1)
                if h + 1 < HEADS:
                    softplus_part(h + 1)
                filled(sc, f"ke{h}")
                nc.scalar.copy(tmp_area[:, 3072:3584], bank(f"ke{h}")[:, :]).then_inc(empty(f"ke{h}"), 1)
                filled(sc, f"o{h}")
                nc.scalar.copy(vtok[:, :, h * DV:(h + 1) * DV],
                               bank(f"o{h}")[:, :].rearrange("p (a n) -> p a n", a=TB)).then_inc(empty(f"o{h}"), 1)
                emptied(sc, f"o{h}")
                for a in range(TB):
                    last = sumsq(vtok[:, a, h * DV:(h + 1) * DV], small_junk(a), ssg[:, a * HEADS + h:a * HEADS + h + 1])
                last.then_inc(osq_ready, 1)
            sc.wait_ge(osq_ready, HEADS)
            nc.scalar.activation(ssg, ssg, ACT.Sqrt, bias=small[:, 63:64], scale=1.0 / DV).then_inc(ss_ready, 1)

            def sigmoid_of(name, k, count):
                filled(sc, name)
                nc.scalar.activation(sg[:, k, :], bank(name)[:, 0:SEQ], ACT.Sigmoid).then_inc(sig_ready, 1)

            filled(sc, f"o{HEADS - 1}")
            for b in range(DB):
                if b >= 4:
                    emptied(sc, f"r{b - 4}")
                sigmoid_of(f"r{b}", b % 4, b + 1)
            for half in range(2):
                for b in range(4 * half, 4 * half + 4):
                    emptied(sc, f"r{4 + b % 4}" if not half else f"wh{b - 4}")
                    filled(sc, f"gg{b}")
                    nc.scalar.activation(sg[:, b % 4, :], bank(f"gg{b}")[:, 0:SEQ], ACT.Sigmoid).then_inc(empty(f"gg{b}"), 1)
                for b in range(4 * half, 4 * half + 4):
                    emptied(sc, f"wg{b}")
                    filled(sc, f"gh{b}")
                    nc.scalar.activation(sg[:, b % 4, :], bank(f"gh{b}")[:, 0:SEQ], ACT.Sigmoid).then_inc(empty(f"gh{b}"), 1)
            sc.wait_ge(ogla_ready, DB)
            sc.dma_start(rw, ins["router_w"].rearrange("(b p) e -> p b e", p=P)).then_inc(router_loaded, 16)
            sc.dma_start(rb, ins["router_b"].rearrange("(o n) -> o n", o=1).to_broadcast([P, E])).then_inc(router_loaded, 16)
            sc.dma_start(bdown, ins["b_down"]).then_inc(router_loaded, 16)
            sc.dma_start(normf, ins["norm_f_w"].rearrange("(o n) -> o n", o=1).to_broadcast([P, D])).then_inc(router_loaded, 16)
            for b in range(4, 8):
                filled(sc, f"wg{b}")
            for a in range(TB):
                emptied(sc, f"wo1{a}")
                emptied(sc, f"wo0{a}")
                link(sumsq(x[:, a, :], junk2, ss2[:, a:a + 1]))
            nc.scalar.activation(ss2, ss2, ACT.Sqrt, bias=small[:, 63:64], scale=1.0 / D).then_inc(ss_ready, 1)
            sc.wait_ge(rs_ready, 4)
            for a in range(TB):
                nc.scalar.mul(hn[:, a, :], x[:, a, :], rs2[:, a:a + 1]).then_inc(hn_ready, 1)
            sc.wait_ge(expo_ready, 1)
            for a in range(TB):
                nc.scalar.activation(expo[:, a, :], logit[:, a, 0:E], ACT.Exp, bias=m1n[:, a:a + 1]).then_inc(expo_ready, 1)
            filled(sc, "cT")
            nc.scalar.copy(combT, bank("cT")[0:E, 0:SEQ]).then_inc(empty("cT"), 1)

            def copy_xe(count):
                sc.wait_ge(xe_psum, count)
                nc.scalar.copy(xe, banks[2][:, :]).then_inc(xe_ready, 1)

            def copy_selT(q, count):
                sc.wait_ge(selT_psum, count)
                nc.scalar.copy(selT[:, q % 4, :], banks[3][:, 0:SEQ]).then_inc(selT_ready, 1)

            def sigmoid(count):
                sc.wait_ge(gate_ready, count)
                nc.scalar.activation(sig, gate, ACT.Sigmoid, scale=ALPHA).then_inc(sigm_ready, 1)

            def copy_actT(count):
                sc.wait_ge(actT_psum, count)
                nc.scalar.copy(actT.rearrange("p c s -> p (c s)"), banks[3][:, :]).then_inc(actT_ready, 1)

            def copy_y(count):
                sc.wait_ge(chunks_used, count)
                nc.scalar.copy(ysb, banks[5][:, :]).then_inc(y_ready, 1)

            copy_xe(1)
            copy_selT(0, 1)
            with sc.Fori(0, E // UNROLL) as i:
                for q in range(UNROLL):
                    e = i * UNROLL + q
                    sigmoid(e + 1)
                    copy_xe(e + 2)
                    copy_selT(q + 1, e + 2)
                    copy_actT(e + 1)
                    copy_y((e + 1) * CH)
            sc.wait_ge(scat_read, 2 + 4 * (E + 1))
            longest = sc.value_load(flag[0:1, 0:1], min_val=0, max_val=SEQ)
            with sc.If(longest > CAP):
                with sc.Fori(0, MORE) as r:
                    with sc.Fori(0, E) as e:
                        t = r * E + e
                        copy_xe(t + (E + 2))
                        copy_selT(0, t + (E + 2))
                        sigmoid(t + (E + 1))
                        copy_actT(t + (E + 1))
                        copy_y(t * CH + (E + 1) * CH)
                sc.wait_ge(scat_read, 2 + 4 * (E + 1) + 4 * E * MORE)
            for a in range(TB):
                link(sumsq(x[:, a, :], v_area[:, 0:D], ss3[:, a:a + 1]))
            nc.scalar.activation(ss3, ss3, ACT.Sqrt, bias=small[:, 63:64], scale=1.0 / D).then_inc(ss_ready, 1)

        @block.vector
        def _(dve):
            steps = [0]

            def link(i):
                steps[0] += 1
                i.then_inc(dve_step, 1)
                dve.wait_ge(dve_step, steps[0])

            nc.vector.memset(ones[:, :], 1.0).then_inc(cleared, 1)
            nc.vector.memset(vecrows[:, :], 0.0).then_inc(cleared, 1)
            nc.vector.memset(small[:, 63:64], EPS)
            nc.vector.memset(small[:, 62:63], 1.0).then_inc(cleared, 1)
            filled(dve, "cols")
            nc.vector.tensor_copy(colw[:, :], bank("cols")[:, 0:P]).then_inc(empty("cols"), 1)
            emptied(dve, "cols")
            dve.wait_ge(ss_ready, 1)
            nc.vector.reciprocal(rs1, sd1).then_inc(rs_ready, 1)

            def sine_argument(name, bias_col):
                filled(dve, name)
                i = nc.vector.tensor_scalar(arg, bank(name)[0:FFN, 0:SEQ], col(bias_col, FFN), col(C_FR, FFN), ALU.add, ALU.mult)
                i.then_inc(empty(name), 1)
                emptied(dve, name)
                link(nc.vector.tensor_scalar(turns, arg, 1.0 / (2 * np.pi), ROUND, ALU.mult, ALU.add))
                link(nc.vector.tensor_scalar(turns, turns, -ROUND, None, ALU.add))
                for part in (TWO_PI_HI, TWO_PI_MID, TWO_PI_LO):
                    link(nc.vector.scalar_tensor_tensor(out=arg, in0=turns, scalar=-part, in1=arg, op0=ALU.mult, op1=ALU.add))
                nc.vector.tensor_scalar(arg, arg, PI_IN, -PI_IN, ALU.min, ALU.max).then_inc(arg_ready, 1)

            sine_argument("f1", C_B1)
            for n in range(4):
                filled(dve, f"xT{n}")
                for k in range(2):
                    last = nc.vector.tensor_scalar(xnT[:, 2 * n + k, :], bank(f"xT{n}")[:, k * SEQ:(k + 1) * SEQ],
                                                   col(C_N1 + 2 * n + k), None, ALU.mult)
                last.then_inc(empty(f"xT{n}"), 1)
            dve.wait_ge(sin_ready, 1)
            sine_argument("f2", C_B2)
            dve.wait_ge(dec_ready, TB)
            for a in range(TB):
                for c in range(4):
                    n = f"hf{a}{c}"
                    filled(dve, n)
                    nc.vector.tensor_tensor(hf[:, a, c * 512:(c + 1) * 512], bank(n)[:, :], dec[a][:, c * 512:(c + 1) * 512],
                                            ALU.mult).then_inc(empty(n), 1)
            for c in range(2, 4):
                emptied(dve, f"hf0{c}")
            nc.vector.memset(hf[0:1, 0, D:2 * D], 0.0).then_inc(hf_ready, 1)
            dve.wait_ge(hf_ready, 1)
            for a in range(TB):
                nc.vector.tensor_tensor(sumh[:, a, :], hf[:, a, 0:D], hf[:, a, D:2 * D], ALU.add).then_inc(sd_ready, 1)
            dve.wait_ge(sq_ready, TB)
            for a in range(TB):
                nc.vector.tensor_tensor(hf[:, a, D:2 * D], hf[:, a, 0:D], hf[:, a, D:2 * D], ALU.subtract).then_inc(sd_ready, 1)
            emptied(dve, "ksum")
            nc.vector.reciprocal(krs, kss).then_inc(rs_ready, 1)

            mids = [0]

            def conv_sides(name, dst, blk):
                mids[0] += 1
                dve.wait_ge(conv_mid, mids[0])
                link(nc.vector.scalar_tensor_tensor(out=dst[:, 1:SEQ], in0=bank(name)[:, 0:SEQ - 1], scalar=col(C_CW + blk),
                                                    in1=dst[:, 1:SEQ], op0=ALU.mult, op1=ALU.add))
                i = nc.vector.scalar_tensor_tensor(out=dst[:, 0:SEQ - 1], in0=bank(name)[:, 1:SEQ],
                                                   scalar=col(C_CW + 6 * DB + blk), in1=dst[:, 0:SEQ - 1],
                                                   op0=ALU.mult, op1=ALU.add)
                i.then_inc(empty(name), 1)

            for half in range(2):
                for b in range(4 * half, 4 * half + 4):
                    conv_sides(f"hv{b}", vbuf[:, b % 4, :], 2 * DB + b)
                for b in range(4 * half, 4 * half + 4):
                    conv_sides(f"hx{b}", xbuf[:, b % 4, :], DB + b)
                    emptied(dve, f"hv{b}")
                    emptied(dve, f"hx{b}")
                    filled(dve, "K111")
                    nc.vector.tensor_tensor(zT[:, b, :], vbuf[:, b % 4, :], xbuf[:, b % 4, :], ALU.mult).then_inc(z_ready, 1)
            for b in range(DB):
                conv_sides(f"h0{b}", ohyT[:, b, :], b)
            for half in range(2):
                for a in range(TB):
                    filled(dve, f"zt{a}{half}")
            for b in range(DB):
                last = nc.vector.tensor_scalar(zT[:, b, :], zT[:, b, :], col(C_HB + b), None, ALU.mult)
            link(last)
            for ri in range(2):
                for kc in range(2):
                    for half in range(2):
                        emptied(dve, f"K{ri}{kc}{half}")
            for kc in range(2):
                for half in range(2):
                    cs = slice(half * 512, (half + 1) * 512)
                    zr, zi = f"Z{kc}{half}0", f"Z{kc}{half}1"
                    filled(dve, zr)
                    filled(dve, zi)
                    tmp = ytmp[:, half]
                    if kc:
                        dve.wait_ge(Y_ready, half + 1)
                    nc.vector.tensor_tensor(Yf[:, 0, kc, cs], bank(zr)[:, :], Kf[:, 0, kc, cs], ALU.mult)
                    nc.vector.tensor_tensor(tmp[:, 0, :], bank(zi)[:, :], Kf[:, 1, kc, cs], ALU.mult)
                    nc.vector.tensor_tensor(Yf[:, 1, kc, cs], bank(zr)[:, :], Kf[:, 1, kc, cs], ALU.mult).then_inc(empty(zr), 1)
                    nc.vector.tensor_tensor(tmp[:, 1, :], bank(zi)[:, :], Kf[:, 0, kc, cs], ALU.mult).then_inc(empty(zi), 1)
                    emptied(dve, zi)
                    nc.vector.tensor_tensor(Yf[:, 0, kc, cs], Yf[:, 0, kc, cs], tmp[:, 0, :], ALU.subtract)
                    nc.vector.tensor_tensor(Yf[:, 1, kc, cs], Yf[:, 1, kc, cs], tmp[:, 1, :], ALU.add).then_inc(Y_ready, 1)
            dve.wait_ge(rs_ready, 2)
            for b in range(DB):
                filled(dve, f"y{b}")
                nc.vector.scalar_tensor_tensor(out=zT[:, b, :], in0=bank(f"y{b}")[:, 0:SEQ], scalar=krs[:, b:b + 1],
                                               in1=zT[:, b, :], op0=ALU.mult, op1=ALU.add).then_inc(empty(f"y{b}"), 1)
                emptied(dve, f"y{b}")
                nc.vector.tensor_tensor(ohyT[:, b, :], zT[:, b, :], ohyT[:, b, :], ALU.mult).then_inc(ohy_ready, 1)

            dve.wait_ge(z_ready, DB)
            nc.vector.memset(gla_area[0:2 * RANK + 1, 0:1280], 0.0).then_inc(cleared, 1)
            dve.wait_ge(cleared, 4)
            nc.vector.memset(gla_area[2 * RANK:2 * RANK + 1, 0:SEQ], 1.0).then_inc(cleared, 1)
            link(nc.vector.memset(tmp_area[:, 3584:3840], 0.0))

            def log_gates(h):
                dve.wait_ge(softplus, h + 1)
                i = nc.vector.scalar_tensor_tensor(out=tmp_area[:, 0:512], in0=bank(f"lg{h}")[:, :], scalar=0.0,
                                                   in1=tmp_area[:, 0:512], op0=ALU.min, op1=ALU.subtract)
                i.then_inc(empty(f"lg{h}"), 1)
                emptied(dve, f"lg{h}")
                nc.vector.engine_nop().then_inc(glog_ready, 1)

            log_gates(0)
            edge = [CHUNK - 1, 0]
            for h in range(HEADS):
                emptied(dve, f"bT{h}")
                if h:
                    filled(dve, f"ke{h - 1}")
                for d in range(2):
                    b4 = bs[:, d, :].rearrange("p (n t) -> p n t", n=4)
                    nc.vector.tensor_tensor(ke[:, d, :].rearrange("p (n t) -> p n t", n=4),
                                            b4[:, :, edge[d]:edge[d] + 1].to_broadcast([P, 4, CHUNK]), b4,
                                            ALU.subtract).then_inc(bdiff_ready, 1)
                if h:
                    filled(dve, f"o{h - 1}")
                dve.wait_ge(exp_ready, 3 * h + 2)
                for d in range(2):
                    nc.vector.scalar_tensor_tensor(out=qt[:, d, :], in0=qkT[:, 0, h, :], scalar=float(DK) ** -0.5,
                                                   in1=e1[:, d, :], op0=ALU.mult, op1=ALU.mult).then_inc(qk_scaled, 1)
                    nc.vector.tensor_tensor(kt[:, d, :], qkT[:, 1, h, :], kt[:, d, :], ALU.mult).then_inc(qk_scaled, 1)
                dve.wait_ge(exp_ready, 3 * h + 3)
                for d in range(2):
                    nc.vector.tensor_tensor(ke[:, d, :], qkT[:, 1, h, :], ke[:, d, :], ALU.mult).then_inc(ke_ready, 1)
                if h + 1 < HEADS:
                    log_gates(h + 1)
                filled(dve, f"sc{h}")
                for d in range(2):
                    for a in range(TB):
                        o = (d * TB + a) * P
                        last = nc.vector.copy_predicated(scm[:, a, :], gla_mask[d], bank(f"sc{h}")[:, o:o + P])
                    if d == 0:
                        link(last)
                last.then_inc(empty(f"sc{h}"), 1)

                def decay(d, n):
                    t = n * CHUNK + edge[d]
                    return e1[:, d, t:t + 1]

                def update(d, m, n, k, half, last):
                    src = bank(f"U{h}{k}")[:, half * DV:(half + 1) * DV]
                    if m == 0:
                        i = nc.vector.tensor_copy(state[:, d, 0, :], src)
                    else:
                        i = nc.vector.scalar_tensor_tensor(out=state[:, d, m, :], in0=state[:, d, m - 1, :], scalar=decay(d, n),
                                                           in1=src, op0=ALU.mult, op1=ALU.add)
                    i.then_inc(state_ready, 1)
                    return i

                for k in range(4):
                    filled(dve, f"U{h}{k}")
                n_st = 6 * h
                for m, (f_tile, b_tile) in enumerate((((0, 0, 0), (3, 3, 0)), ((1, 1, 0), (2, 2, 0)), ((2, 0, 1), (1, 1, 1)))):
                    if m:
                        dve.wait_ge(state_ready, n_st)
                    update(0, m, f_tile[0], f_tile[1], f_tile[2], False)
                    update(1, m, b_tile[0], b_tile[1], b_tile[2], False)
                    n_st += 2
                for k in range(4):
                    nc.vector.engine_nop().then_inc(empty(f"U{h}{k}"), 1)

            dve.wait_ge(ss_ready, 2)
            nc.vector.reciprocal(rsg, ssg).then_inc(rs_ready, 1)
            dve.wait_ge(rs_ready, 3)
            for a in range(TB):
                for h in range(HEADS):
                    nc.vector.tensor_scalar(vtok[:, a, h * DV:(h + 1) * DV], vtok[:, a, h * DV:(h + 1) * DV],
                                            rsg[:, a * HEADS + h:a * HEADS + h + 1], None, ALU.mult).then_inc(onorm_ready, 1)
            for b in range(DB):
                dve.wait_ge(sig_ready, b + 1)
                nc.vector.tensor_tensor(silu_r[:, b, :], bank(f"r{b}")[:, 0:SEQ], sg[:, b % 4, :], ALU.mult).then_inc(empty(f"r{b}"), 1)
            for n in range(4):
                for k in range(2):
                    emptied(dve, f"r{2 * n + k}")
                filled(dve, f"oT{n}")
                for k in range(2):
                    b = 2 * n + k
                    i = nc.vector.scalar_tensor_tensor(out=oglaT[:, b, :], in0=bank(f"oT{n}")[:, k * SEQ:(k + 1) * SEQ],
                                                       scalar=col(C_GN + b % 2), in1=silu_r[:, b, :],
                                                       op0=ALU.mult, op1=ALU.mult)
                    i.then_inc(ogla_ready, 1)
                nc.vector.engine_nop().then_inc(empty(f"oT{n}"), 1)
            for half in range(2):
                for b in range(4 * half, 4 * half + 4):
                    emptied(dve, f"gg{b}")
                    filled(dve, f"wg{b}")
                    nc.vector.tensor_tensor(mergedT[:, b, :], bank(f"wg{b}")[:, 0:SEQ], sg[:, b % 4, :], ALU.mult).then_inc(empty(f"wg{b}"), 1)
                for b in range(4 * half, 4 * half + 4):
                    emptied(dve, f"gh{b}")
                    filled(dve, f"wh{b}")
                    nc.vector.tensor_tensor(mtmp[:, b % 2, :], bank(f"wh{b}")[:, 0:SEQ], sg[:, b % 4, :], ALU.mult).then_inc(empty(f"wh{b}"), 1)
                    emptied(dve, f"wh{b}")
                    nc.vector.tensor_tensor(mergedT[:, b, :], mergedT[:, b, :], mtmp[:, b % 2, :], ALU.add).then_inc(merged_ready, 1)
            for half in range(2):
                for a in range(TB):
                    n = f"wo{half}{a}"
                    filled(dve, n)
                    xs = x[:, a, half * 512:(half + 1) * 512]
                    nc.vector.tensor_tensor(xs, bank(n)[:, :], xs, ALU.add).then_inc(empty(n), 1)
            dve.wait_ge(ss_ready, 3)
            nc.vector.reciprocal(rs2, ss2).then_inc(rs_ready, 1)
            for n in range(4):
                filled(dve, f"hnT{n}")
                for k in range(2):
                    last = nc.vector.tensor_scalar(hnT[:, 2 * n + k, :], bank(f"hnT{n}")[:, k * SEQ:(k + 1) * SEQ],
                                                   col(C_N2 + 2 * n + k), None, ALU.mult)
                last.then_inc(empty(f"hnT{n}"), 1)
            dve.wait_ge(router_loaded, 16 * 4)
            nc.vector.memset(tmp_area[:, 1824:1984], NEG)
            link(nc.vector.memset(tmp_area[:, 2128:2264], -1.0))
            link(nc.vector.memset(comb[:, :, 0:1], 0.0))
            filled(dve, "rl")
            for a in range(TB):
                last = nc.vector.tensor_tensor(logit[:, a, 0:E], bank("rl")[:, a * E:(a + 1) * E], rb, ALU.add)
            last.then_inc(empty("rl"), 1)
            emptied(dve, "rl")
            for a in range(TB):
                link(nc.vector.max(top8[:, a, :], logit[:, a, 0:E]))
            nc.vector.tensor_scalar(m1n, top8[:, :, 0], -1.0, None, ALU.mult).then_inc(expo_ready, 1)
            dve.wait_ge(expo_ready, 1)
            link(nc.vector.memset(top8[:, :, TOPK:8], NEG))
            for a in range(TB):
                link(nc.vector.match_replace(gone[:, a, :], top8[:, a, :], logit[:, a, :], NEG))
            nc.vector.tensor_tensor(mask, gone[:, :, 0:E], logit[:, :, 0:E], ALU.not_equal).then_inc(mask_ready, 1)
            dve.wait_ge(mask_ready, 1)
            dve.wait_ge(expo_ready, 1 + TB)
            link(nc.vector.tensor_tensor(expo, expo, mask, ALU.mult))
            link(nc.vector.tensor_reduce(den, expo, AX.X, ALU.add))
            link(nc.vector.reciprocal(den, den))
            for a in range(TB):
                last = nc.vector.tensor_scalar(comb[:, a, 1:1 + E], expo[:, a, :], den[:, a:a + 1], None, ALU.mult)
            last.then_inc(comb_ready, 1)
            filled(dve, "rank")
            for a in range(TB):
                link(nc.vector.scalar_tensor_tensor(out=pos[:, a, 0:E], in0=bank("rank")[:, a * E:(a + 1) * E], scalar=1.0,
                                                    in1=mask[:, a, :], op0=ALU.add, op1=ALU.mult))
            nc.vector.engine_nop().then_inc(empty("rank"), 1)
            link(nc.vector.tensor_scalar(pos[:, :, 0:E], pos[:, :, 0:E], -1.0, None, ALU.add))
            filled(dve, "cnt")
            nc.vector.tensor_reduce(cntm, bank("cnt")[:, 0:E], AX.X, ALU.max).then_inc(empty("cnt"), 1)
            emptied(dve, "cnt")
            nc.vector.tensor_copy(flag[:, :], cntm[0:1, :]).then_inc(count_ready, 1)

            def select(q, e):
                nc.vector.tensor_tensor(sel[:, q % 2, :, :], iota.rearrange("p (o s) -> p o s", o=1).to_broadcast([P, TB, 2 * CAP]),
                                        pos[:, :, bass.ds(e, 1)].to_broadcast([P, TB, 2 * CAP]), ALU.is_equal).then_inc(sel_ready, 1)

            norm2 = colw[:, C_N2:C_N2 + DB].rearrange("p (h c o) -> p c h o", h=2, o=1).to_broadcast([P, 4, 2, CAP])

            def scale_xeT(q, count):
                dve.wait_ge(xeT_psum, count)
                nc.vector.tensor_tensor(xeT[:, q % 2].rearrange("p c (h s) -> p c h s", h=2),
                                        banks[4][:, :].rearrange("p (c h s) -> p c h s", c=4, h=2), norm2,
                                        ALU.mult).then_inc(xeT_ready, 1)

            def swiglu(used, count):
                dve.wait_ge(chunks_used, used)
                nc.vector.tensor_scalar(gate, banks[0][:, :], LIMIT, None, ALU.min).then_inc(gate_ready, 1)
                nc.vector.tensor_scalar(up, banks[1][:, :], LIMIT, -LIMIT, ALU.min, ALU.max).then_inc(up_clipped, 1)
                dve.wait_ge(up_clipped, count)
                nc.vector.scalar_tensor_tensor(out=up, in0=up, scalar=1.0, in1=gate, op0=ALU.add, op1=ALU.mult).then_inc(up_gated, 1)
                dve.wait_ge(up_gated, count)
                dve.wait_ge(sigm_ready, count)
                nc.vector.tensor_tensor(act, up, sig, ALU.mult).then_inc(act_ready, 1)

            def add_back(count, column):
                for k in range(4):
                    a, half = k // 2, k % 2
                    dve.wait_ge(scat_psum, count + k + 1)
                    xs = x[:, a, half * 512:(half + 1) * 512]
                    nc.vector.scalar_tensor_tensor(out=xs, in0=banks[6 + half][:, :], scalar=comb[:, a, bass.ds(column, 1)], in1=xs,
                                                   op0=ALU.mult, op1=ALU.add).then_inc(scat_read, 1)

            select(0, 0)
            select(1, 1)
            for a in range(TB):
                for half in range(2):
                    n = f"bd{a}{half}"
                    filled(dve, n)
                    xs = x[:, a, half * 512:(half + 1) * 512]
                    nc.vector.tensor_tensor(xs, bank(n)[:, :], xs, ALU.add).then_inc(empty(n), 1)
                    emptied(dve, n)
            nc.vector.memset(ysb, 0.0).then_inc(y_ready, 1)
            nc.vector.memset(selT[:, 3, :], 0.0).then_inc(selT_ready, 1)
            for _ in range(2):
                nc.vector.engine_nop().then_inc(scat_read, 1)
            scale_xeT(0, 1)
            with dve.Fori(0, E // UNROLL) as i:
                for q in range(UNROLL):
                    e = i * UNROLL + q
                    swiglu(e * CH + GU_CH, e + 1)
                    add_back(e * 4, e)
                    scale_xeT(q + 1, e + 2)
                    select(q + 2, e + 2)
            add_back(E * 4, E)
            longest = dve.value_load(flag[0:1, 0:1], min_val=0, max_val=SEQ)
            with dve.If(longest > CAP):
                with dve.Fori(0, MORE) as r:
                    nc.vector.tensor_scalar(pos[:, :, 0:E], pos[:, :, 0:E], -float(CAP), None, ALU.add).then_inc(pos_moved, 1)
                    with dve.Fori(0, E) as e:
                        t = r * E + e
                        dve.wait_ge(pos_moved, r + 1)
                        select(0, e)
                        scale_xeT(0, t + (E + 2))
                        swiglu(t * CH + (E * CH + GU_CH), t + (E + 1))
                        add_back(t * 4 + 4 * (E + 1), e + 1)
                dve.wait_ge(scat_read, 2 + 4 * (E + 1) + 4 * E * MORE)
            dve.wait_ge(ss_ready, 4)
            nc.vector.reciprocal(rs3, ss3).then_inc(rs_ready, 1)
            dve.wait_ge(rs_ready, 5)
            for a in range(TB):
                nc.vector.scalar_tensor_tensor(out=x[:, a, :], in0=x[:, a, :], scalar=rs3[:, a:a + 1], in1=normf,
                                               op0=ALU.mult, op1=ALU.mult).then_inc(out_ready, 1)

        @block.gpsimd
        def _(pool):
            pool.wait_ge(cleared, 5)
            for d in range(2):
                pool.dma_start(w2ext[d * RANK:(d + 1) * RANK, d, :], ins["gla_gate_w2"][d]).then_inc(gla_loaded, 16)
                pool.dma_start(w2ext[2 * RANK:2 * RANK + 1, d, :], ins["gla_gate_b"][d:d + 1, :]).then_inc(gla_loaded, 16)


_INS = ["x", "norm1_w", "w_in", "gla_gate_w2", "gla_gate_b", "gla_norm_w", "hy_conv_w", "hy_conv_b", "hy_freq",
        "hy_ffn_w1", "hy_ffn_b1", "hy_ffn_w2", "hy_ffn_b2", "hy_ffn_w3", "hy_decay", "hy_bias", "w_branch_gla",
        "w_branch_hy", "w_out", "norm2_w", "router_w", "router_b", "w_gate_up", "b_gate_up", "w_down", "b_down",
        "norm_f_w"]


def kernel(**inputs):
    import concourse.bacc as bacc
    from concourse.bass_utils import run_bass_kernel_spmd

    nc = bacc.Bacc("TRN2", target_bir_lowering=False, num_devices=1)
    arrays = {n: np.ascontiguousarray(inputs[n]) for n in _INS}
    arrays["shape_table"], arrays["dft_table"], arrays["filter_features"] = shape_tables()
    aps = {n: nc.dram_tensor(f"in_{n}", a.shape, mybir.dt.from_np(a.dtype), kind="ExternalInput").ap()
           for n, a in arrays.items()}
    out = nc.dram_tensor("out_y", (1, SEQ, D), F32, kind="ExternalOutput").ap()
    build(nc, aps, out)
    r = run_bass_kernel_spmd(nc, [{f"in_{n}": a for n, a in arrays.items()}], core_ids=[0])
    return r.results[0]["out_y"]
```

```python
from contextlib import ExitStack

import numpy as np

import concourse.bass as bass
from concourse import mybir

ALU = mybir.AluOpType
ACT = mybir.ActivationFunctionType
AX = mybir.AxisListType
F32 = mybir.dt.float32
I32 = mybir.dt.int32
F32R = mybir.dt.float32r

P = 128
SEQ = 256
D = 1024
TB = SEQ // P
DB = D // P
EPS = 1e-6
HEADS = 4
DK = 128
DV = 256
CHUNK = 64
RANK = 16
BANDS = 16
EMB = 1 + 2 * BANDS
FFN = 64
E = 32
TOPK = 4
LIMIT = 7.0
ALPHA = 1.702
GATE_TEMP = 16.0

Q0 = 0
K0 = Q0 + HEADS * DK
V0 = K0 + HEADS * DK
R0 = V0 + HEADS * DV
A0 = R0 + HEADS * DV
HY0 = A0 + 2 * RANK
GG0 = HY0 + 3 * D
GH0 = GG0 + D

SLOT = 2048
SLOTS = 16
HALF = 512
FCOLS = 256
FSLOTS = 4
HI_BUFS = 3
MOE_SHIFT = 8

CAP = 64
GU_CH = 8
DN_CH = 4
CH = GU_CH + DN_CH
MORE = SEQ // CAP - 1
UNROLL = 4
NEG = -3.0e38

T_ID = 0
T_TRIF = T_ID + P
T_TRIB = T_TRIF + P
T_MASKB = T_TRIB + P
T_UP = T_MASKB + P
T_IOTA = T_UP + P
T_NEGT = T_IOTA + 2 * CAP
T_COLS = T_NEGT + TB

C_N1 = 0
C_N2 = C_N1 + DB
C_CW = C_N2 + DB
C_CB = C_CW + 3 * 3 * DB
C_HB = C_CB + 3 * DB
C_GN = C_HB + DB
C_FR = C_GN + DV // P
C_B1 = C_FR + 1
C_B2 = C_B1 + 1
C_ALL = C_B2 + 1

TWO_PI_HI = 6.28125
TWO_PI_MID = float((np.float32(2 * np.pi - TWO_PI_HI).view(np.uint32) & np.uint32(0xFFFFF000)).view(np.float32))
TWO_PI_LO = 2 * np.pi - TWO_PI_HI - TWO_PI_MID
ROUND = 1.5 * 2.0 ** 23
PI_IN = 3.1415925


def shape_tables():
    t = np.zeros((P, T_COLS), np.float32)
    s = np.arange(P)
    same = (s[:, None] // CHUNK) == (s[None, :] // CHUNK)
    t[:, T_ID:T_ID + P] = np.eye(P)
    t[:, T_TRIF:T_TRIF + P] = (same & (s[:, None] <= s[None, :])) / GATE_TEMP
    t[:, T_TRIB:T_TRIB + P] = (same & (s[:, None] >= s[None, :])) / GATE_TEMP
    t[:, T_MASKB:T_MASKB + P] = same & (s[:, None] > s[None, :])
    t[:, T_UP:T_UP + P] = s[:, None] < s[None, :]
    t[:, T_IOTA:T_IOTA + 2 * CAP] = (np.arange(2 * CAP) % CAP)[None, :]
    lin = np.linspace(0.0, 1.0, SEQ, dtype=np.float32)
    t[:, T_NEGT:T_NEGT + TB] = -lin.reshape(TB, P).T
    w = 2 * np.pi * (np.arange(SEQ) + 0.5) / (2 * SEQ)
    ang = np.arange(SEQ)[:, None] * w[None, :]
    fwd = np.concatenate([np.cos(ang), np.sin(ang)], 1)
    inv = fwd.T / SEQ
    dft = np.concatenate([fwd.reshape(TB, P, 2 * SEQ).transpose(1, 0, 2).reshape(P, -1),
                          inv.reshape(4, P, SEQ).transpose(1, 0, 2).reshape(P, -1)], 1).astype(np.float32)
    omega = (np.float32(2.0 * np.pi) * np.arange(SEQ, dtype=np.float32) / np.float32(SEQ)).astype(np.float32)
    f = np.linspace(1e-4, BANDS - 1, BANDS, dtype=np.float32)
    a = (omega[:, None] * f[None, :]).astype(np.float32).astype(np.float64)
    z = np.concatenate([lin[:, None], np.cos(a), -np.sin(a)], 1).T.astype(np.float32)
    return np.ascontiguousarray(t), np.ascontiguousarray(dft), np.ascontiguousarray(z)


FRONT = [("v0", "w_in", V0), ("v1", "w_in", V0 + HALF), ("q", "w_in", Q0), ("k", "w_in", K0),
         ("hv0", "w_in", HY0 + 2 * D), ("hx0", "w_in", HY0 + D),
         ("hv1", "w_in", HY0 + 2 * D + HALF), ("hx1", "w_in", HY0 + D + HALF),
         ("h00", "w_in", HY0), ("h01", "w_in", HY0 + HALF), ("r0", "w_in", R0), ("r1", "w_in", R0 + HALF),
         ("gg0", "w_in", GG0), ("wg0", "w_branch_gla", 0), ("gh0", "w_in", GH0), ("wh0", "w_branch_hy", 0),
         ("gg1", "w_in", GG0 + HALF), ("wg1", "w_branch_gla", HALF), ("gh1", "w_in", GH0 + HALF),
         ("wh1", "w_branch_hy", HALF), ("wo0", "w_out", 0), ("wo1", "w_out", HALF)]
CHUNKS = [(n, w, c0 + sub * FCOLS, sub) for n, w, c0 in FRONT for sub in range(HALF // FCOLS)]
CHUNK_OF = {(n, sub): c for c, (n, _, _, sub) in enumerate(CHUNKS)}


def chunk_of(kind, b):
    return CHUNK_OF[(kind if kind in "qk" else f"{kind}{b // 4}"), b % 4 // 2]


def last_user(c):
    name, _, _, sub = CHUNKS[c]
    if name[:-1] in ("v", "wo"):
        return (name[:-1], int(name[-1]), 1)
    if name in "qk":
        return ("proj", name, 2 * sub + 1)
    return ("proj", name[:-1], 4 * int(name[-1]) + 2 * sub + 1)


def schedule():
    hyena = [("proj", k, 4 * half + b) for half in range(2) for k in ("hv", "hx") for b in range(4)]
    hyena += [("proj", "h0", b) for b in range(DB)]
    st = [("xT", n) for n in range(4)] + [("filter", 1), ("xn_parts",), ("v", 0, 0), ("filter", 2), ("decay",), ("v", 0, 1)]
    st += [("a_low",), ("v", 1, 0), ("gates", 0), ("v", 1, 1)]
    st += [("proj", "q", h) for h in range(HEADS)] + [("taps", 0, c) for c in range(4)]
    st += [("proj", "k", 0), ("proj", "k", 1), ("sums", 0)] + [("taps", 1, c) for c in range(4)]
    st += [("proj", "k", 2), ("proj", "k", 3), ("energy",)]
    for h in range(HEADS):
        if h == 1:
            st += [("ksum",)]
        st += [("scores", h)] + ([("gates", h + 1)] if h + 1 < HEADS else []) + hyena[6 * h:6 * h + 2]
        st += [("updates", h)] + hyena[6 * h + 2:6 * h + 4] + [("output", h)]
        st += ([("sums", h + 1)] if h + 1 < HEADS else []) + hyena[6 * h + 4:6 * h + 6]
    st += [("onorm",)] + [("zt", a, half) for half in range(2) for a in range(TB)]
    st += [("K", ri, kc, half) for ri in range(2) for kc in range(2) for half in range(2)] + [("zbias",)]
    st += [("Z", kc, half) for kc in range(2) for half in range(2)]
    st += [("proj", "r", b) for b in range(DB)] + [("oT", n) for n in range(4)] + [("ogla_parts",)]
    st += [("y", b) for b in range(DB)]
    for half in range(2):
        for k in ("gg", "wg", "gh", "wh"):
            st += [("proj", k, b) for b in range(4 * half, 4 * half + 4)]
            if (k, half) == ("wg", 0):
                st += [("ohy_parts",)]
    st += [("wo", 0, 0), ("wo", 1, 0), ("wo", 0, 1), ("hT", 0, 0), ("hT", 0, 1), ("wo", 1, 1), ("hT", 1, 0), ("hT", 1, 1)]
    blocks = [s for s in st if s[0] == "proj"]
    for j, (_, kind, b) in enumerate(blocks):
        c = chunk_of(kind, b)
        after = [st.index(last_user(c - FSLOTS))] if c >= FSLOTS else [st.index(("xn_parts",))]
        if j >= HI_BUFS:
            after.append(st.index(blocks[j - HI_BUFS]))
        if j:
            after.append(st.index(("parts", *blocks[j - 1][1:])))
        st.insert(max(after) + 1, ("parts", kind, b))
    return st


STAGES = schedule()
BLOCKS = [s[1:] for s in STAGES if s[0] == "parts"]
assert BLOCKS == [s[1:] for s in STAGES if s[0] == "proj"]


def tiles_of(stage):
    kind, *at = stage
    if kind == "proj":
        return [f"{at[0]}{at[1]}"]
    if kind in ("decay", "energy", "onorm", "zbias", "parts", "xn_parts", "ohy_parts", "ogla_parts"):
        return []
    if kind == "scores":
        return [f"sc{at[0]}", f"ke{at[0]}"]
    if kind == "updates":
        return [f"U{at[0]}{k}" for k in range(4)]
    if kind == "Z":
        return [f"Z{at[0]}{at[1]}{ri}" for ri in range(2)]
    return [kind + "".join(map(str, at))]


def psum_plan():
    names = [n for s in STAGES for n in tiles_of(s)] + ["rl", "rank", "cnt"]
    assert len(set(names)) == len(names)
    return {n: (i % 8, i // 8 + 1) for i, n in enumerate(names)}, [(len(names) - b + 7) // 8 for b in range(8)]


def build(nc, ins, out):
    plan, bank_uses = psum_plan()
    with ExitStack() as ctx:
        def sb(name, shape, dt=F32):
            return ctx.enter_context(nc.sbuf_tensor(name, shape, dt))

        def sem(name):
            return ctx.enter_context(nc.semaphore(name))

        areas = {"ring": SLOTS * SLOT, **{n: DB * SEQ for n in ("xn_area", "hy_area", "v_area", "gla_area")}}
        ring_parts = {"front": FSLOTS, "slot4": 1, "slot5": 1, "slot6": 1, "slots7_12": 6, "slot13": 1, "slot14": 1, "slot15": 1}
        parts = {**{n: k * SLOT for n, k in ring_parts.items()}, **{n: k for n, k in areas.items() if n != "ring"}}
        assert sum(ring_parts.values()) == SLOTS
        with ExitStack() as first:
            as_r = {n: first.enter_context(nc.sbuf_tensor(f"{n}_r", [P, size], F32R)) for n, size in parts.items()}
        ring, xn_area, hy_area, v_area, gla_area = (sb(n, [P, size]) for n, size in areas.items())
        qk_area = sb("qk_area", [P, DB * SEQ])
        x = sb("x", [P, TB, D])
        tmp_area = sb("tmp_area", [P, 5632])
        tab = sb("tab", [P, T_COLS])
        ones = sb("ones", [P, P])
        colw = sb("colw", [P, C_ALL])
        w_a = sb("w_a", [P, DB, 2 * RANK])
        small = sb("small", [P, 64])
        flag = sb("flag", [1, 1], I32)

        banks = [ctx.enter_context(nc.psum_tensor(f"bank{b}", [P, 512], F32)) for b in range(8)]

        ident = tab[:, T_ID:T_ID + P]
        tri = [tab[:, T_TRIF:T_TRIF + P], tab[:, T_TRIB:T_TRIB + P]]
        gla_mask = [tab[:, T_TRIF:T_TRIF + P].bitcast(I32), tab[:, T_MASKB:T_MASKB + P].bitcast(I32)]
        upper = tab[:, T_UP:T_UP + P]
        iota = tab[:, T_IOTA:T_IOTA + 2 * CAP]

        def col(c, rows=P):
            return colw[0:rows, c:c + 1]

        xnT = hy_area[:, :].rearrange("p (b t) -> p b t", b=DB)
        hT = xn_area[:, :].rearrange("p (b t) -> p b t", b=DB)
        ohyT = hy_area[:, :].rearrange("p (b t) -> p b t", b=DB)
        oglaT = gla_area[:, :].rearrange("p (b t) -> p b t", b=DB)
        mergedT = qk_area[:, :].rearrange("p (b t) -> p b t", b=DB)
        qkT = qk_area[:, :].rearrange("p (a h t) -> p a h t", a=2, h=HEADS)
        vtok = v_area[:, :].rearrange("p (a n) -> p a n", a=TB)
        xhat = vtok
        hn = vtok

        def hyreg(lo, n):
            return ring[:, 8 * SLOT + lo:8 * SLOT + lo + n]

        Kf = hyreg(0, 4096).rearrange("p (r k c) -> p r k c", r=2, k=2)
        hf = hyreg(4096, 4096).rearrange("p (a n) -> p a n", a=TB)
        Yf = hyreg(4096, 4096).rearrange("p (r k c) -> p r k c", r=2, k=2)
        zreg = hyreg(8192, 2048)
        zT = zreg.rearrange("p (b t) -> p b t", b=DB)
        sumreg = ring[:, 5 * SLOT:6 * SLOT]
        sumh = sumreg.rearrange("p (a n) -> p a n", a=TB)
        gatereg = ring[:, 7 * SLOT:8 * SLOT]
        ztokreg = hyreg(10240, 2048)
        ztok = ztokreg.rearrange("p (a n) -> p a n", a=TB)
        dec = [hyreg(0, 2048), hyreg(2048, 2048)]
        dft = hyreg(12288, 1024).rearrange("p (a k) -> p a k", a=TB)
        idft = hyreg(13312, 1024).rearrange("p (a t) -> p a t", a=4)
        w3 = zreg
        absdec = gla_area[:, :]
        sq = [absdec, ztokreg]
        w_hi = [as_r["slot15"][:, 0:1024], as_r["slot15"][:, 1024:2048], as_r["slot4"][:, 0:1024]]
        w_hi = [m.rearrange("p (b n) -> p b n", b=DB) for m in w_hi]
        parts_of = {"xn": (xnT, as_r["slot6"][:, :], as_r["xn_area"][:, :]),
                    "ohy": (ohyT, as_r["slot13"][:, :], as_r["hy_area"][:, :]),
                    "ogla": (oglaT, as_r["v_area"][:, :], as_r["gla_area"][:, :])}
        parts_of = {k: (v, *(m.rearrange("p (b t) -> p b t", b=DB) for m in ms)) for k, (v, *ms) in parts_of.items()}
        xbuf = ring[:, 4 * SLOT + 1024:5 * SLOT].rearrange("p (b t) -> p b t", b=4)
        ytmp = sumreg.rearrange("p (q a n) -> p q a n", q=2, a=2)
        zfeat = tmp_area[0:EMB, 0:SEQ]
        w1 = tmp_area[0:EMB, 256:256 + FFN]
        w2 = tmp_area[0:FFN, 320:320 + FFN]
        arg = tmp_area[0:FFN, 384:640]
        turns = tmp_area[0:FFN, 640:896]
        s1 = tmp_area[0:FFN, 896:1152]
        s2 = tmp_area[0:FFN, 5376:5632]
        junk = tmp_area[:, 1920:2944]
        aT = gatereg[0:2 * RANK + 1, 0:SEQ]
        w2ext = gatereg[0:2 * RANK + 1, 256:256 + 2 * HEADS * DK].rearrange("p (a n) -> p a n", a=2)
        glog = tmp_area[:, 0:512].rearrange("p (d a n) -> p d a n", d=2, a=TB)
        bs = tmp_area[:, 512:1024].rearrange("p (d t) -> p d t", d=2)
        e1 = tmp_area[:, 1024:1536].rearrange("p (d t) -> p d t", d=2)
        kt = tmp_area[:, 1536:2048].rearrange("p (d t) -> p d t", d=2)
        ke = tmp_area[:, 2048:2560].rearrange("p (d t) -> p d t", d=2)
        qt = tmp_area[:, 2560:3072].rearrange("p (d t) -> p d t", d=2)
        ketok = tmp_area[:, 3072:3584].rearrange("p (d a n) -> p d a n", d=2, a=TB)
        scm = tmp_area[:, 3584:3840].rearrange("p (a n) -> p a n", a=TB)
        state = tmp_area[:, 3840:5376].rearrange("p (d n e) -> p d n e", d=2, n=3)
        silu_r = gla_area[:, :].rearrange("p (b t) -> p b t", b=DB)
        sg = tmp_area[:, 0:1024].rearrange("p (b t) -> p b t", b=4)
        mtmp = tmp_area[:, 1024:1536].rearrange("p (b t) -> p b t", b=2)
        junk2 = gla_area[:, 0:1024]
        rw = tmp_area[:, 1536:1792].rearrange("p (b e) -> p b e", b=DB)
        rb = tmp_area[:, 1792:1824]
        LW = E + 8
        logit = tmp_area[:, 1824:1824 + TB * LW].rearrange("p (a e) -> p a e", a=TB)
        gone = tmp_area[:, 1904:1904 + TB * LW].rearrange("p (a e) -> p a e", a=TB)
        mask = tmp_area[:, 1984:2048].rearrange("p (a e) -> p a e", a=TB)
        expo = tmp_area[:, 2048:2112].rearrange("p (a e) -> p a e", a=TB)
        top8 = tmp_area[:, 2112:2128].rearrange("p (a e) -> p a e", a=TB)
        PW = E + 2
        pos = tmp_area[:, 2128:2128 + TB * PW].rearrange("p (a e) -> p a e", a=TB)
        comb = tmp_area[:, 2196:2196 + TB * PW].rearrange("p (a e) -> p a e", a=TB)
        combx = tmp_area[:, 2264:2264 + SEQ].rearrange("p (a h s) -> p a h s", a=TB, h=2)
        normf = tmp_area[:, 3544:3544 + D]
        sel = tmp_area[:, 4568:4568 + 512].rearrange("p (q a s) -> p q a s", q=2, a=TB)
        xe = tmp_area[:, 5080:5080 + 512]
        xeT = hy_area[:, 0:1024].rearrange("p (q c s) -> p q c s", q=2, c=4)
        act = hy_area[:, 1024:1536]
        gate = hy_area[:, 1536:2048]
        sig = qk_area[:, 0:512]
        up = qk_area[:, 512:1024]
        actT = qk_area[:, 1024:1536].rearrange("p (c s) -> p c s", c=4)
        ysb = qk_area[:, 1536:2048]
        selT = gla_area[:, 0:1024].rearrange("p (q t) -> p q t", q=4)
        ebias = gla_area[0:4, 1024:2048].rearrange("p (q n) -> p q n", q=2)
        def small_junk(a):
            return gatereg[:, 1280 + a * DV:1280 + (a + 1) * DV]

        ss1, sd1, rs1 = small[:, 0:2], small[:, 2:4], small[:, 4:6]
        kss, krs = small[:, 6:14], small[:, 14:22]
        ssg, rsg = small[:, 22:30], small[:, 30:38]
        ss2, rs2 = small[:, 38:40], small[:, 40:42]
        m1n, den = small[:, 42:44], small[:, 44:46]
        ss3, rs3 = small[:, 46:48], small[:, 48:50]
        cntm = small[:, 50:51]

        tile_ready = [sem(f"tile_ready{b}") for b in range(8)]
        tile_read = [sem(f"tile_read{b}") for b in range(8)]
        x_loaded = [sem(f"x_loaded{a}") for a in range(TB)]
        tab_loaded = sem("tab_loaded")
        filt_loaded = sem("filt_loaded")
        dft_loaded = sem("dft_loaded")
        col_loaded = sem("col_loaded")
        gla_loaded = sem("gla_loaded")
        router_loaded = sem("router_loaded")
        front_loaded = [sem(f"front_loaded{p}") for p in range(FSLOTS)]
        w_hi_ready = sem("w_hi_ready")
        w_parts_ready = sem("w_parts_ready")
        act_hi_ready = sem("act_hi_ready")
        act_parts_ready = sem("act_parts_ready")
        cleared = sem("cleared")
        dve_step = sem("dve_step")
        act_step = sem("act_step")
        ss_ready = sem("ss_ready")
        rs_ready = sem("rs_ready")
        xhat_ready = sem("xhat_ready")
        arg_ready = sem("arg_ready")
        sin_ready = sem("sin_ready")
        dec_ready = sem("dec_ready")
        hf_ready = sem("hf_ready")
        sq_ready = sem("sq_ready")
        sq_summed = sem("sq_summed")
        sd_ready = sem("sd_ready")
        conv_mid = sem("conv_mid")
        z_ready = sem("z_ready")
        x0_ready = sem("x0_ready")
        Y_ready = sem("Y_ready")
        ohy_ready = sem("ohy_ready")
        softplus = sem("softplus")
        glog_ready = sem("glog_ready")
        b_ready = sem("b_ready")
        bdiff_ready = sem("bdiff_ready")
        exp_ready = sem("exp_ready")
        qk_scaled = sem("qk_scaled")
        ke_ready = sem("ke_ready")
        state_ready = sem("state_ready")
        osq_ready = sem("osq_ready")
        onorm_ready = sem("onorm_ready")
        ogla_ready = sem("ogla_ready")
        sig_ready = sem("sig_ready")
        merged_ready = sem("merged_ready")
        hn_ready = sem("hn_ready")
        expo_ready = sem("expo_ready")
        mask_ready = sem("mask_ready")
        comb_ready = sem("comb_ready")
        combT_psum = sem("combT_psum")
        bdown_loaded = sem("bdown_loaded")
        sel_ready = sem("sel_ready")
        moe_loaded = [sem(f"moe_loaded{s}") for s in range(SLOTS)]
        chunks_used = sem("chunks_used")
        bias_loaded = [sem(f"bias_loaded{b}") for b in range(2)]
        gate_ready = sem("gate_ready")
        up_clipped = sem("up_clipped")
        up_gated = sem("up_gated")
        sigm_ready = sem("sigm_ready")
        act_ready = sem("act_ready")
        actT_psum = sem("actT_psum")
        actT_ready = sem("actT_ready")
        y_ready = sem("y_ready")
        selT_psum = sem("selT_psum")
        selT_ready = sem("selT_ready")
        xe_psum = sem("xe_psum")
        xe_ready = sem("xe_ready")
        xeT_psum = sem("xeT_psum")
        xeT_ready = sem("xeT_ready")
        scat_psum = sem("scat_psum")
        scat_read = sem("scat_read")
        count_ready = sem("count_ready")
        pos_moved = sem("pos_moved")
        more_loaded = sem("more_loaded")
        out_ready = sem("out_ready")
        stored = sem("stored")

        def bank(name):
            return banks[plan[name][0]]

        def filled(eng, name):
            b, g = plan[name]
            eng.wait_ge(tile_ready[b], g)

        def emptied(eng, name):
            b, g = plan[name]
            eng.wait_ge(tile_read[b], g)

        def fill(name):
            return tile_ready[plan[name][0]]

        def empty(name):
            return tile_read[plan[name][0]]

        def front_tile(c):
            return ring[:, c % FSLOTS * SLOT:(c % FSLOTS + 1) * SLOT].rearrange("p (b n) -> p b n", b=DB)

        def front_arrival(c):
            return front_loaded[c % FSLOTS], 16 * (c // FSLOTS + 1)

        def used_up(eng, c):
            filled(eng, tiles_of(last_user(c))[0])

        def block_of(kind, b, area=ring):
            at = chunk_of(kind, b) % FSLOTS * SLOT
            return area[:, at:at + SLOT].rearrange("p (b n) -> p b n", b=DB)[:, :, b % 2 * P:(b % 2 + 1) * P]

        def slot(s):
            return ring[:, s * SLOT:(s + 1) * SLOT]

        wgu, wdn = ins["w_gate_up"], ins["w_down"]

        block = ctx.enter_context(nc.Block())

        @block.sync
        def _(sp):
            for a in range(TB):
                sp.dma_start(x[:, a, :], ins["x"][0, a * P:(a + 1) * P, :]).then_inc(x_loaded[a], 16)
            sp.dma_start(tab[:, :], ins["shape_table"]).then_inc(tab_loaded, 16)
            sp.dma_start(zfeat, ins["filter_features"]).then_inc(filt_loaded, 16)
            sp.dma_start(w1, ins["hy_ffn_w1"]).then_inc(filt_loaded, 16)
            sp.dma_start(w2, ins["hy_ffn_w2"]).then_inc(filt_loaded, 16)

            sp.wait_ge(cleared, 4)
            for d in range(2):
                sp.dma_start(w2ext[d * RANK:(d + 1) * RANK, d, :], ins["gla_gate_w2"][d]).then_inc(gla_loaded, 16)
                sp.dma_start(w2ext[2 * RANK:2 * RANK + 1, d, :], ins["gla_gate_b"][d:d + 1, :]).then_inc(gla_loaded, 16)

            def front(c):
                _, w, c0, _ = CHUNKS[c]
                if c >= FSLOTS:
                    used_up(sp, c - FSLOTS)
                src = ins[w][:, c0:c0 + FCOLS].rearrange("(b p) n -> p b n", p=P)
                sp.dma_start(front_tile(c), src).then_inc(front_arrival(c)[0], 16)

            def load_chunk(e, j, s, done):
                if j < GU_CH:
                    sp.dma_start(slot(s), wgu[e, j * P:(j + 1) * P, :]).then_inc(done, 16)
                else:
                    r = (j - GU_CH) * 2 * P
                    sp.dma_start(slot(s).rearrange("p (c n) -> p c n", c=2),
                                 wdn[e, r:r + 2 * P, :].rearrange("(c p) n -> p c n", p=P)).then_inc(done, 16)

            def load_bias(e, q, done):
                sp.dma_start(ebias[:, q, :], ins["b_gate_up"][e, :].rearrange("(r n) -> r n", r=4)).then_inc(done, 16)

            def moe(n, e, j):
                s = (n + MOE_SHIFT) % SLOTS
                load_chunk(e, j, s, moe_loaded[s])
                if j == 0 and n >= 16:
                    load_bias(e, n // CH % 2, bias_loaded[n // CH % 2])

            for c in range(FSLOTS):
                front(c)
            sp.dma_start(w_a[:, :, :], ins["w_in"][:, A0:A0 + 2 * RANK].rearrange("(b p) n -> p b n", p=P)).then_inc(dft_loaded, 16)
            sp.dma_start(w3[0:FFN, :], ins["hy_ffn_w3"]).then_inc(dft_loaded, 16)
            sp.dma_start(absdec, ins["hy_decay"].rearrange("(o a) n -> o (a n)", o=1).to_broadcast([P, 2 * D])).then_inc(dft_loaded, 16)
            sp.dma_start(hyreg(12288, 2048), ins["dft_table"]).then_inc(dft_loaded, 16)
            first_late = CHUNK_OF["gh0", 0]
            for c in range(FSLOTS, first_late):
                front(c)
            sp.wait_ge(ohy_ready, DB)
            sp.wait_ge(osq_ready, HEADS)
            early = [0, 1, 2, 3, 4, 6, 13, 15]
            for c in range(first_late, len(CHUNKS)):
                for n in early[:1]:
                    moe(n, n // CH, n % CH)
                early = early[1:]
                front(c)
            filled(sp, "wh7")
            for n in (5, 7, 14, 12):
                moe(n, n // CH, n % CH)
            for n in range(8, 12):
                used_up(sp, len(CHUNKS) - 12 + n)
                moe(n, n // CH, n % CH)
            for a in range(TB):
                emptied(sp, f"wo1{a}")
            load_bias(0, 0, bias_loaded[0])
            load_bias(1, 1, bias_loaded[1])
            for half in range(2):
                sp.dma_start(ysb[half * CAP:half * CAP + E, :], ins["b_down"][:, half * 512:(half + 1) * 512]).then_inc(bdown_loaded, 16)
            with sp.Fori(0, E // UNROLL - 1) as i:
                for m in range(16, 16 + UNROLL * CH):
                    sp.wait_ge(chunks_used, i * (UNROLL * CH) + (m - 15))
                    moe(m, i * UNROLL + m // CH, m % CH)
            for n in range(E * CH - UNROLL * CH + 16, E * CH):
                sp.wait_ge(chunks_used, n - 15)
                moe(n, n // CH, n % CH)
            sp.wait_ge(count_ready, 1)
            longest = sp.value_load(flag[0:1, 0:1], min_val=0, max_val=SEQ)
            with sp.If(longest > CAP):
                with sp.Fori(0, MORE) as r:
                    with sp.Fori(0, E) as e:
                        t = r * E + e
                        sp.wait_ge(chunks_used, t * CH + E * CH)
                        load_bias(e, 0, more_loaded)
                        for j in range(CH):
                            load_chunk(e, j, j, more_loaded)
            for a in range(TB):
                sp.wait_ge(out_ready, a + 1)
                sp.dma_start(out[0, a * P:(a + 1) * P, :], x[:, a, :]).then_inc(stored, 16)
            sp.wait_ge(stored, 16 * TB)

        @block.tensor
        def _(pe):
            def begin(name):
                b, g = plan[name]
                if g > 1:
                    pe.wait_ge(tile_read[b], g - 1)
                return banks[b]

            def transposes(name, parts):
                t = begin(name)
                for o, i, idn in parts:
                    last = pe.transpose(t[o], i, idn)
                last.then_inc(fill(name), 1)

            def arrive(c):
                s, v = front_arrival(c)
                pe.wait_ge(s, v)

            moving = {"wg": "ogla", "wh": "ohy"}
            order = {"xn": 1, "ogla": 2, "ohy": 3}

            def to_feature_major(name, src, n):
                transposes(name, [((slice(None), slice((2 * k + a) * P, (2 * k + a + 1) * P)),
                                   src[:, a, (2 * n + k) * P:(2 * n + k + 1) * P], ident)
                                  for k in range(2) for a in range(TB)])

            def project(kind, b):
                name = f"{kind}{b}"
                j = BLOCKS.index((kind, b))
                what = moving.get(kind, "xn")
                _, a_hi, a_lo = parts_of[what]
                pe.wait_ge(act_parts_ready, order[what])
                pe.wait_ge(w_parts_ready, j + 1)
                t = begin(name)
                hi, lo = w_hi[j % HI_BUFS], block_of(kind, b, as_r["front"])
                for m, (w, act) in enumerate(((hi, a_lo), (lo, a_hi), (hi, a_hi))):
                    for d in range(DB):
                        last = pe.matmul(t[:, 0:SEQ], w[:, d, :], act[:, d, :], start=(m == 0 and d == 0), stop=(m == 2 and d == DB - 1))
                last.then_inc(fill(name), 1)

            def token_major(kind, half, lhs, a):
                name = f"{kind}{half}{a}"
                t = begin(name)
                for sub in range(HALF // FCOLS):
                    c = CHUNK_OF[f"{kind}{half}", sub]
                    arrive(c)
                    for d in range(DB):
                        last = pe.matmul(t[:, sub * FCOLS:(sub + 1) * FCOLS], lhs[:, d, a * P:(a + 1) * P], front_tile(c)[:, d, :],
                                         start=(d == 0), stop=(d == DB - 1))
                last.then_inc(fill(name), 1)

            def spectrum(name, ri, kc, src):
                t = begin(name)
                for a in range(TB):
                    last = pe.matmul(t[:, :], dft[:, a, ri * SEQ + kc * P:ri * SEQ + (kc + 1) * P], src(a),
                                     start=(a == 0), stop=(a == TB - 1))
                last.then_inc(fill(name), 1)

            pe.wait_ge(tab_loaded, 16)
            for stage in STAGES:
                kind, *at = stage
                if kind == "xT":
                    pe.wait_ge(xhat_ready, TB)
                    to_feature_major(f"xT{at[0]}", xhat, at[0])
                elif kind == "filter":
                    n = f"filter{at[0]}"
                    t = begin(n)
                    if at[0] == 1:
                        pe.wait_ge(filt_loaded, 16 * 3)
                        i = pe.matmul(t[0:FFN, 0:SEQ], w1, zfeat, start=True, stop=True)
                    else:
                        pe.wait_ge(sin_ready, 1)
                        i = pe.matmul(t[0:FFN, 0:SEQ], w2, s1, start=True, stop=True)
                    i.then_inc(fill(n), 1)
                elif kind == "proj":
                    project(*at)
                elif kind == "a_low":
                    pe.wait_ge(dft_loaded, 16 * 4)
                    t = begin("a_low")
                    for b in range(DB):
                        last = pe.matmul(t[0:2 * RANK, 0:SEQ], w_a[:, b, :], xnT[:, b, :], start=(b == 0), stop=(b == DB - 1))
                    last.then_inc(fill("a_low"), 1)
                elif kind == "gates":
                    h, = at
                    if h == 0:
                        pe.wait_ge(gla_loaded, 16 * 4)
                        emptied(pe, "a_low")
                    t = begin(f"gates{h}")
                    for d in range(2):
                        for a in range(TB):
                            o = (d * TB + a) * P
                            last = pe.matmul(t[:, o:o + P], aT[:, a * P:(a + 1) * P], w2ext[:, d, h * DK:(h + 1) * DK],
                                             start=True, stop=True)
                    last.then_inc(fill(f"gates{h}"), 1)
                elif kind == "taps":
                    a, c = at
                    pe.wait_ge(sin_ready, 2)
                    n = f"taps{a}{c}"
                    begin(n)
                    pe.matmul(bank(n)[:, :], s2[:, a * P:(a + 1) * P], w3[0:FFN, c * 512:(c + 1) * 512],
                              start=True, stop=True).then_inc(fill(n), 1)
                elif kind == "v":
                    half, a = at
                    for n in range(4):
                        emptied(pe, f"xT{n}")
                    token_major("v", half, xnT, a)
                elif kind == "sums":
                    h, = at
                    t = begin(f"sums{h}")
                    pe.wait_ge(glog_ready, h + 1)
                    for d in range(2):
                        for a in range(TB):
                            o = (d * TB + a) * P
                            last = pe.matmul(t[:, o:o + P], glog[:, d, a, :], tri[d], start=True, stop=True)
                    last.then_inc(fill(f"sums{h}"), 1)
                elif kind == "ksum":
                    t = begin("ksum")
                    pe.wait_ge(sq_summed, 3)
                    pe.wait_ge(cleared, 2)
                    for b in range(DB):
                        last = pe.matmul(t[:, b:b + 1], sq[0][:, b * P:(b + 1) * P], ones[:, 0:1], start=True, stop=True)
                    last.then_inc(fill("ksum"), 1)
                elif kind == "scores":
                    h, = at
                    t = begin(f"sc{h}")
                    pe.wait_ge(qk_scaled, 4 * (h + 1))
                    for d in range(2):
                        for a in range(TB):
                            o = (d * TB + a) * P
                            last = pe.matmul(t[:, o:o + P], kt[:, d, a * P:(a + 1) * P], qt[:, d, a * P:(a + 1) * P],
                                             start=True, stop=True)
                    last.then_inc(fill(f"sc{h}"), 1)
                    pe.wait_ge(ke_ready, 2 * (h + 1))
                    transposes(f"ke{h}", [((slice(None), slice((d * TB + a) * P, (d * TB + a + 1) * P)),
                                           ke[:, d, a * P:(a + 1) * P], ident) for d in range(2) for a in range(TB)])
                elif kind == "updates":
                    h, = at
                    emptied(pe, f"ke{h}")
                    if h == 0:
                        for half in range(2):
                            for a in range(TB):
                                emptied(pe, f"v{half}{a}")
                    for k, parts in enumerate((((0, 0), (0, 2)), ((0, 1), (1, 1)), ((1, 2),), ((1, 3),))):
                        t = begin(f"U{h}{k}")
                        for m, (d, n) in enumerate(parts):
                            r = (n % 2) * CHUNK
                            last = pe.matmul(t[:, m * DV:(m + 1) * DV], ketok[r:r + CHUNK, d, n // 2, :],
                                             vtok[r:r + CHUNK, n // 2, h * DV:(h + 1) * DV], start=True, stop=True)
                        last.then_inc(fill(f"U{h}{k}"), 1)
                elif kind == "output":
                    h, = at
                    t = begin(f"output{h}")
                    emptied(pe, f"sc{h}")
                    pe.wait_ge(state_ready, 6 * (h + 1))
                    for a in range(TB):
                        o = a * DV
                        pe.matmul(t[:, o:o + DV], scm[:, a, :], vtok[:, a, h * DV:(h + 1) * DV], start=True, stop=True)
                        for n in (2 * a, 2 * a + 1):
                            r = (n % 2) * CHUNK
                            for d in range(2):
                                m = n - 1 if d == 0 else 2 - n
                                if m >= 0:
                                    last = pe.matmul(t[r:r + CHUNK, o:o + DV], qt[:, d, n * CHUNK:(n + 1) * CHUNK],
                                                     state[:, d, m, :], start=False, stop=True, skip_group_check=True)
                    last.then_inc(fill(f"output{h}"), 1)
                elif kind == "zt":
                    a, half = at
                    pe.wait_ge(z_ready, 4 * (half + 1))
                    transposes(f"zt{a}{half}", [((slice(None), slice(k * P, (k + 1) * P)),
                                                 zT[:, 4 * half + k, a * P:(a + 1) * P], ident) for k in range(4)])
                elif kind == "K":
                    ri, kc, half = at
                    pe.wait_ge(sd_ready, 2 * TB)
                    spectrum(f"K{ri}{kc}{half}", ri, kc,
                             lambda a: sumh[:, a, half * 512:(half + 1) * 512] if ri == 0 else
                             hf[:, a, D + half * 512:D + (half + 1) * 512])
                elif kind == "Z":
                    kc, half = at
                    if stage == ("Z", 0, 0):
                        for hh in range(2):
                            for a in range(TB):
                                emptied(pe, f"zt{a}{hh}")
                    for ri in range(2):
                        spectrum(f"Z{kc}{half}{ri}", ri, kc, lambda a: ztok[:, a, half * 512:(half + 1) * 512])
                elif kind == "y":
                    b, = at
                    pe.wait_ge(Y_ready, 4)
                    t = begin(f"y{b}")
                    for k in range(4):
                        last = pe.matmul(t[:, 0:SEQ], Yf[:, k // 2, k % 2, b * P:(b + 1) * P], idft[:, k, :],
                                         start=(k == 0), stop=(k == 3))
                    last.then_inc(fill(f"y{b}"), 1)
                elif kind == "oT":
                    pe.wait_ge(onorm_ready, 8)
                    to_feature_major(f"oT{at[0]}", vtok, at[0])
                elif kind == "wo":
                    half, a = at
                    pe.wait_ge(merged_ready, DB)
                    token_major("wo", half, mergedT, a)
                elif kind == "hT":
                    a, n = at
                    emptied(pe, f"wo{n}{a}")
                    transposes(f"hT{a}{n}", [((slice(None), slice(k * P, (k + 1) * P)),
                                              x[:, a, (4 * n + k) * P:(4 * n + k + 1) * P], ident) for k in range(4)])

            for a in range(TB):
                for n in range(2):
                    emptied(pe, f"hT{a}{n}")
            pe.wait_ge(router_loaded, 16 * 3)
            t = begin("rl")
            for a in range(TB):
                for b in range(DB):
                    last = pe.matmul(t[:, a * E:(a + 1) * E], hT[:, b, a * P:(a + 1) * P], rw[:, b, :],
                                     start=(b == 0), stop=(b == DB - 1))
            last.then_inc(fill("rl"), 1)
            pe.wait_ge(mask_ready, 1)
            t = begin("rank")
            pe.matmul(t[:, 0:E], upper, mask[:, 0, :], start=True, stop=True)
            pe.matmul(t[:, E:2 * E], ones[:, :], mask[:, 0, :], start=True, stop=False)
            pe.matmul(t[:, E:2 * E], upper, mask[:, 1, :], start=False, stop=True).then_inc(fill("rank"), 1)
            t = begin("cnt")
            pe.matmul(t[:, 0:E], ones[:, :], mask[:, 0, :], start=True, stop=False)
            pe.matmul(t[:, 0:E], ones[:, :], mask[:, 1, :], start=False, stop=True).then_inc(fill("cnt"), 1)
            for b in range(8):
                pe.wait_ge(tile_read[b], bank_uses[b])

            def gather(q):
                for a in range(TB):
                    for half in range(2):
                        last = pe.matmul(banks[2][half * CAP:(half + 1) * CAP, :], sel[:, q % 2, a, 0:CAP],
                                         hn[:, a, half * 512:(half + 1) * 512], start=(a == 0), stop=(a == TB - 1))
                last.then_inc(xe_psum, 1)

            def turn_sel(q):
                for a in range(TB):
                    last = pe.transpose(banks[3][:, a * P:(a + 1) * P], sel[:, q % 2, a, :], ident)
                last.then_inc(selT_psum, 1)

            def turn(dst, src, done):
                for c in range(4):
                    last = pe.transpose(dst[:, c * P:(c + 1) * P], src[:, c * P:(c + 1) * P], ident)
                last.then_inc(done, 1)

            def half_of(m, k):
                return m[:, k % 4, (k // 4) * CAP:(k // 4 + 1) * CAP]

            def gate_up(q, where, arrived):
                for bk in range(2):
                    for half in range(2):
                        r = 2 * bk + half
                        pe.matmul(banks[bk][half * CAP:(half + 1) * CAP, :], ident[0:4, r:r + 1].to_broadcast([4, CAP]),
                                  ebias[:, q % 2, :], start=True, stop=False)
                for j in range(GU_CH):
                    arrived(j)
                    for bk in range(2):
                        for half in range(2):
                            c = bk * D + half * 512
                            last = pe.matmul(banks[bk][half * CAP:(half + 1) * CAP, :], half_of(xeT[:, q % 2], j),
                                             slot(where(j))[:, c:c + 512], start=False, stop=(j == GU_CH - 1))
                    last.then_inc(chunks_used, 1)

            def down(where, arrived):
                for j in range(GU_CH, CH):
                    arrived(j)
                    for c in range(2):
                        f = 2 * (j - GU_CH) + c
                        for half in range(2):
                            last = pe.matmul(banks[5][half * CAP:(half + 1) * CAP, :], half_of(actT, f),
                                             slot(where(j))[:, c * D + half * 512:c * D + (half + 1) * 512],
                                             start=(f == 0), stop=(f == DB - 1))
                    last.then_inc(chunks_used, 1)

            def scatter(q, count, banks_of=(6, 7, 6, 7)):
                for k in range(4):
                    a, half = k // 2, k % 2
                    if banks_of[k] >= 6:
                        pe.wait_ge(scat_read, count + k + 1)
                    pe.matmul(banks[banks_of[k]][:, :], selT[half * CAP:(half + 1) * CAP, q % 4, a * P:(a + 1) * P],
                              ysb[half * CAP:(half + 1) * CAP, :], start=True, stop=True).then_inc(scat_psum, 1)

            pe.wait_ge(hn_ready, TB)
            pe.wait_ge(sel_ready, 1)
            gather(0)
            turn_sel(0)
            pe.wait_ge(xe_ready, 1)
            turn(banks[4], xe, xeT_psum)
            pe.wait_ge(comb_ready, 1)
            for a in range(TB):
                last = pe.transpose(banks[5][:, a * P:(a + 1) * P], combx[:, a].rearrange("p h s -> p (h s)"), ident)
            last.then_inc(combT_psum, 1)
            pe.wait_ge(selT_ready, 2)
            pe.wait_ge(bdown_loaded, 16 * 2)
            with pe.Fori(0, E // UNROLL) as i:
                for q in range(UNROLL):
                    e = i * UNROLL + q

                    def where(j):
                        return (q * CH + j + MOE_SHIFT) % SLOTS

                    def arrived(j):
                        pe.wait_ge(moe_loaded[where(j)], (i * 3 + ((q * CH + j) // SLOTS + 1)) * 16)

                    pe.wait_ge(xeT_ready, e + 1)
                    pe.wait_ge(bias_loaded[q % 2], (i * 2 + (q // 2 + 1)) * 16)
                    gate_up(q, where, arrived)
                    pe.wait_ge(sel_ready, e + 2)
                    gather(q + 1)
                    turn_sel(q + 1)
                    pe.wait_ge(selT_ready, e + 1)
                    pe.wait_ge(y_ready, e + 1)
                    scatter(q - 1, e * 4)
                    pe.wait_ge(selT_ready, e + 3)
                    pe.wait_ge(act_ready, e + 1)
                    turn(banks[3], act, actT_psum)
                    pe.wait_ge(xe_ready, e + 2)
                    turn(banks[4], xe, xeT_psum)
                    pe.wait_ge(actT_ready, e + 1)
                    down(where, arrived)
            pe.wait_ge(y_ready, E + 1)
            scatter(UNROLL - 1, E * 4, (6, 7, 0, 1))

            longest = pe.value_load(flag[0:1, 0:1], min_val=0, max_val=SEQ)
            with pe.If(longest > CAP):
                with pe.Fori(0, MORE) as r:
                    with pe.Fori(0, E) as e:
                        t = r * E + e
                        pe.wait_ge(sel_ready, t + (E + 3))
                        gather(0)
                        turn_sel(0)
                        pe.wait_ge(xe_ready, t + (E + 2))
                        turn(banks[4], xe, xeT_psum)
                        pe.wait_ge(more_loaded, t * (16 * (CH + 1)) + 16 * (CH + 1))
                        pe.wait_ge(xeT_ready, t + (E + 2))
                        gate_up(0, lambda j: j, lambda j: None)
                        pe.wait_ge(selT_ready, t + (E + 3))
                        pe.wait_ge(act_ready, t + (E + 1))
                        turn(banks[3], act, actT_psum)
                        pe.wait_ge(actT_ready, t + (E + 1))
                        down(lambda j: j, lambda j: None)
                        pe.wait_ge(y_ready, t + (E + 2))
                        scatter(0, t * 4 + 4 * (E + 1))

        @block.scalar
        def _(sc):
            steps = [0]

            def link(i):
                steps[0] += 1
                i.then_inc(act_step, 1)
                sc.wait_ge(act_step, steps[0])

            sc.wait_ge(cleared, 1)
            nc.scalar.activation(small[:, 61:62], small[:, 63:64], ACT.Sqrt)
            sc.dma_start(colw[:, :], ins["vector_columns"]).then_inc(col_loaded, 16)

            def sumsq(src, scratch, dst):
                return nc.scalar.activation(scratch, src, ACT.Square, accum_out=dst)

            for a in range(TB):
                sc.wait_ge(x_loaded[a], 16)
                link(sumsq(x[:, a, :], junk, ss1[:, a:a + 1]))
            sc.wait_ge(cleared, 2)
            nc.scalar.activation(sd1, ss1, ACT.Sqrt, bias=small[:, 63:64], scale=1.0 / D).then_inc(ss_ready, 1)
            sc.wait_ge(rs_ready, 1)
            nc.scalar.mul(xhat[:, 0, :], x[:, 0, :], rs1[:, 0:1]).then_inc(xhat_ready, 1)

            def conv_centre(name, dst, blk):
                filled(sc, name)
                nc.scalar.activation(dst, bank(name)[:, 0:SEQ], ACT.Identity, bias=col(C_CB + blk),
                                     scale=col(C_CW + 3 * DB + blk)).then_inc(conv_mid, 1)

            def sigmoid_tile(name, k, done):
                filled(sc, name)
                nc.scalar.activation(sg[:, k, :], bank(name)[:, 0:SEQ], ACT.Sigmoid).then_inc(done, 1)

            def copy_tile(name, dst, src):
                filled(sc, name)
                nc.scalar.copy(dst, src).then_inc(empty(name), 1)

            for stage in STAGES:
                kind, *at = stage
                if kind == "parts":
                    j = BLOCKS.index(tuple(at))
                    s, v = front_arrival(chunk_of(*at))
                    sc.wait_ge(s, v)
                    if j >= HI_BUFS:
                        kind0, b0 = BLOCKS[j - HI_BUFS]
                        filled(sc, f"{kind0}{b0}")
                    nc.scalar.copy(w_hi[j % HI_BUFS], block_of(*at)).then_inc(w_hi_ready, 1)
                elif kind.endswith("_parts"):
                    what = kind[:-6]
                    if what == "xn":
                        for n in range(4):
                            emptied(sc, f"xT{n}")
                    elif what == "ohy":
                        sc.wait_ge(ohy_ready, DB)
                    else:
                        sc.wait_ge(ogla_ready, DB)
                        filled(sc, "oT3")
                    val, hi, _ = parts_of[what]
                    nc.scalar.copy(hi, val).then_inc(act_hi_ready, 1)
                elif kind == "filter":
                    sc.wait_ge(arg_ready, at[0])
                    nc.scalar.activation([s1, s2][at[0] - 1], arg, ACT.Sin).then_inc(sin_ready, 1)
                elif kind == "decay":
                    sc.wait_ge(dft_loaded, 16 * 4)
                    link(nc.scalar.activation(absdec, absdec, ACT.Abs))
                    for a in range(TB):
                        nc.scalar.activation(dec[a], absdec, ACT.Exp, scale=tab[:, T_NEGT + a:T_NEGT + a + 1]).then_inc(dec_ready, 1)
                elif kind == "energy":
                    sc.wait_ge(dec_ready, TB)
                    sc.wait_ge(hf_ready, 1)
                    for a in range(TB):
                        nc.scalar.activation(sq[a], hf[:, a, :], ACT.Square).then_inc(sq_ready, 1)
                elif kind == "ksum":
                    filled(sc, "ksum")
                    nc.scalar.activation(kss, bank("ksum")[:, 0:DB], ACT.Sqrt, bias=small[:, 63:64]).then_inc(empty("ksum"), 1)
                elif kind == "K":
                    ri, kc, half = at
                    n = f"K{ri}{kc}{half}"
                    copy_tile(n, Kf[:, ri, kc, half * 512:(half + 1) * 512], bank(n)[:, :])
                elif kind == "zt":
                    a, half = at
                    if stage == ("zt", 0, 0):
                        emptied(sc, "ksum")
                    copy_tile(f"zt{a}{half}", ztok[:, a, half * 512:(half + 1) * 512], bank(f"zt{a}{half}")[:, :])
                elif kind == "a_low":
                    sc.wait_ge(cleared, 4)
                    copy_tile("a_low", aT[0:2 * RANK, :], bank("a_low")[0:2 * RANK, 0:SEQ])
                elif kind == "v":
                    half, a = at
                    copy_tile(f"v{half}{a}", vtok[:, a, half * 512:(half + 1) * 512], bank(f"v{half}{a}")[:, :])
                elif kind == "gates":
                    h, = at
                    filled(sc, f"gates{h}")
                    g2 = tmp_area[:, 0:512]
                    if h:
                        filled(sc, f"sums{h - 1}")
                    else:
                        sc.wait_ge(sin_ready, 2)
                    link(nc.scalar.activation(g2, bank(f"gates{h}")[:, :], ACT.Abs))
                    link(nc.scalar.activation(g2, g2, ACT.Exp, scale=-1.0))
                    nc.scalar.activation(g2, g2, ACT.Ln, bias=small[:, 62:63]).then_inc(softplus, 1)
                elif kind == "sums":
                    h, = at
                    copy_tile(f"sums{h}", tmp_area[:, 512:1024], bank(f"sums{h}")[:, :])
                    emptied(sc, f"sums{h}")
                    if h:
                        sc.wait_ge(state_ready, 6 * h)
                        filled(sc, f"ke{h - 1}")
                    nc.scalar.activation(tmp_area[:, 1024:1536], tmp_area[:, 512:1024], ACT.Exp).then_inc(exp_ready, 1)
                    nc.scalar.activation(tmp_area[:, 1536:2048], tmp_area[:, 512:1024], ACT.Exp, scale=-1.0).then_inc(exp_ready, 1)
                    sc.wait_ge(bdiff_ready, 2 * (h + 1))
                    nc.scalar.activation(tmp_area[:, 2048:2560], tmp_area[:, 2048:2560], ACT.Exp).then_inc(exp_ready, 1)
                elif kind == "scores":
                    h, = at
                    copy_tile(f"ke{h}", tmp_area[:, 3072:3584], bank(f"ke{h}")[:, :])
                elif kind == "output":
                    h, = at
                    n = f"output{h}"
                    copy_tile(n, vtok[:, :, h * DV:(h + 1) * DV], bank(n)[:, :].rearrange("p (a n) -> p a n", a=TB))
                    emptied(sc, n)
                    if h:
                        sc.wait_ge(osq_ready, h)
                    for a in range(TB):
                        last = sumsq(vtok[:, a, h * DV:(h + 1) * DV], small_junk(a), ssg[:, a * HEADS + h:a * HEADS + h + 1])
                    last.then_inc(osq_ready, 1)
                elif kind == "onorm":
                    sc.wait_ge(osq_ready, HEADS)
                    nc.scalar.activation(ssg, ssg, ACT.Sqrt, bias=small[:, 63:64], scale=1.0 / DV).then_inc(ss_ready, 1)
                elif kind == "proj":
                    nm, b = at
                    n = f"{nm}{b}"
                    if nm in "qk":
                        copy_tile(n, qkT[:, "qk".index(nm), b, :], bank(n)[:, 0:SEQ])
                    elif nm in ("hv", "hx"):
                        if nm == "hx" and b >= 4:
                            sc.wait_ge(z_ready, b - 3)
                        conv_centre(n, zT[:, b, :] if nm == "hv" else xbuf[:, b % 4, :], (2 if nm == "hv" else 1) * DB + b)
                    elif nm == "h0":
                        conv_centre(n, ohyT[:, b, :], b)
                    elif nm == "r":
                        if b >= 4:
                            emptied(sc, f"r{b - 4}")
                        sigmoid_tile(n, b % 4, sig_ready)
                    elif nm == "gg":
                        emptied(sc, f"r{4 + b}" if b < 4 else f"wh{b - 4}")
                        sigmoid_tile(n, b % 4, empty(n))
                    elif nm == "gh":
                        emptied(sc, f"wg{b}")
                        sigmoid_tile(n, b % 4, empty(n))
            sc.wait_ge(ogla_ready, DB)
            sc.dma_start(rw, ins["router_w"].rearrange("(b p) e -> p b e", p=P)).then_inc(router_loaded, 16)
            sc.dma_start(rb, ins["router_b"].rearrange("(o n) -> o n", o=1).to_broadcast([P, E])).then_inc(router_loaded, 16)
            sc.dma_start(normf, ins["norm_f_w"].rearrange("(o n) -> o n", o=1).to_broadcast([P, D])).then_inc(router_loaded, 16)
            for b in range(4, 8):
                filled(sc, f"wg{b}")
            for a in range(TB):
                if a:
                    for half in range(2):
                        emptied(sc, f"wo{half}{a}")
                    sc.wait_ge(act_step, steps[0])
                else:
                    nc.scalar.activation(small[:, 61:62], small[:, 63:64], ACT.Sqrt)
                    for half in range(2):
                        emptied(sc, f"wo{half}{a}")
                link(sumsq(x[:, a, :], junk2, ss2[:, a:a + 1]))
                nc.scalar.activation(ss2[:, a:a + 1], ss2[:, a:a + 1], ACT.Sqrt, bias=small[:, 63:64], scale=1.0 / D).then_inc(ss_ready, 1)
                sc.wait_ge(rs_ready, 4 + a)
                nc.scalar.mul(hn[:, a, :], x[:, a, :], rs2[:, a:a + 1]).then_inc(hn_ready, 1)
            sc.wait_ge(expo_ready, 1)
            for a in range(TB):
                nc.scalar.activation(expo[:, a, :], logit[:, a, 0:E], ACT.Exp, bias=m1n[:, a:a + 1]).then_inc(expo_ready, 1)

            def copy_xe(count):
                sc.wait_ge(xe_psum, count)
                nc.scalar.copy(xe, banks[2][:, :]).then_inc(xe_ready, 1)

            def copy_selT(q, count):
                sc.wait_ge(selT_psum, count)
                nc.scalar.copy(selT[:, q % 4, :], banks[3][:, 0:SEQ]).then_inc(selT_ready, 1)

            def sigmoid(count):
                sc.wait_ge(gate_ready, count)
                nc.scalar.activation(sig, gate, ACT.Sigmoid, scale=ALPHA).then_inc(sigm_ready, 1)

            def copy_actT(count):
                sc.wait_ge(actT_psum, count)
                nc.scalar.copy(actT.rearrange("p c s -> p (c s)"), banks[3][:, :]).then_inc(actT_ready, 1)

            def copy_y(count):
                sc.wait_ge(chunks_used, count)
                nc.scalar.copy(ysb, banks[5][:, :]).then_inc(y_ready, 1)

            copy_xe(1)
            copy_selT(0, 1)
            sc.wait_ge(combT_psum, 1)
            nc.scalar.copy(selT[:, 3, :], banks[5][:, 0:SEQ]).then_inc(selT_ready, 1)
            with sc.Fori(0, E // UNROLL) as i:
                for q in range(UNROLL):
                    e = i * UNROLL + q
                    sigmoid(e + 1)
                    copy_xe(e + 2)
                    copy_selT(q + 1, e + 2)
                    copy_actT(e + 1)
                    copy_y((e + 1) * CH)
            longest = sc.value_load(flag[0:1, 0:1], min_val=0, max_val=SEQ)
            with sc.If(longest > CAP):
                with sc.Fori(0, MORE) as r:
                    with sc.Fori(0, E) as e:
                        t = r * E + e
                        copy_xe(t + (E + 2))
                        copy_selT(0, t + (E + 2))
                        sigmoid(t + (E + 1))
                        copy_actT(t + (E + 1))
                        copy_y(t * CH + (E + 1) * CH)
                sc.wait_ge(scat_read, 2 + 4 * (E + 1) + 4 * E * MORE)
            nc.scalar.activation(small[:, 61:62], small[:, 63:64], ACT.Sqrt)
            for a in range(TB):
                sc.wait_ge(scat_read, 2 + 4 * E + 2 * (a + 1))
                link(sumsq(x[:, a, :], v_area[:, a * D:(a + 1) * D], ss3[:, a:a + 1]))
                nc.scalar.activation(ss3[:, a:a + 1], ss3[:, a:a + 1], ACT.Sqrt, bias=small[:, 63:64], scale=1.0 / D).then_inc(ss_ready, 1)

        @block.vector
        def _(dve):
            steps = [0]

            def link(i):
                steps[0] += 1
                i.then_inc(dve_step, 1)
                dve.wait_ge(dve_step, steps[0])

            nc.vector.memset(small[:, 63:64], EPS).then_inc(cleared, 1)
            nc.vector.memset(small[:, 62:63], 1.0)
            nc.vector.memset(ones[:, :], 1.0).then_inc(cleared, 1)
            nc.vector.memset(gatereg[0:2 * RANK + 1, 0:1280], 0.0).then_inc(cleared, 1)
            dve.wait_ge(cleared, 3)
            nc.vector.memset(gatereg[2 * RANK:2 * RANK + 1, 0:SEQ], 1.0).then_inc(cleared, 1)
            nc.vector.memset(tmp_area[:, 3584:3840], 0.0).then_inc(cleared, 1)
            dve.wait_ge(ss_ready, 1)
            nc.vector.reciprocal(rs1, sd1).then_inc(rs_ready, 1)
            dve.wait_ge(rs_ready, 1)
            nc.vector.tensor_scalar(xhat[:, 1, :], x[:, 1, :], rs1[:, 1:2], None, ALU.mult).then_inc(xhat_ready, 1)
            dve.wait_ge(col_loaded, 16)
            mids = [0]

            def conv_sides(name, dst, blk):
                mids[0] += 1
                dve.wait_ge(conv_mid, mids[0])
                link(nc.vector.scalar_tensor_tensor(out=dst[:, 1:SEQ], in0=bank(name)[:, 0:SEQ - 1], scalar=col(C_CW + blk),
                                                    in1=dst[:, 1:SEQ], op0=ALU.mult, op1=ALU.add))
                i = nc.vector.scalar_tensor_tensor(out=dst[:, 0:SEQ - 1], in0=bank(name)[:, 1:SEQ],
                                                   scalar=col(C_CW + 6 * DB + blk), in1=dst[:, 0:SEQ - 1],
                                                   op0=ALU.mult, op1=ALU.add)
                i.then_inc(empty(name), 1)

            edge = [CHUNK - 1, 0]

            def decay(d, n):
                t = n * CHUNK + edge[d]
                return e1[:, d, t:t + 1]

            for stage in STAGES:
                kind, *at = stage
                if kind == "parts":
                    j = BLOCKS.index(tuple(at))
                    dve.wait_ge(w_hi_ready, j + 1)
                    nc.vector.tensor_tensor(block_of(*at, as_r["front"]), block_of(*at), w_hi[j % HI_BUFS].bitcast(F32),
                                            ALU.subtract).then_inc(w_parts_ready, 1)
                elif kind.endswith("_parts"):
                    what = kind[:-6]
                    dve.wait_ge(act_hi_ready, ["xn", "ogla", "ohy"].index(what) + 1)
                    val, hi, lo = parts_of[what]
                    nc.vector.tensor_tensor(lo, val, hi.bitcast(F32), ALU.subtract).then_inc(act_parts_ready, 1)
                elif kind == "xT":
                    n, = at
                    filled(dve, f"xT{n}")
                    for k in range(2):
                        last = nc.vector.tensor_scalar(xnT[:, 2 * n + k, :], bank(f"xT{n}")[:, k * SEQ:(k + 1) * SEQ],
                                                       col(C_N1 + 2 * n + k), None, ALU.mult)
                    last.then_inc(empty(f"xT{n}"), 1)
                elif kind == "filter":
                    name = f"filter{at[0]}"
                    bias_col = [C_B1, C_B2][at[0] - 1]
                    filled(dve, name)
                    if at[0] == 2:
                        dve.wait_ge(sin_ready, 1)
                    i = nc.vector.tensor_scalar(arg, bank(name)[0:FFN, 0:SEQ], col(bias_col, FFN), col(C_FR, FFN), ALU.add, ALU.mult)
                    i.then_inc(empty(name), 1)
                    emptied(dve, name)
                    link(nc.vector.tensor_scalar(turns, arg, 1.0 / (2 * np.pi), ROUND, ALU.mult, ALU.add))
                    link(nc.vector.tensor_scalar(turns, turns, -ROUND, None, ALU.add))
                    for part in (TWO_PI_HI, TWO_PI_MID, TWO_PI_LO):
                        link(nc.vector.scalar_tensor_tensor(out=arg, in0=turns, scalar=-part, in1=arg, op0=ALU.mult, op1=ALU.add))
                    nc.vector.tensor_scalar(arg, arg, PI_IN, -PI_IN, ALU.min, ALU.max).then_inc(arg_ready, 1)
                elif kind == "taps":
                    a, c = at
                    n = f"taps{a}{c}"
                    dve.wait_ge(dec_ready, TB)
                    filled(dve, n)
                    nc.vector.tensor_tensor(hf[:, a, c * 512:(c + 1) * 512], bank(n)[:, :], dec[a][:, c * 512:(c + 1) * 512],
                                            ALU.mult).then_inc(empty(n), 1)
                elif kind == "energy":
                    for a in range(TB):
                        for c in range(4):
                            emptied(dve, f"taps{a}{c}")
                    nc.vector.memset(hf[0:1, 0, D:2 * D], 0.0).then_inc(hf_ready, 1)
                    dve.wait_ge(hf_ready, 1)
                    for a in range(TB):
                        nc.vector.tensor_tensor(sumh[:, a, :], hf[:, a, 0:D], hf[:, a, D:2 * D], ALU.add).then_inc(sd_ready, 1)
                    dve.wait_ge(sd_ready, TB)
                    dve.wait_ge(sq_ready, TB)
                    for a in range(TB):
                        nc.vector.tensor_tensor(hf[:, a, D:2 * D], hf[:, a, 0:D], hf[:, a, D:2 * D], ALU.subtract).then_inc(sd_ready, 1)
                elif kind == "ksum":
                    emptied(dve, "ksum")
                    nc.vector.reciprocal(krs, kss).then_inc(rs_ready, 1)
                elif kind == "gates":
                    h, = at
                    dve.wait_ge(softplus, h + 1)
                    i = nc.vector.scalar_tensor_tensor(out=tmp_area[:, 0:512], in0=bank(f"gates{h}")[:, :], scalar=0.0,
                                                       in1=tmp_area[:, 0:512], op0=ALU.min, op1=ALU.subtract)
                    i.then_inc(empty(f"gates{h}"), 1)
                    emptied(dve, f"gates{h}")
                    nc.vector.engine_nop().then_inc(glog_ready, 1)
                elif kind == "sums":
                    h, = at
                    emptied(dve, f"sums{h}")
                    emptied(dve, f"q{h}")
                    emptied(dve, f"k{h}")
                    if h:
                        filled(dve, f"ke{h - 1}")
                    for d in range(2):
                        b4 = bs[:, d, :].rearrange("p (n t) -> p n t", n=4)
                        nc.vector.tensor_tensor(ke[:, d, :].rearrange("p (n t) -> p n t", n=4),
                                                b4[:, :, edge[d]:edge[d] + 1].to_broadcast([P, 4, CHUNK]), b4,
                                                ALU.subtract).then_inc(bdiff_ready, 1)
                    if h:
                        filled(dve, f"output{h - 1}")
                    dve.wait_ge(exp_ready, 3 * h + 2)
                    for d in range(2):
                        nc.vector.scalar_tensor_tensor(out=qt[:, d, :], in0=qkT[:, 0, h, :], scalar=float(DK) ** -0.5,
                                                       in1=e1[:, d, :], op0=ALU.mult, op1=ALU.mult).then_inc(qk_scaled, 1)
                        nc.vector.tensor_tensor(kt[:, d, :], qkT[:, 1, h, :], kt[:, d, :], ALU.mult).then_inc(qk_scaled, 1)
                    dve.wait_ge(exp_ready, 3 * h + 3)
                    for d in range(2):
                        nc.vector.tensor_tensor(ke[:, d, :], qkT[:, 1, h, :], ke[:, d, :], ALU.mult).then_inc(ke_ready, 1)
                elif kind == "scores":
                    h, = at
                    filled(dve, f"sc{h}")
                    if h:
                        emptied(dve, f"sc{h - 1}")
                    for d in range(2):
                        for a in range(TB):
                            o = (d * TB + a) * P
                            last = nc.vector.copy_predicated(scm[:, a, :], gla_mask[d], bank(f"sc{h}")[:, o:o + P])
                        if d == 0:
                            link(last)
                    last.then_inc(empty(f"sc{h}"), 1)
                elif kind == "updates":
                    h, = at
                    for k in range(4):
                        filled(dve, f"U{h}{k}")
                    for m, pair in enumerate((((0, 0, 0), (3, 3, 0)), ((1, 1, 0), (2, 2, 0)), ((2, 0, 1), (1, 1, 1)))):
                        if m:
                            dve.wait_ge(state_ready, 6 * h + 2 * m)
                        for d, (n, k, half) in enumerate(pair):
                            src = bank(f"U{h}{k}")[:, half * DV:(half + 1) * DV]
                            if m == 0:
                                i = nc.vector.tensor_copy(state[:, d, 0, :], src)
                            else:
                                i = nc.vector.scalar_tensor_tensor(out=state[:, d, m, :], in0=state[:, d, m - 1, :],
                                                                   scalar=decay(d, n), in1=src, op0=ALU.mult, op1=ALU.add)
                            i.then_inc(state_ready, 1)
                    for k in range(4):
                        nc.vector.engine_nop().then_inc(empty(f"U{h}{k}"), 1)
                elif kind == "onorm":
                    dve.wait_ge(ss_ready, 2)
                    nc.vector.reciprocal(rsg, ssg).then_inc(rs_ready, 1)
                    dve.wait_ge(rs_ready, 3)
                    for a in range(TB):
                        for h in range(HEADS):
                            nc.vector.tensor_scalar(vtok[:, a, h * DV:(h + 1) * DV], vtok[:, a, h * DV:(h + 1) * DV],
                                                    rsg[:, a * HEADS + h:a * HEADS + h + 1], None, ALU.mult).then_inc(onorm_ready, 1)
                elif kind == "zbias":
                    for half in range(2):
                        for a in range(TB):
                            filled(dve, f"zt{a}{half}")
                    for b in range(DB):
                        last = nc.vector.tensor_scalar(zT[:, b, :], zT[:, b, :], col(C_HB + b), None, ALU.mult)
                    link(last)
                    for ri in range(2):
                        for kc in range(2):
                            for half in range(2):
                                emptied(dve, f"K{ri}{kc}{half}")
                elif kind == "Z":
                    kc, half = at
                    cs = slice(half * 512, (half + 1) * 512)
                    zr, zi = f"Z{kc}{half}0", f"Z{kc}{half}1"
                    filled(dve, zr)
                    filled(dve, zi)
                    tmp = ytmp[:, half]
                    if kc:
                        dve.wait_ge(Y_ready, half + 1)
                    nc.vector.tensor_tensor(Yf[:, 0, kc, cs], bank(zr)[:, :], Kf[:, 0, kc, cs], ALU.mult)
                    nc.vector.tensor_tensor(tmp[:, 0, :], bank(zi)[:, :], Kf[:, 1, kc, cs], ALU.mult)
                    nc.vector.tensor_tensor(Yf[:, 1, kc, cs], bank(zr)[:, :], Kf[:, 1, kc, cs], ALU.mult).then_inc(empty(zr), 1)
                    nc.vector.tensor_tensor(tmp[:, 1, :], bank(zi)[:, :], Kf[:, 0, kc, cs], ALU.mult).then_inc(empty(zi), 1)
                    emptied(dve, zi)
                    nc.vector.tensor_tensor(Yf[:, 0, kc, cs], Yf[:, 0, kc, cs], tmp[:, 0, :], ALU.subtract)
                    nc.vector.tensor_tensor(Yf[:, 1, kc, cs], Yf[:, 1, kc, cs], tmp[:, 1, :], ALU.add).then_inc(Y_ready, 1)
                elif kind == "y":
                    b, = at
                    if b == 0:
                        dve.wait_ge(rs_ready, 2)
                        for bb in range(DB):
                            emptied(dve, f"h0{bb}")
                    filled(dve, f"y{b}")
                    nc.vector.scalar_tensor_tensor(out=zT[:, b, :], in0=bank(f"y{b}")[:, 0:SEQ], scalar=krs[:, b:b + 1],
                                                   in1=zT[:, b, :], op0=ALU.mult, op1=ALU.add).then_inc(empty(f"y{b}"), 1)
                    emptied(dve, f"y{b}")
                    nc.vector.tensor_tensor(ohyT[:, b, :], zT[:, b, :], ohyT[:, b, :], ALU.mult).then_inc(ohy_ready, 1)
                elif kind == "oT":
                    n, = at
                    filled(dve, f"oT{n}")
                    for k in range(2):
                        b = 2 * n + k
                        emptied(dve, f"r{b}")
                        i = nc.vector.scalar_tensor_tensor(out=oglaT[:, b, :], in0=bank(f"oT{n}")[:, k * SEQ:(k + 1) * SEQ],
                                                           scalar=col(C_GN + b % 2), in1=silu_r[:, b, :],
                                                           op0=ALU.mult, op1=ALU.mult)
                        i.then_inc(ogla_ready, 1)
                    nc.vector.engine_nop().then_inc(empty(f"oT{n}"), 1)
                elif kind == "proj":
                    nm, b = at
                    n = f"{nm}{b}"
                    if nm == "hv":
                        conv_sides(n, zT[:, b, :], 2 * DB + b)
                    elif nm == "hx":
                        conv_sides(n, xbuf[:, b % 4, :], DB + b)
                        emptied(dve, f"hv{b}")
                        emptied(dve, f"hx{b}")
                        nc.vector.tensor_tensor(zT[:, b, :], zT[:, b, :], xbuf[:, b % 4, :], ALU.mult).then_inc(z_ready, 1)
                    elif nm == "h0":
                        conv_sides(n, ohyT[:, b, :], b)
                    elif nm == "r":
                        dve.wait_ge(sig_ready, b + 1)
                        nc.vector.tensor_tensor(silu_r[:, b, :], bank(n)[:, 0:SEQ], sg[:, b % 4, :], ALU.mult).then_inc(empty(n), 1)
                    elif nm == "wg":
                        emptied(dve, f"gg{b}")
                        filled(dve, n)
                        nc.vector.tensor_tensor(mergedT[:, b, :], bank(n)[:, 0:SEQ], sg[:, b % 4, :], ALU.mult).then_inc(empty(n), 1)
                    elif nm == "wh":
                        emptied(dve, f"gh{b}")
                        filled(dve, n)
                        nc.vector.tensor_tensor(mtmp[:, b % 2, :], bank(n)[:, 0:SEQ], sg[:, b % 4, :], ALU.mult).then_inc(empty(n), 1)
                        emptied(dve, n)
                        nc.vector.tensor_tensor(mergedT[:, b, :], mergedT[:, b, :], mtmp[:, b % 2, :], ALU.add).then_inc(merged_ready, 1)
                elif kind == "wo":
                    half, a = at
                    n = f"wo{half}{a}"
                    filled(dve, n)
                    xs = x[:, a, half * 512:(half + 1) * 512]
                    nc.vector.tensor_tensor(xs, bank(n)[:, :], xs, ALU.add).then_inc(empty(n), 1)
                elif kind == "hT":
                    a, n = at
                    t = f"hT{a}{n}"
                    filled(dve, t)
                    w = colw[:, C_N2 + 4 * n:C_N2 + 4 * n + 4].rearrange("p (k o) -> p k o", o=1).to_broadcast([P, 4, P])
                    nc.vector.tensor_tensor(hT[:, 4 * n:4 * n + 4, a * P:(a + 1) * P],
                                            bank(t)[:, :].rearrange("p (k t) -> p k t", k=4), w, ALU.mult).then_inc(empty(t), 1)
            for a in range(TB):
                dve.wait_ge(ss_ready, 3 + a)
                nc.vector.reciprocal(rs2[:, a:a + 1], ss2[:, a:a + 1]).then_inc(rs_ready, 1)
            dve.wait_ge(router_loaded, 16 * 3)
            nc.vector.memset(tmp_area[:, 1824:1984], NEG)
            link(nc.vector.memset(tmp_area[:, 2128:2264], -1.0))
            link(nc.vector.memset(comb[:, :, 0:1], 1.0))
            link(nc.vector.memset(tmp_area[:, 2264:2264 + SEQ], 0.0))
            filled(dve, "rl")
            dve.wait_ge(rs_ready, 3 + TB)
            for a in range(TB):
                last = nc.vector.scalar_tensor_tensor(out=logit[:, a, 0:E], in0=bank("rl")[:, a * E:(a + 1) * E],
                                                      scalar=rs2[:, a:a + 1], in1=rb, op0=ALU.mult, op1=ALU.add)
            last.then_inc(empty("rl"), 1)
            emptied(dve, "rl")
            for a in range(TB):
                link(nc.vector.max(top8[:, a, :], logit[:, a, 0:E]))
            nc.vector.tensor_scalar(m1n, top8[:, :, 0], -1.0, None, ALU.mult).then_inc(expo_ready, 1)
            dve.wait_ge(expo_ready, 1)
            link(nc.vector.memset(top8[:, :, TOPK:8], NEG))
            for a in range(TB):
                link(nc.vector.match_replace(gone[:, a, :], top8[:, a, :], logit[:, a, :], NEG))
            nc.vector.tensor_tensor(mask, gone[:, :, 0:E], logit[:, :, 0:E], ALU.not_equal).then_inc(mask_ready, 1)
            dve.wait_ge(mask_ready, 1)
            filled(dve, "rank")
            for a in range(TB):
                link(nc.vector.scalar_tensor_tensor(out=pos[:, a, 0:E], in0=bank("rank")[:, a * E:(a + 1) * E], scalar=1.0,
                                                    in1=mask[:, a, :], op0=ALU.add, op1=ALU.mult))
            nc.vector.engine_nop().then_inc(empty("rank"), 1)
            link(nc.vector.tensor_scalar(pos[:, :, 0:E], pos[:, :, 0:E], -1.0, None, ALU.add))
            def select(q, e):
                nc.vector.tensor_tensor(sel[:, q % 2, :, :], iota.rearrange("p (o s) -> p o s", o=1).to_broadcast([P, TB, 2 * CAP]),
                                        pos[:, :, bass.ds(e, 1)].to_broadcast([P, TB, 2 * CAP]), ALU.is_equal).then_inc(sel_ready, 1)

            select(0, 0)
            dve.wait_ge(expo_ready, 1 + TB)
            link(nc.vector.tensor_tensor(expo, expo, mask, ALU.mult))
            link(nc.vector.tensor_reduce(den, expo, AX.X, ALU.add))
            link(nc.vector.reciprocal(den, den))
            for a in range(TB):
                link(nc.vector.tensor_scalar(comb[:, a, 1:1 + E], expo[:, a, :], den[:, a:a + 1], None, ALU.mult))
            for h in range(2):
                last = nc.vector.tensor_copy(combx[:, :, h, 0:E], comb[:, :, 1:1 + E])
            last.then_inc(comb_ready, 1)
            filled(dve, "cnt")
            nc.vector.tensor_reduce(cntm, bank("cnt")[:, 0:E], AX.X, ALU.max).then_inc(empty("cnt"), 1)
            emptied(dve, "cnt")
            nc.vector.tensor_copy(flag[:, :], cntm[0:1, :]).then_inc(count_ready, 1)

            select(1, 1)

            norm2 = colw[:, C_N2:C_N2 + DB].rearrange("p (h c o) -> p c h o", h=2, o=1).to_broadcast([P, 4, 2, CAP])

            def scale_xeT(q, count):
                dve.wait_ge(xeT_psum, count)
                nc.vector.tensor_tensor(xeT[:, q % 2].rearrange("p c (h s) -> p c h s", h=2),
                                        banks[4][:, :].rearrange("p (c h s) -> p c h s", c=4, h=2), norm2,
                                        ALU.mult).then_inc(xeT_ready, 1)

            def swiglu(used, count):
                dve.wait_ge(chunks_used, used)
                nc.vector.tensor_scalar(gate, banks[0][:, :], LIMIT, None, ALU.min).then_inc(gate_ready, 1)
                nc.vector.tensor_scalar(up, banks[1][:, :], LIMIT, -LIMIT, ALU.min, ALU.max).then_inc(up_clipped, 1)
                dve.wait_ge(up_clipped, count)
                nc.vector.scalar_tensor_tensor(out=up, in0=up, scalar=1.0, in1=gate, op0=ALU.add, op1=ALU.mult).then_inc(up_gated, 1)
                dve.wait_ge(up_gated, count)
                dve.wait_ge(sigm_ready, count)
                nc.vector.tensor_tensor(act, up, sig, ALU.mult).then_inc(act_ready, 1)

            def add_back(count, column, banks_of=(6, 7, 6, 7)):
                for k in range(4):
                    a, half = k // 2, k % 2
                    dve.wait_ge(scat_psum, count + k + 1)
                    xs = x[:, a, half * 512:(half + 1) * 512]
                    nc.vector.scalar_tensor_tensor(out=xs, in0=banks[banks_of[k]][:, :], scalar=comb[:, a, bass.ds(column, 1)], in1=xs,
                                                   op0=ALU.mult, op1=ALU.add).then_inc(scat_read, 1)

            for r in (E, CAP + E):
                last = nc.vector.memset(ysb[r:r + E, :], 0.0)
            last.then_inc(y_ready, 1)
            for _ in range(2):
                nc.vector.engine_nop().then_inc(scat_read, 1)
            scale_xeT(0, 1)
            with dve.Fori(0, E // UNROLL) as i:
                for q in range(UNROLL):
                    e = i * UNROLL + q
                    swiglu(e * CH + GU_CH, e + 1)
                    add_back(e * 4, e)
                    scale_xeT(q + 1, e + 2)
                    select(q + 2, e + 2)
            add_back(E * 4, E, (6, 7, 0, 1))
            longest = dve.value_load(flag[0:1, 0:1], min_val=0, max_val=SEQ)
            with dve.If(longest > CAP):
                with dve.Fori(0, MORE) as r:
                    nc.vector.tensor_scalar(pos[:, :, 0:E], pos[:, :, 0:E], -float(CAP), None, ALU.add).then_inc(pos_moved, 1)
                    with dve.Fori(0, E) as e:
                        t = r * E + e
                        dve.wait_ge(pos_moved, r + 1)
                        select(0, e)
                        scale_xeT(0, t + (E + 2))
                        swiglu(t * CH + (E * CH + GU_CH), t + (E + 1))
                        add_back(t * 4 + 4 * (E + 1), e + 1)
                dve.wait_ge(scat_read, 2 + 4 * (E + 1) + 4 * E * MORE)
            for a in range(TB):
                dve.wait_ge(ss_ready, 5 + a)
                nc.vector.reciprocal(rs3[:, a:a + 1], ss3[:, a:a + 1]).then_inc(rs_ready, 1)
                dve.wait_ge(rs_ready, 6 + a)
                nc.vector.scalar_tensor_tensor(out=x[:, a, :], in0=x[:, a, :], scalar=rs3[:, a:a + 1], in1=normf,
                                               op0=ALU.mult, op1=ALU.mult).then_inc(out_ready, 1)

        @block.gpsimd
        def _(pool):
            pool.wait_ge(sq_ready, TB)
            for a in range(TB):
                nc.gpsimd.tensor_tensor(sq[a][:, 0:D], sq[a][:, 0:D], sq[a][:, D:2 * D], ALU.add).then_inc(sq_summed, 1)
            pool.wait_ge(sq_summed, TB)
            nc.gpsimd.tensor_tensor(sq[0][:, 0:D], sq[0][:, 0:D], sq[1][:, 0:D], ALU.add).then_inc(sq_summed, 1)


def vector_columns(a):
    parts = [a[n].reshape(-1, P) for n in ("norm1_w", "norm2_w", "hy_conv_w", "hy_conv_b", "hy_bias", "gla_norm_w")]
    parts += [np.pad(a[n][None, :], ((0, 0), (0, P - FFN))) for n in ("hy_freq", "hy_ffn_b1", "hy_ffn_b2")]
    return np.ascontiguousarray(np.concatenate(parts, 0).T)


_INS = ["x", "w_in", "gla_gate_w2", "gla_gate_b", "hy_ffn_w1", "hy_ffn_w2", "hy_ffn_w3", "hy_decay", "w_branch_gla",
        "w_branch_hy", "w_out", "router_w", "router_b", "w_gate_up", "b_gate_up", "w_down", "b_down", "norm_f_w"]


def kernel(**inputs):
    import concourse.bacc as bacc
    from concourse.bass_utils import run_bass_kernel_spmd

    nc = bacc.Bacc("TRN2", target_bir_lowering=False, num_devices=1)
    arrays = {n: np.ascontiguousarray(inputs[n]) for n in _INS}
    arrays["shape_table"], arrays["dft_table"], arrays["filter_features"] = shape_tables()
    arrays["vector_columns"] = vector_columns({n: np.asarray(v) for n, v in inputs.items()})
    aps = {n: nc.dram_tensor(f"in_{n}", a.shape, mybir.dt.from_np(a.dtype), kind="ExternalInput").ap()
           for n, a in arrays.items()}
    out = nc.dram_tensor("out_y", (1, SEQ, D), F32, kind="ExternalOutput").ap()
    build(nc, aps, out)
    r = run_bass_kernel_spmd(nc, [{f"in_{n}": a for n, a in arrays.items()}], core_ids=[0])
    return r.results[0]["out_y"]
```
